# Optimizing a Trainium2 kernel written in Bass

```python
import jax, jax.numpy as jnp
from jax import lax
import numpy as np
import math

D_MODEL = 1024
BATCH = 1
SEQ = 256
DEPTH = 1

D_MIX = D_MODEL
ATT_HEADS = 8
ATT_HEAD_DIM = 64
ATT_WIDTH = ATT_HEADS * ATT_HEAD_DIM
DILATED_PATTERNS = ((128, 1), (512, 4), (2048, 16))
Q_BLOCK = 128
ROPE_THETA = 10000.0
GLA_HEADS = 4
GLA_KEY_DIM = 64
GLA_VAL_DIM = 128
GLA_KEY_WIDTH = GLA_HEADS * GLA_KEY_DIM
GLA_VAL_WIDTH = GLA_HEADS * GLA_VAL_DIM
GLA_GATE_RANK = 16
GLA_GATE_NORMALIZER = 16.0
GLA_CHUNK = 64
IN_SPLITS = (ATT_WIDTH, ATT_WIDTH, ATT_WIDTH, GLA_KEY_WIDTH, GLA_KEY_WIDTH,
             GLA_VAL_WIDTH, GLA_VAL_WIDTH, GLA_GATE_RANK)
D_IN = sum(IN_SPLITS)
N_EXPERTS = 32
TOP_K = 4
D_FF = D_MODEL
SWIGLU_LIMIT = 7.0
SWIGLU_ALPHA = 1.702
MOE_BLOCK = 128
NORM_EPS = 1e-6
N_MOD = 6


def rms_norm(x, g):
    xf = x.astype(jnp.float32)
    y = xf * lax.rsqrt(jnp.mean(xf * xf, axis=-1, keepdims=True) + NORM_EPS)
    return (y * g.astype(jnp.float32)).astype(x.dtype)

def rope(x, positions):
    half = x.shape[-1] // 2
    inv_freq = ROPE_THETA ** (-jnp.arange(half, dtype=jnp.float32) / half)
    ang = positions.astype(jnp.float32)[:, None] * inv_freq[None, :]
    cos, sin = jnp.cos(ang), jnp.sin(ang)
    xf = x.astype(jnp.float32)
    x1, x2 = xf[..., :half], xf[..., half:]
    return jnp.concatenate([x1 * cos - x2 * sin, x2 * cos + x1 * sin], axis=-1).astype(x.dtype)

def dilated_attention(q, k, v):
    B, H, S, hd = q.shape
    n_blk = S // Q_BLOCK

    def block(i):
        q0 = i * Q_BLOCK
        qb = lax.dynamic_slice_in_dim(q, q0, Q_BLOCK, axis=2).astype(jnp.float32)
        t = q0 + jnp.arange(Q_BLOCK)
        outs, lses = [], []
        for window, dil in DILATED_PATTERNS:
            offs = jnp.arange(window // dil + 1) * dil
            idx = t[:, None] - offs[None, :]
            valid = idx >= 0
            idx = jnp.maximum(idx, 0)
            kg = jnp.take(k, idx, axis=2).astype(jnp.float32)
            vg = jnp.take(v, idx, axis=2).astype(jnp.float32)
            s = jnp.einsum('bhqd,bhqjd->bhqj', qb, kg)
            s = jnp.where(valid, s, -jnp.inf)
            m = jnp.max(s, axis=-1, keepdims=True)
            p = jnp.exp(s - m)
            l = jnp.sum(p, axis=-1, keepdims=True)
            outs.append(jnp.einsum('bhqj,bhqjd->bhqd', p, vg) / l)
            lses.append(m + jnp.log(l))
        w = jax.nn.softmax(jnp.stack(lses, axis=0), axis=0)
        return jnp.sum(w * jnp.stack(outs, axis=0), axis=0)

    o = lax.map(block, jnp.arange(n_blk))
    o = o.transpose(1, 0, 3, 2, 4).reshape(B, S, H * hd)
    return o.astype(q.dtype)

def gated_linear_attention(q, k, v, log_a):
    B, H, S, dk = q.shape
    dv = v.shape[-1]
    C = GLA_CHUNK
    N = S // C
    qf = q.astype(jnp.float32).reshape(B, H, N, C, dk) * (dk ** -0.5)
    kf = k.astype(jnp.float32).reshape(B, H, N, C, dk)
    vf = v.astype(jnp.float32).reshape(B, H, N, C, dv)
    b = jnp.cumsum(log_a.reshape(B, H, N, C, dk), axis=3)
    b_last = b[:, :, :, -1:, :]
    q_dec = qf * jnp.exp(b)
    att = jnp.einsum('bhncd,bhnjd->bhncj', q_dec, kf * jnp.exp(-b))
    causal = jnp.tril(jnp.ones((C, C), dtype=bool))
    att = jnp.where(causal, att, 0.0)
    o_intra = jnp.einsum('bhncj,bhnje->bhnce', att, vf)
    u = jnp.einsum('bhncd,bhnce->nbhde', kf * jnp.exp(b_last - b), vf)
    a = jnp.exp(b_last[:, :, :, 0, :]).transpose(2, 0, 1, 3)

    def step(state, inp):
        a_n, u_n = inp
        return a_n[..., None] * state + u_n, state

    _, s_prev = lax.scan(step, jnp.zeros((B, H, dk, dv), jnp.float32), (a, u))
    o_inter = jnp.einsum('bhncd,nbhde->bhnce', q_dec, s_prev)
    return (o_intra + o_inter).reshape(B, H, S, dv)

def hybrid_mixer(h, w_in, w_gate_lr, b_gate, g_gla, w_out):
    B, S, _ = h.shape
    proj = h @ w_in
    split_points = [int(s) for s in np.cumsum(IN_SPLITS)[:-1]]
    q_a, k_a, v_a, q_g, k_g, v_g, r_g, g_lr = jnp.split(proj, split_points, axis=-1)

    def heads(t, n):
        return t.reshape(B, S, n, -1).transpose(0, 2, 1, 3)

    pos = jnp.arange(S)
    qa = rope(heads(q_a, ATT_HEADS), pos) * (ATT_HEAD_DIM ** -0.5)
    ka = rope(heads(k_a, ATT_HEADS), pos)
    o_att = dilated_attention(qa, ka, heads(v_a, ATT_HEADS))
    gate_logit = (g_lr @ w_gate_lr + b_gate).astype(jnp.float32)
    log_a = jax.nn.log_sigmoid(gate_logit) / GLA_GATE_NORMALIZER
    o_g = gated_linear_attention(heads(q_g, GLA_HEADS), heads(k_g, GLA_HEADS),
                                 heads(v_g, GLA_HEADS), heads(log_a, GLA_HEADS))
    o_g = rms_norm(o_g, g_gla)
    o_g = o_g.transpose(0, 2, 1, 3).reshape(B, S, GLA_VAL_WIDTH).astype(h.dtype) * jax.nn.silu(r_g)
    return jnp.concatenate([o_att, o_g], axis=-1) @ w_out

def moe_ffn(h, router_w, router_b, w_gate_up, b_gate_up, w_down, b_down):
    B, S, D = h.shape
    T = B * S
    xt = h.reshape(T, D)
    logits = (xt @ router_w + router_b).astype(jnp.float32)
    top_v, top_i = lax.top_k(logits, TOP_K)
    gates = jax.nn.softmax(top_v, axis=-1)
    A = T * TOP_K
    e_flat = top_i.reshape(A)
    tok_flat = jnp.arange(A, dtype=jnp.int32) // TOP_K
    g_flat = gates.reshape(A)
    order = jnp.argsort(e_flat)
    e_sorted = e_flat[order]
    counts = jnp.bincount(e_flat, length=N_EXPERTS)
    start = jnp.cumsum(counts) - counts
    padded = (counts + MOE_BLOCK - 1) // MOE_BLOCK * MOE_BLOCK
    pend = jnp.cumsum(padded)
    pstart = pend - padded
    dest = pstart[e_sorted] + jnp.arange(A, dtype=jnp.int32) - start[e_sorted]
    n_blocks = -(-(A + N_EXPERTS * (MOE_BLOCK - 1)) // MOE_BLOCK)
    P = n_blocks * MOE_BLOCK
    tok_buf = jnp.full((P,), T, dtype=jnp.int32).at[dest].set(tok_flat[order])
    gate_buf = jnp.zeros((P,), jnp.float32).at[dest].set(g_flat[order])
    blk_e = jnp.minimum(jnp.searchsorted(pend, jnp.arange(n_blocks) * MOE_BLOCK, side='right'),
                        N_EXPERTS - 1)
    xpad = jnp.concatenate([xt, jnp.zeros((1, D), xt.dtype)], axis=0)

    def expert_block(args):
        idx, e = args
        xb = xpad[idx]
        gu = xb @ w_gate_up[e] + b_gate_up[e]
        x_glu = jnp.minimum(gu[:, ::2], SWIGLU_LIMIT)
        x_lin = jnp.clip(gu[:, 1::2], -SWIGLU_LIMIT, SWIGLU_LIMIT)
        act = x_glu * jax.nn.sigmoid(SWIGLU_ALPHA * x_glu) * (x_lin + 1.0)
        return act @ w_down[e] + b_down[e]

    out_buf = lax.map(expert_block, (tok_buf.reshape(n_blocks, MOE_BLOCK), blk_e))
    out_buf = out_buf.reshape(P, D) * gate_buf[:, None].astype(out_buf.dtype)
    out = jnp.zeros((T + 1, D), out_buf.dtype).at[tok_buf].add(out_buf)
    return out[:T].reshape(B, S, D)

def first_inputs(seed: int = 0) -> dict:
    key = jax.random.key(seed)
    ks = jax.random.split(key, 20)
    L = DEPTH

    def nrm(k, shape, scale):
        return jax.random.normal(k, shape, jnp.float32) * scale

    return {
        "x": nrm(ks[0], (BATCH, SEQ, D_MODEL), 1.0),
        "c": nrm(ks[1], (BATCH, D_MODEL), 1.0),
        "w_mod": nrm(ks[2], (L, D_MODEL, N_MOD * D_MODEL), 0.5 * D_MODEL ** -0.5),
        "b_mod": nrm(ks[3], (L, N_MOD * D_MODEL), 0.02),
        "g_pre_mix": 1.0 + nrm(ks[4], (L, D_MODEL), 0.05),
        "w_in": nrm(ks[5], (L, D_MODEL, D_IN), D_MODEL ** -0.5),
        "w_gate_lr": nrm(ks[6], (L, GLA_GATE_RANK, GLA_KEY_WIDTH), GLA_GATE_RANK ** -0.5),
        "b_gate": nrm(ks[7], (L, GLA_KEY_WIDTH), 0.1),
        "g_gla": 1.0 + nrm(ks[8], (L, GLA_VAL_DIM), 0.05),
        "w_out": nrm(ks[9], (L, D_MIX, D_MODEL), D_MIX ** -0.5),
        "g_post_mix": 1.0 + nrm(ks[10], (L, D_MODEL), 0.05),
        "g_pre_ffn": 1.0 + nrm(ks[11], (L, D_MODEL), 0.05),
        "router_w": nrm(ks[12], (L, D_MODEL, N_EXPERTS), D_MODEL ** -0.5),
        "router_b": nrm(ks[13], (L, N_EXPERTS), 0.01),
        "w_gate_up": nrm(ks[14], (L, N_EXPERTS, D_MODEL, 2 * D_FF), D_MODEL ** -0.5),
        "b_gate_up": nrm(ks[15], (L, N_EXPERTS, 2 * D_FF), 0.02),
        "w_down": nrm(ks[16], (L, N_EXPERTS, D_FF, D_MODEL), D_FF ** -0.5),
        "b_down": nrm(ks[17], (L, N_EXPERTS, D_MODEL), 0.02),
        "g_post_ffn": 1.0 + nrm(ks[18], (L, D_MODEL), 0.05),
    }

def first_block(x, c, w_mod, b_mod, g_pre_mix, w_in, w_gate_lr, b_gate, g_gla, w_out,
              g_post_mix, g_pre_ffn, router_w, router_b, w_gate_up, b_gate_up,
              w_down, b_down, g_post_ffn):
    for l in range(DEPTH):
        mod = jax.nn.silu(c) @ w_mod[l] + b_mod[l]
        shift1, scale1, gate1, shift2, scale2, gate2 = jnp.split(mod[:, None, :], N_MOD, axis=-1)
        h = rms_norm(x, g_pre_mix[l]) * (1.0 + scale1) + shift1
        y = hybrid_mixer(h, w_in[l], w_gate_lr[l], b_gate[l], g_gla[l], w_out[l])
        x = x + gate1 * rms_norm(y, g_post_mix[l])
        h = rms_norm(x, g_pre_ffn[l]) * (1.0 + scale2) + shift2
        y = moe_ffn(h, router_w[l], router_b[l], w_gate_up[l], b_gate_up[l], w_down[l], b_down[l])
        x = x + gate2 * rms_norm(y, g_post_ffn[l])
    return x


MLA_HEADS = 8
MLA_Q_RANK = 384
MLA_KV_RANK = 256
MLA_NOPE = 64
MLA_ROPE = 32
MLA_V = 64
ROPE_BASE = 10000.0
DIFF_HEADS = 4
DIFF_D = 64
IN_SPLITS_2 = (MLA_Q_RANK, MLA_KV_RANK, MLA_ROPE,
             2 * DIFF_HEADS * DIFF_D, 2 * DIFF_HEADS * DIFF_D, DIFF_HEADS * 2 * DIFF_D)
IN_WIDTH = sum(IN_SPLITS_2)
IN_OFFSETS = tuple(int(v) for v in np.cumsum(IN_SPLITS_2)[:-1])
REL_BUCKETS = 32
REL_MAX_DIST = 128
MEM_LEN = 256
MEM_HEADS = 4
MEM_HEAD_DIM = D_MODEL // MEM_HEADS
D_FF_2 = 2816
ALPHA = (2.0 * DEPTH) ** 0.25
BETA = (8.0 * DEPTH) ** -0.25
LN_EPS = 1e-5
RMS_EPS = 1e-6


def layer_norm(x, g, b):
    xf = x.astype(jnp.float32)
    mu = jnp.mean(xf, axis=-1, keepdims=True)
    var = jnp.mean(jnp.square(xf - mu), axis=-1, keepdims=True)
    y = (xf - mu) * lax.rsqrt(var + LN_EPS) * g.astype(jnp.float32) + b.astype(jnp.float32)
    return y.astype(x.dtype)

def rms_norm_2(x, g):
    xf = x.astype(jnp.float32)
    y = xf * lax.rsqrt(jnp.mean(jnp.square(xf), axis=-1, keepdims=True) + RMS_EPS)
    return (y * g.astype(jnp.float32)).astype(x.dtype)

def swiglu(x, w1, w3, w2):
    return (jax.nn.silu(x @ w1) * (x @ w3)) @ w2

def rope_2(x, cos, sin):
    half = x.shape[-1] // 2
    x1, x2 = x[..., :half], x[..., half:]
    c, s = cos[None, :, None, :], sin[None, :, None, :]
    return jnp.concatenate([x1 * c - x2 * s, x2 * c + x1 * s], axis=-1)

def t5_bucket(q_pos, k_pos):
    n = jnp.maximum(q_pos[:, None] - k_pos[None, :], 0)
    max_exact = REL_BUCKETS // 2
    nf = jnp.maximum(n, 1).astype(jnp.float32)
    large = max_exact + (jnp.log(nf / max_exact) / math.log(REL_MAX_DIST / max_exact)
                         * (REL_BUCKETS - max_exact)).astype(jnp.int32)
    large = jnp.minimum(large, REL_BUCKETS - 1)
    return jnp.where(n < max_exact, n, large)

def parallel_mixer(h, rel_bias, w_in, q_norm_g, kv_norm_g, w_q_b, w_kv_b,
                   lam_q1, lam_k1, lam_q2, lam_k2, lam_init, diff_norm_g,
                   w_gate, b_gate, w_up_mla, w_up_diff, w_o):
    B, S, _ = h.shape
    proj = h @ w_in
    c_q, c_kv, k_rope, q_d, k_d, v_d = jnp.split(proj, IN_OFFSETS, axis=-1)

    q = (rms_norm_2(c_q, q_norm_g) @ w_q_b).reshape(B, S, MLA_HEADS, MLA_NOPE + MLA_ROPE)
    q_nope, q_rope = q[..., :MLA_NOPE], q[..., MLA_NOPE:]
    kv = (rms_norm_2(c_kv, kv_norm_g) @ w_kv_b).reshape(B, S, MLA_HEADS, MLA_NOPE + MLA_V)
    k_nope, v_m = kv[..., :MLA_NOPE], kv[..., MLA_NOPE:]
    pos = jnp.arange(S)
    inv_freq = ROPE_BASE ** (-jnp.arange(0, MLA_ROPE, 2, dtype=jnp.float32) / MLA_ROPE)
    ang = pos.astype(jnp.float32)[:, None] * inv_freq[None, :]
    cos, sin = jnp.cos(ang).astype(h.dtype), jnp.sin(ang).astype(h.dtype)
    q_rope = rope_2(q_rope, cos, sin)
    k_rope = rope_2(k_rope[:, :, None, :], cos, sin)[:, :, 0]

    q_d = q_d.reshape(B, S, 2 * DIFF_HEADS, DIFF_D)
    k_d = k_d.reshape(B, S, 2 * DIFF_HEADS, DIFF_D)
    v_d = v_d.reshape(B, S, DIFF_HEADS, 2 * DIFF_D)
    f32 = jnp.float32
    lam = (jnp.exp(jnp.sum(lam_q1.astype(f32) * lam_k1.astype(f32)))
           - jnp.exp(jnp.sum(lam_q2.astype(f32) * lam_k2.astype(f32))) + lam_init)

    mla_scale = (MLA_NOPE + MLA_ROPE) ** -0.5
    diff_scale = DIFF_D ** -0.5
    outs_m, outs_d = [], []
    for i in range(S // Q_BLOCK):
        lo, hi = i * Q_BLOCK, (i + 1) * Q_BLOCK
        q_pos = jnp.arange(lo, hi)
        k_pos = jnp.arange(hi)
        causal = q_pos[:, None] >= k_pos[None, :]
        s = (jnp.einsum('bqhd,bkhd->bhqk', q_nope[:, lo:hi], k_nope[:, :hi])
             + jnp.einsum('bqhr,bkr->bhqk', q_rope[:, lo:hi], k_rope[:, :hi]))
        p = jax.nn.softmax(jnp.where(causal, s.astype(f32) * mla_scale, -jnp.inf), axis=-1)
        outs_m.append(jnp.einsum('bhqk,bkhd->bqhd', p.astype(v_m.dtype), v_m[:, :hi]))
        bias = jnp.transpose(rel_bias[t5_bucket(q_pos, k_pos)], (2, 0, 1)).astype(f32)
        s = jnp.einsum('bqhd,bkhd->bhqk', q_d[:, lo:hi], k_d[:, :hi]).astype(f32) * diff_scale + bias
        p = jax.nn.softmax(jnp.where(causal, s, -jnp.inf), axis=-1)
        p = p.reshape(B, DIFF_HEADS, 2, Q_BLOCK, hi)
        a = p[:, :, 0] - lam * p[:, :, 1]
        outs_d.append(jnp.einsum('bhqk,bkhd->bqhd', a.astype(v_d.dtype), v_d[:, :hi]))

    o_m = jnp.concatenate(outs_m, axis=1).reshape(B, S, MLA_HEADS * MLA_V)
    o_d = jnp.concatenate(outs_d, axis=1)
    o_d = (rms_norm_2(o_d, diff_norm_g) * (1.0 - lam_init)).reshape(B, S, DIFF_HEADS * 2 * DIFF_D)

    y_m = o_m @ w_up_mla
    y_d = o_d @ w_up_diff
    g = jax.nn.sigmoid(h @ w_gate + b_gate)
    g_m, g_d = g[..., :D_MODEL], g[..., D_MODEL:]
    return (g_m * y_m + g_d * y_d) @ w_o

def memory_attention(h, mem, w_q, w_kv, w_o):
    B, S, _ = h.shape
    M = mem.shape[1]
    q = (h @ w_q).reshape(B, S, MEM_HEADS, MEM_HEAD_DIM)
    kv = mem @ w_kv
    k = kv[..., :D_MODEL].reshape(B, M, MEM_HEADS, MEM_HEAD_DIM)
    v = kv[..., D_MODEL:].reshape(B, M, MEM_HEADS, MEM_HEAD_DIM)
    s = jnp.einsum('bqhd,bkhd->bhqk', q, k).astype(jnp.float32) * MEM_HEAD_DIM ** -0.5
    p = jax.nn.softmax(s, axis=-1)
    o = jnp.einsum('bhqk,bkhd->bqhd', p.astype(v.dtype), v).reshape(B, S, D_MODEL)
    return o @ w_o

def second_inputs(seed: int = 0) -> dict:
    key = jax.random.key(seed)
    ks = iter(jax.random.split(key, 64))
    L, D, F = DEPTH, D_MODEL, D_FF_2

    def dense(shape, fan_in, scale=1.0):
        return jax.random.normal(next(ks), shape, jnp.float32) * (fan_in ** -0.5) * scale

    def gain(shape):
        return 1.0 + 0.05 * jax.random.normal(next(ks), shape, jnp.float32)

    def small(shape, scale=0.05):
        return scale * jax.random.normal(next(ks), shape, jnp.float32)

    mla_in = MLA_HEADS * MLA_V
    diff_in = DIFF_HEADS * 2 * DIFF_D
    return {
        "x": jax.random.normal(next(ks), (BATCH, SEQ, D), jnp.float32),
        "mem": jax.random.normal(next(ks), (BATCH, MEM_LEN, D), jnp.float32),
        "rel_bias": small((REL_BUCKETS, 2 * DIFF_HEADS), 0.3),
        "ffn1_w1": dense((L, D, F), D),
        "ffn1_w3": dense((L, D, F), D),
        "ffn1_w2": dense((L, F, D), F, BETA),
        "ln1_g": gain((L, D)),
        "ln1_b": small((L, D)),
        "w_in": dense((L, D, IN_WIDTH), D),
        "q_norm_g": gain((L, MLA_Q_RANK)),
        "kv_norm_g": gain((L, MLA_KV_RANK)),
        "w_q_b": dense((L, MLA_Q_RANK, MLA_HEADS * (MLA_NOPE + MLA_ROPE)), MLA_Q_RANK),
        "w_kv_b": dense((L, MLA_KV_RANK, MLA_HEADS * (MLA_NOPE + MLA_V)), MLA_KV_RANK),
        "lam_q1": small((L, DIFF_D), 0.1),
        "lam_k1": small((L, DIFF_D), 0.1),
        "lam_q2": small((L, DIFF_D), 0.1),
        "lam_k2": small((L, DIFF_D), 0.1),
        "diff_norm_g": gain((L, 2 * DIFF_D)),
        "w_gate": dense((L, D, 2 * D), D),
        "b_gate": small((L, 2 * D), 0.1),
        "w_up_mla": dense((L, mla_in, D), mla_in, BETA),
        "w_up_diff": dense((L, diff_in, D), diff_in, BETA),
        "w_o": dense((L, D, D), D, BETA),
        "ln2_g": gain((L, D)),
        "ln2_b": small((L, D)),
        "mem_w_q": dense((L, D, D), D),
        "mem_w_kv": dense((L, D, 2 * D), D),
        "mem_w_o": dense((L, D, D), D, BETA),
        "ln3_g": gain((L, D)),
        "ln3_b": small((L, D)),
        "ffn2_w1": dense((L, D, F), D),
        "ffn2_w3": dense((L, D, F), D),
        "ffn2_w2": dense((L, F, D), F, BETA),
        "ln4_g": gain((L, D)),
        "ln4_b": small((L, D)),
    }

def second_block(x, mem, rel_bias, ffn1_w1, ffn1_w3, ffn1_w2, ln1_g, ln1_b,
              w_in, q_norm_g, kv_norm_g, w_q_b, w_kv_b, lam_q1, lam_k1, lam_q2, lam_k2,
              diff_norm_g, w_gate, b_gate, w_up_mla, w_up_diff, w_o, ln2_g, ln2_b,
              mem_w_q, mem_w_kv, mem_w_o, ln3_g, ln3_b,
              ffn2_w1, ffn2_w3, ffn2_w2, ln4_g, ln4_b):
    h = x
    for l in range(DEPTH):
        lam_init = 0.8 - 0.6 * math.exp(-0.3 * l)
        h = layer_norm(ALPHA * h + 0.5 * swiglu(h, ffn1_w1[l], ffn1_w3[l], ffn1_w2[l]),
                       ln1_g[l], ln1_b[l])
        mix = parallel_mixer(h, rel_bias, w_in[l], q_norm_g[l], kv_norm_g[l], w_q_b[l], w_kv_b[l],
                             lam_q1[l], lam_k1[l], lam_q2[l], lam_k2[l], lam_init, diff_norm_g[l],
                             w_gate[l], b_gate[l], w_up_mla[l], w_up_diff[l], w_o[l])
        h = layer_norm(ALPHA * h + mix, ln2_g[l], ln2_b[l])
        h = layer_norm(ALPHA * h + memory_attention(h, mem, mem_w_q[l], mem_w_kv[l], mem_w_o[l]),
                       ln3_g[l], ln3_b[l])
        h = layer_norm(ALPHA * h + 0.5 * swiglu(h, ffn2_w1[l], ffn2_w3[l], ffn2_w2[l]),
                       ln4_g[l], ln4_b[l])
    return h


HEAD_DIM = 64
N_HEADS_DSA = 8
N_HEADS_MOBA = 8
N_IDX_HEADS = 4
IDX_DIM = 64
DSA_TOPK = 256
MOBA_BLOCK = 256
MOBA_TOPK = 3
N_BUCKETS = 32
MAX_DISTANCE = 128
D_FF_3 = 2816
MOBA_Q_CHUNK = 32
EPS = 1e-6

W_DSA = N_HEADS_DSA * HEAD_DIM
W_MOBA = N_HEADS_MOBA * HEAD_DIM
W_IDX_Q = N_IDX_HEADS * IDX_DIM
SPLIT_SIZES = (W_DSA, W_DSA, W_DSA, W_MOBA, W_MOBA, W_MOBA, W_IDX_Q, IDX_DIM, N_IDX_HEADS, 2 * D_MODEL)
SPLIT_POINTS = tuple(int(v) for v in np.cumsum(SPLIT_SIZES)[:-1])
D_IN_3 = int(sum(SPLIT_SIZES))


def rmsnorm(x, g):
    xf = x.astype(jnp.float32)
    y = xf * lax.rsqrt(jnp.mean(xf * xf, axis=-1, keepdims=True) + EPS)
    return (y * g.astype(jnp.float32)).astype(x.dtype)

def swiglu_3(x, w_gu, w_down):
    gate, up = jnp.split(x @ w_gu, 2, axis=-1)
    return (jax.nn.silu(gate) * up) @ w_down

def t5_bucket_3(dist):
    max_exact = N_BUCKETS // 2
    d = jnp.maximum(dist, 0)
    df = jnp.maximum(d, 1).astype(jnp.float32)
    large = max_exact + (jnp.log(df / max_exact) / math.log(MAX_DISTANCE / max_exact)
                         * (N_BUCKETS - max_exact)).astype(jnp.int32)
    large = jnp.minimum(large, N_BUCKETS - 1)
    return jnp.where(d < max_exact, d, large)

def dsa_attention(q, k, v, q_idx, k_idx, w_idx, bias_tab):
    B, S, H, Dh = q.shape
    topk = min(DSA_TOPK, S // 4)
    scale = Dh ** -0.5
    key_pos = jnp.arange(S)
    b_ix = jnp.arange(B)[:, None, None]
    k_idx_f = k_idx.astype(jnp.float32)

    def block(i):
        t0 = i * Q_BLOCK
        qb = lax.dynamic_slice_in_dim(q, t0, Q_BLOCK, axis=1)
        qib = lax.dynamic_slice_in_dim(q_idx, t0, Q_BLOCK, axis=1).astype(jnp.float32)
        wib = lax.dynamic_slice_in_dim(w_idx, t0, Q_BLOCK, axis=1).astype(jnp.float32)
        q_pos = t0 + jnp.arange(Q_BLOCK)
        dots = jnp.einsum('bqhd,bsd->bqhs', qib, k_idx_f) * (IDX_DIM ** -0.5)
        scores = jnp.einsum('bqh,bqhs->bqs', wib, jax.nn.relu(dots))
        causal = key_pos[None, :] <= q_pos[:, None]
        scores = jnp.where(causal[None], scores, -jnp.inf)
        _, idx = lax.top_k(scores, topk)
        k_sel = k[b_ix, idx]
        v_sel = v[b_ix, idx]
        logits = jnp.einsum('bqhd,bqkhd->bqhk', qb, k_sel).astype(jnp.float32) * scale
        dist = q_pos[None, :, None] - idx
        bias = bias_tab[t5_bucket_3(dist)].astype(jnp.float32)
        logits = logits + jnp.transpose(bias, (0, 1, 3, 2))
        logits = jnp.where((dist >= 0)[:, :, None, :], logits, -jnp.inf)
        p = jax.nn.softmax(logits, axis=-1)
        return jnp.einsum('bqhk,bqkhd->bqhd', p.astype(v.dtype), v_sel)

    outs = lax.map(block, jnp.arange(S // Q_BLOCK))
    return jnp.transpose(outs, (1, 0, 2, 3, 4)).reshape(B, S, H * Dh)

def moba_attention(q, k, v, bias_tab):
    B, S, H, Dh = q.shape
    scale = Dh ** -0.5
    nb = -(-S // MOBA_BLOCK)
    pad = nb * MOBA_BLOCK - S
    kp = jnp.pad(k, ((0, 0), (0, pad), (0, 0), (0, 0))).reshape(B, nb, MOBA_BLOCK, H, Dh)
    vp = jnp.pad(v, ((0, 0), (0, pad), (0, 0), (0, 0))).reshape(B, nb, MOBA_BLOCK, H, Dh)
    counts = jnp.minimum(S - jnp.arange(nb) * MOBA_BLOCK, MOBA_BLOCK).astype(jnp.float32)
    k_mean = kp.astype(jnp.float32).sum(axis=2) / counts[None, :, None, None]
    kbT = jnp.transpose(kp, (0, 3, 1, 2, 4))
    vbT = jnp.transpose(vp, (0, 3, 1, 2, 4))
    n_sel = min(MOBA_TOPK, nb - 1)
    C = MOBA_Q_CHUNK
    b_ix = jnp.arange(B)[:, None, None, None]
    h_ix = jnp.arange(H)[None, None, :, None]
    h_ix5 = jnp.arange(H)[None, None, :, None, None]
    blk_ids = jnp.arange(nb)
    offs = jnp.arange(MOBA_BLOCK)

    def chunk(i):
        t0 = i * C
        qc = lax.dynamic_slice_in_dim(q, t0, C, axis=1)
        q_pos = t0 + jnp.arange(C)
        own = q_pos // MOBA_BLOCK
        own_b = jnp.broadcast_to(own[None, :, None, None], (B, C, H, 1))
        if n_sel > 0:
            gate = jnp.einsum('bqhd,bnhd->bqhn', qc.astype(jnp.float32), k_mean)
            past = blk_ids[None, :] < own[:, None]
            gate = jnp.where(past[None, :, None, :], gate, -jnp.inf)
            _, sel = lax.top_k(gate, n_sel)
            blocks = jnp.concatenate([sel, own_b], axis=-1)
            blk_valid = jnp.concatenate([sel < own[None, :, None, None],
                                         jnp.ones((B, C, H, 1), bool)], axis=-1)
        else:
            blocks = own_b
            blk_valid = jnp.ones((B, C, H, 1), bool)
        k_g = kbT[b_ix, h_ix, blocks]
        v_g = vbT[b_ix, h_ix, blocks]
        logits = jnp.einsum('bqhd,bqhjld->bqhjl', qc, k_g).astype(jnp.float32) * scale
        key_pos = blocks[..., None] * MOBA_BLOCK + offs
        dist = q_pos[None, :, None, None, None] - key_pos
        logits = logits + bias_tab[t5_bucket_3(dist), h_ix5].astype(jnp.float32)
        valid = (dist >= 0) & blk_valid[..., None]
        logits = jnp.where(valid, logits, -jnp.inf)
        J = blocks.shape[-1]
        p = jax.nn.softmax(logits.reshape(B, C, H, J * MOBA_BLOCK), axis=-1)
        p = p.reshape(B, C, H, J, MOBA_BLOCK).astype(v.dtype)
        return jnp.einsum('bqhjl,bqhjld->bqhd', p, v_g)

    outs = lax.map(chunk, jnp.arange(S // C))
    return jnp.transpose(outs, (1, 0, 2, 3, 4)).reshape(B, S, H * Dh)

def third_inputs(seed: int = 0) -> dict:
    key = jax.random.key(seed)
    ks = jax.random.split(key, 20)
    f32 = jnp.float32
    L = DEPTH

    def dense(k, shape):
        return jax.random.normal(k, shape, f32) * (shape[-2] ** -0.5)

    def gain(k, shape):
        return 1.0 + 0.02 * jax.random.normal(k, shape, f32)

    return {
        'x': jax.random.normal(ks[0], (BATCH, SEQ, D_MODEL), f32),
        'ffn1_norm': gain(ks[1], (L, D_MODEL)),
        'ffn1_w_gu': dense(ks[2], (L, D_MODEL, 2 * D_FF_3)),
        'ffn1_w_down': dense(ks[3], (L, D_FF_3, D_MODEL)),
        'mix_norm': gain(ks[4], (L, D_MODEL)),
        'w_in': dense(ks[5], (L, D_MODEL, D_IN_3)),
        'b_gate': 0.1 * jax.random.normal(ks[6], (L, 2 * D_MODEL), f32),
        'q_norm_dsa': gain(ks[7], (L, HEAD_DIM)),
        'k_norm_dsa': gain(ks[8], (L, HEAD_DIM)),
        'q_norm_moba': gain(ks[9], (L, HEAD_DIM)),
        'k_norm_moba': gain(ks[10], (L, HEAD_DIM)),
        'w_branch_dsa': dense(ks[11], (L, W_DSA, D_MODEL)),
        'w_branch_moba': dense(ks[12], (L, W_MOBA, D_MODEL)),
        'w_out': dense(ks[13], (L, D_MODEL, D_MODEL)),
        'ffn2_norm': gain(ks[14], (L, D_MODEL)),
        'ffn2_w_gu': dense(ks[15], (L, D_MODEL, 2 * D_FF_3)),
        'ffn2_w_down': dense(ks[16], (L, D_FF_3, D_MODEL)),
        'rel_bias': 0.1 * jax.random.normal(ks[17], (N_BUCKETS, N_HEADS_DSA + N_HEADS_MOBA), f32),
    }

def third_block(x, ffn1_norm, ffn1_w_gu, ffn1_w_down, mix_norm, w_in, b_gate,
              q_norm_dsa, k_norm_dsa, q_norm_moba, k_norm_moba,
              w_branch_dsa, w_branch_moba, w_out,
              ffn2_norm, ffn2_w_gu, ffn2_w_down, rel_bias):
    B, S, _ = x.shape
    bias_dsa = rel_bias[:, :N_HEADS_DSA]
    bias_moba = rel_bias[:, N_HEADS_DSA:]
    h = x
    for l in range(DEPTH):
        h = h + 0.5 * swiglu_3(rmsnorm(h, ffn1_norm[l]), ffn1_w_gu[l], ffn1_w_down[l])
        u = rmsnorm(h, mix_norm[l])
        qa, ka, va, qb, kb, vb, qi, ki, wi, g = jnp.split(u @ w_in[l], SPLIT_POINTS, axis=-1)
        qa = rmsnorm(qa.reshape(B, S, N_HEADS_DSA, HEAD_DIM), q_norm_dsa[l])
        ka = rmsnorm(ka.reshape(B, S, N_HEADS_DSA, HEAD_DIM), k_norm_dsa[l])
        va = va.reshape(B, S, N_HEADS_DSA, HEAD_DIM)
        qb = rmsnorm(qb.reshape(B, S, N_HEADS_MOBA, HEAD_DIM), q_norm_moba[l])
        kb = rmsnorm(kb.reshape(B, S, N_HEADS_MOBA, HEAD_DIM), k_norm_moba[l])
        vb = vb.reshape(B, S, N_HEADS_MOBA, HEAD_DIM)
        qi = qi.reshape(B, S, N_IDX_HEADS, IDX_DIM)
        wi = wi * (N_IDX_HEADS ** -0.5)
        out_a = dsa_attention(qa, ka, va, qi, ki, wi, bias_dsa)
        out_b = moba_attention(qb, kb, vb, bias_moba)
        gates = jax.nn.sigmoid((g + b_gate[l]).astype(jnp.float32)).astype(h.dtype)
        g_a, g_b = jnp.split(gates, 2, axis=-1)
        mixed = g_a * (out_a @ w_branch_dsa[l]) + g_b * (out_b @ w_branch_moba[l])
        h = h + mixed @ w_out[l]
        h = h + 0.5 * swiglu_3(rmsnorm(h, ffn2_norm[l]), ffn2_w_gu[l], ffn2_w_down[l])
    return h


def setup_inputs(seed=0):
    out = dict(first_inputs(seed))
    for name, value in second_inputs(seed + 1).items():
        if name != "x":
            out[name + "_2"] = value
    for name, value in third_inputs(seed + 2).items():
        if name != "x":
            out[name + "_3"] = value
    return out


def reference(
    x, c, w_mod, b_mod, g_pre_mix, w_in, w_gate_lr, b_gate, g_gla, w_out, g_post_mix, g_pre_ffn,
    router_w, router_b, w_gate_up, b_gate_up, w_down, b_down, g_post_ffn, mem_2, rel_bias_2,
    ffn1_w1_2, ffn1_w3_2, ffn1_w2_2, ln1_g_2, ln1_b_2, w_in_2, q_norm_g_2, kv_norm_g_2, w_q_b_2,
    w_kv_b_2, lam_q1_2, lam_k1_2, lam_q2_2, lam_k2_2, diff_norm_g_2, w_gate_2, b_gate_2,
    w_up_mla_2, w_up_diff_2, w_o_2, ln2_g_2, ln2_b_2, mem_w_q_2, mem_w_kv_2, mem_w_o_2, ln3_g_2,
    ln3_b_2, ffn2_w1_2, ffn2_w3_2, ffn2_w2_2, ln4_g_2, ln4_b_2, ffn1_norm_3, ffn1_w_gu_3,
    ffn1_w_down_3, mix_norm_3, w_in_3, b_gate_3, q_norm_dsa_3, k_norm_dsa_3, q_norm_moba_3,
    k_norm_moba_3, w_branch_dsa_3, w_branch_moba_3, w_out_3, ffn2_norm_3, ffn2_w_gu_3,
    ffn2_w_down_3, rel_bias_3,
):
    x = first_block(
        x, c, w_mod, b_mod, g_pre_mix, w_in, w_gate_lr, b_gate, g_gla, w_out, g_post_mix,
        g_pre_ffn, router_w, router_b, w_gate_up, b_gate_up, w_down, b_down, g_post_ffn,
    )
    x = second_block(
        x, mem_2, rel_bias_2, ffn1_w1_2, ffn1_w3_2, ffn1_w2_2, ln1_g_2, ln1_b_2, w_in_2,
        q_norm_g_2, kv_norm_g_2, w_q_b_2, w_kv_b_2, lam_q1_2, lam_k1_2, lam_q2_2, lam_k2_2,
        diff_norm_g_2, w_gate_2, b_gate_2, w_up_mla_2, w_up_diff_2, w_o_2, ln2_g_2, ln2_b_2,
        mem_w_q_2, mem_w_kv_2, mem_w_o_2, ln3_g_2, ln3_b_2, ffn2_w1_2, ffn2_w3_2, ffn2_w2_2,
        ln4_g_2, ln4_b_2,
    )
    return third_block(
        x, ffn1_norm_3, ffn1_w_gu_3, ffn1_w_down_3, mix_norm_3, w_in_3, b_gate_3, q_norm_dsa_3,
        k_norm_dsa_3, q_norm_moba_3, k_norm_moba_3, w_branch_dsa_3, w_branch_moba_3, w_out_3,
        ffn2_norm_3, ffn2_w_gu_3, ffn2_w_down_3, rel_bias_3,
    )


_drawn_inputs = setup_inputs


def setup_inputs(seed=0):
    import zlib

    import numpy as np

    out = dict(_drawn_inputs(seed))
    spreads = {}
    factors = {'router_b': 2.776,
     'b_gate_up': 4.908,
     'b_down': 5.831,
     'g_post_ffn': 2.838,
     'q_norm_g_2': 8.0,
     'kv_norm_g_2': 8.0,
     'lam_q1_2': 3.386,
     'lam_k1_2': 3.084,
     'lam_q2_2': 8.0,
     'lam_k2_2': 8.0,
     'diff_norm_g_2': 5.011,
     'b_gate_2': 6.204,
     'ffn1_norm_3': 4.508,
     'mix_norm_3': 4.056,
     'b_gate_3': 6.575,
     'q_norm_dsa_3': 8.0,
     'k_norm_dsa_3': 8.0,
     'q_norm_moba_3': 8.0,
     'k_norm_moba_3': 8.0,
     'ffn2_norm_3': 7.807,
     'rel_bias_3': 4.147}
    for name, (base, spread) in spreads.items():
        noise = np.random.default_rng([zlib.crc32(name.encode()), seed]).standard_normal(out[name].shape)
        drawn = base * np.exp(spread * noise) if base else spread * noise
        out[name] = __import__('jax').numpy.asarray(drawn.astype(out[name].dtype))
    for name, factor in factors.items():
        out[name] = (out[name] * factor).astype(out[name].dtype)
    return out
```

```python
import math
from contextlib import ExitStack

import numpy as np

import concourse.bass as bass
from concourse import mybir

P = 128
D = 1024
S = 256
TT = S // P
KD = D // P
NEG = -1.0e30
TAKEN = -3.0e38

N_EXP, TOP_K, F_MOE = 32, 4, 1024
CAP = P
F_FFN = 2816
GLU = 256
ATT_W, HD = 512, 64
IN1 = 3088
IN2 = 2208
IN3 = 5444
MLA_H, MLA_NOPE, MLA_ROPE = 8, 64, 32
MLA_QK = MLA_NOPE + MLA_ROPE
DSA_TOPK = 64
ALPHA = 2.0 ** 0.25
LAM_INIT = 0.8 - 0.6 * math.exp(-0.3 * 0)
SLOTS = 6
SLOT_K = 4
GEMM_BANKS = 4
LOOKAHEAD = 2

ALU = mybir.AluOpType
ACT = mybir.ActivationFunctionType
AX = mybir.AxisListType.X
F32 = mybir.dt.float32
I32 = mybir.dt.int32
U32 = mybir.dt.uint32


def shape_constants():
    t = np.arange(P)
    q, k = P + t[:, None], np.arange(S)[None, :]
    dist = q - k
    count = ((dist >= 0) & (dist <= 128)).astype(np.float64)
    count += (dist >= 0) & (dist % 4 == 0)
    count += (dist >= 0) & (dist % 16 == 0)
    lnc = np.where(count > 0, np.log(np.maximum(count, 1)), NEG)
    causal = np.where(dist >= 0, 0.0, NEG)
    same = (t[:, None] // 64) == (t[None, :] // 64)
    upto = same & (t[:, None] <= t[None, :])
    chunk = np.stack([t // 64 == 0, t // 64 == 1], 1)
    before = t[:, None] < t[None, :]

    def angles(inv):
        a = np.arange(S, dtype=np.float32)[:, None] * inv[None, :].astype(np.float32)
        a = a.reshape(TT, P, -1).transpose(1, 0, 2).reshape(P, -1)
        return np.cos(a), np.sin(a)

    half1 = np.float32(10000.0) ** (-np.arange(32, dtype=np.float32) / np.float32(32))
    half2 = np.float32(10000.0) ** (-np.arange(0, 32, 2, dtype=np.float32) / np.float32(32))
    cos1, sin1 = angles(half1)
    cos2, sin2 = angles(half2)
    parts = {
        "ident": np.eye(P), "lnc": lnc, "causal": causal, "upto": upto, "same": same, "chunk": chunk,
        "before": before, "ones": np.ones((P, P)), "ramp": np.tile(np.arange(P), (P, 1)),
        "ramp32": np.tile(np.arange(N_EXP), (P, 1)), "cos1": cos1, "sin1": sin1, "cos2": cos2, "sin2": sin2,
        "half": np.full((P, 16), -0.5),
    }
    at, n = {}, 0
    for name, a in parts.items():
        at[name] = (n, a.shape[1])
        n += a.shape[1]
    table = np.concatenate([np.asarray(a, np.float32) for a in parts.values()], 1)
    d = (S - 1) - np.arange(384)
    n_ = np.maximum(d, 1).astype(np.float32)
    large = 16 + (np.log(n_ / np.float32(16)) / np.float32(math.log(8.0)) * np.float32(16)).astype(np.int32)
    bucket = np.where(np.maximum(d, 0) < 16, np.maximum(d, 0), np.minimum(large, 31))
    onehot = (np.arange(32)[:, None] == bucket[None, :]) & (d >= 0)[None, :]
    ahead = np.tile(np.where(d >= 0, 0.0, NEG)[None, :], (32, 1))
    buckets = np.concatenate([onehot, ahead], 1).astype(np.float32)
    mask = np.tile(upto.astype(np.int32), (1, 4))
    return table, at, buckets, mask


TABLE, TABLE_AT, BUCKETS, GLA_MASK = shape_constants()


class Chunk:

    def __init__(self, number, parts, kts, cols):
        self.number, self.parts, self.kts, self.cols = number, parts, kts, cols
        self.slot = None
        self.landed = None
        self.after = None
        self.released = None


class Block:

    def __init__(self, col, cols, chunks):
        self.col, self.cols, self.chunks = col, cols, chunks


def build(nc, I, out):
    ctx = ExitStack()
    with ctx:
        sb = lambda name, shape, dt=F32: ctx.enter_context(nc.sbuf_tensor(name, shape, dt))
        sems = {}

        def sem(name):
            if name not in sems:
                sems[name] = ctx.enter_context(nc.semaphore(name))
            return sems[name]

        ring = sb("ring", [P, SLOTS, SLOT_K, 512])
        arena = sb("arena", [P, 12672])
        X = sb("X", [P, TT, D])
        HT = sb("HT", [P, KD, S])
        Y = sb("Y", [P, TT, D])
        H = sb("H", [P, TT, D])
        QT = sb("QT", [P, KD, S])
        KT = sb("KT", [P, KD, S])
        MIX = sb("MIX", [P, TT, D])
        BIAS = sb("BIAS", [P, 8, S])
        VEC = sb("VEC", [P, 4, D])
        PR = sb("PR", [P, 3, 512])
        PT = sb("PT", [P, 2, 512])
        SMALL = sb("SMALL", [P, 1696])
        TAB = sb("TAB", [P, TABLE.shape[1]])
        TMASK = KT[:, 0:2, :].rearrange("p a b -> p (a b)").bitcast(I32)
        st_in = sb("st_in", [P, 16])
        st_out = sb("st_out", [P, 16])
        MX = sb("MX", [P, 3, 2])
        NM = sb("NM", [P, 3, 2])
        LS = sb("LS", [P, 3, 2])
        RL = sb("RL", [P, 2])
        MISC = sb("MISC", [P, 64])
        TOPV = sb("TOPV", [P, 8])
        TOPI = sb("TOPI", [P, 8], U32)
        NPASS = sb("NPASS", [P, 1], I32)
        TOPF = sb("TOPF", [P, 8])
        WGLR = sb("WGLR", [16, 256])
        ZERO = sb("ZERO", [1, 512])
        bank = [ctx.enter_context(nc.psum_tensor(f"bank{i}", [P, 512], F32)) for i in range(8)]

        def tab(name):
            a, n = TABLE_AT[name]
            return TAB[:, a:a + n]

        ident = tab("ident")
        arr_dram = nc.dram_tensor("rel_rows", [24, 384], F32)
        skew_dram = nc.dram_tensor("rel_skew", [24, P * 384], F32)

        def arena_at(a, *shape):
            n = int(np.prod(shape))
            v = arena[:, a:a + n]
            if len(shape) == 2:
                return v.rearrange("p (a b) -> p a b", a=shape[0])
            if len(shape) == 3:
                return v.rearrange("p (a b c) -> p a b c", a=shape[0], b=shape[1])
            return v

        chunks = []

        def product(w, inner, cols, block=512):
            kts = inner // P
            blocks = []
            for c in range(0, cols, block):
                n = min(block, cols - c)
                mine = []
                for k in range(0, kts, SLOT_K):
                    m = min(SLOT_K, kts - k)
                    src = w[k * P:(k + m) * P, c:c + n].rearrange("(k p) n -> p k n", p=P)
                    mine.append(Chunk(len(chunks), [(0, n, src)], m, n))
                    chunks.append(mine[-1])
                blocks.append(Block(c, n, mine))
            return blocks

        def glu_product(w_gate, w_up):
            blocks = []
            for c in range(0, F_FFN, GLU):
                mine = []
                for k in range(0, KD, SLOT_K):
                    parts = [(i * GLU, GLU, w[k * P:(k + SLOT_K) * P, c:c + GLU].rearrange("(k p) n -> p k n", p=P))
                             for i, w in enumerate((w_gate, w_up))]
                    mine.append(Chunk(len(chunks), parts, SLOT_K, 2 * GLU))
                    chunks.append(mine[-1])
                blocks.append(Block(c, GLU, mine))
            return blocks

        G = {}
        vecs = []
        vec_at = {}
        order = []

        def plan_product(name, blocks):
            G[name] = blocks
            for b in blocks:
                order.extend(("chunk", c) for c in b.chunks)

        def plan_vec(name, src, users):
            vec_at[name] = len(vecs)
            order.append(("vec", len(vecs)))
            vecs.append((src, users))

        for i in range(6):
            plan_vec(f"b_mod{i}", I["b_mod"][0:1, i * D:(i + 1) * D], 1)
            plan_product(f"mod{i}", product(I["w_mod"][0][:, i * D:(i + 1) * D], D, D))
        plan_vec("g_pre_mix", I["g_pre_mix"], 1)
        plan_product("in1", product(I["w_in"][0], D, IN1))
        plan_vec("g_post_mix", I["g_post_mix"], 1)
        plan_product("out1", product(I["w_out"][0], D, D))
        plan_vec("g_pre_ffn", I["g_pre_ffn"], 1)
        plan_product("router", product(I["router_w"][0], D, N_EXP))
        order.append(("moe", None))
        order.append(("mem", None))
        plan_vec("g_post_ffn", I["g_post_ffn"], 1)

        def plan_ffn(name, w1, w3, w2):
            plan_product(name + "_up", glu_product(w1, w3))
            plan_product(name + "_down", product(w2, F_FFN, D))

        def plan_ln(n):
            plan_vec(f"ln{n}_g", I[f"ln{n}_g_2"], 1)
            plan_vec(f"ln{n}_b", I[f"ln{n}_b_2"], 1)

        plan_ffn("f1", I["ffn1_w1_2"][0], I["ffn1_w3_2"][0], I["ffn1_w2_2"][0])
        plan_ln(1)
        plan_product("in2", product(I["w_in_2"][0], D, IN2))
        for i in range(2):
            plan_vec(f"b_gate2_{i}", I["b_gate_2"][0:1, i * D:(i + 1) * D], 1)
        plan_product("gate2", product(I["w_gate_2"][0], D, 2 * D))
        plan_product("q_b", product(I["w_q_b_2"][0], 384, MLA_H * MLA_QK))
        plan_product("kv_b", product(I["w_kv_b_2"][0], 256, D))
        plan_product("up_mla", product(I["w_up_mla_2"][0], 512, D))
        plan_product("up_diff", product(I["w_up_diff_2"][0], 512, D))
        plan_product("o2", product(I["w_o_2"][0], D, D))
        order.append(("bias", 1))
        plan_ln(2)
        plan_product("mem_q", product(I["mem_w_q_2"][0], D, D))
        plan_product("mem_kv", product(I["mem_w_kv_2"][0], D, 2 * D))
        plan_product("mem_o", product(I["mem_w_o_2"][0], D, D))
        plan_ln(3)
        plan_ffn("f2", I["ffn2_w1_2"][0], I["ffn2_w3_2"][0], I["ffn2_w2_2"][0])
        plan_ln(4)
        plan_vec("ffn1_norm", I["ffn1_norm_3"], 1)
        plan_ffn("f3", I["ffn1_w_gu_3"][0][:, 0:F_FFN], I["ffn1_w_gu_3"][0][:, F_FFN:2 * F_FFN], I["ffn1_w_down_3"][0])
        plan_vec("mix_norm", I["mix_norm_3"], 1)
        for i in range(2):
            plan_vec(f"b_gate3_{i}", I["b_gate_3"][0:1, i * D:(i + 1) * D], 1)
        plan_product("in3", product(I["w_in_3"][0], D, IN3))
        order.append(("bias", 2))
        plan_product("br_dsa", product(I["w_branch_dsa_3"][0], 512, D))
        plan_product("br_moba", product(I["w_branch_moba_3"][0], 512, D))
        plan_product("out3", product(I["w_out_3"][0], D, D))
        plan_vec("ffn2_norm", I["ffn2_norm_3"], 1)
        plan_ffn("f4", I["ffn2_w_gu_3"][0][:, 0:F_FFN], I["ffn2_w_gu_3"][0][:, F_FFN:2 * F_FFN], I["ffn2_w_down_3"][0])

        loads_of = [0] * SLOTS
        owner = [None] * SLOTS
        turn = 0
        before_moe = None
        for kind, c in order:
            if kind == "moe":
                before_moe = list(owner)
                owner = ["moe"] * SLOTS
                turn = 0
            if kind == "chunk":
                c.slot = turn % SLOTS
                turn += 1
                c.after = owner[c.slot]
                loads_of[c.slot] += 16 * len(c.parts)
                c.landed = loads_of[c.slot]
                owner[c.slot] = c

        landed = [sem(f"ring_landed{i}") for i in range(SLOTS)]
        chunk_used = sem("chunk_used")
        unit_done = sem("unit_done")
        unit_read = sem("unit_read")
        turned = sem("turned")
        turned_read = sem("turned_read")
        att_shifted = sem("att_shifted")
        att_exp = sem("att_exp")
        out_done = sem("out_done")
        out_read = sem("out_read")
        pow_in = sem("pow_in")
        pow_out = sem("pow_out")
        vec_landed = [sem(f"vec_landed{i}") for i in range(4)]
        vec_used = sem("vec_used")
        E = sem

        used = done = 0

        MOD = arena_at(0, 6, D)
        PROJ1 = arena_at(6144, TT, IN1)
        AF = arena_at(0, TT, F_FFN)
        AFT = arena_at(5632, F_FFN // P, S)
        PROJ2 = arena_at(0, TT, IN2)
        GATE2 = arena_at(4416, TT, 2 * D)
        QM = arena_at(8512, TT, MLA_H * MLA_QK)
        KV = arena_at(10048, TT, D)
        CT = PT[:, :, :].rearrange("p a b -> p (a b)")
        KVM = arena_at(0, TT, 2 * D)
        QMEM = arena_at(4096, TT, D)
        PROJ3 = arena_at(0, TT, IN3)
        SEL = arena_at(10888, TT, S)

        small_at = {}

        def small(name, n, src=None):
            if name not in small_at:
                a = sum(m for _, m, _ in small_at.values())
                small_at[name] = (a, n, src)
            a, n, _ = small_at[name]
            return SMALL[:, a:a + n]

        for name, n in (("g_gla", 128), ("b_gate", 256), ("q_norm_g_2", 384), ("kv_norm_g_2", 256), ("lam_q1_2", 64),
                        ("lam_k1_2", 64), ("lam_q2_2", 64), ("lam_k2_2", 64), ("diff_norm_g_2", 128),
                        ("q_norm_dsa_3", 64), ("k_norm_dsa_3", 64), ("q_norm_moba_3", 64), ("k_norm_moba_3", 64),
                        ("router_b", 32)):
            small(name, n, I[name])

        class Attention:

            def __init__(self, heads, scale, q, k, v, dv, bias, put, causal=True, extra=None, step=2):
                self.heads, self.scale, self.q, self.k, self.v, self.dv = heads, scale, q, k, v, dv
                self.bias, self.put, self.causal, self.extra = bias, put, causal, extra
                self.step = step
                self.units = [(h, tt) for h in range(heads) if h % (2 * step) < step for tt in range(TT)]

            def keys(self, tt):
                return P * (tt + 1) if self.causal else S

        def pair_t(t, base, h):
            r = HD * (h % 2)
            return [t[r:r + HD, base + h // 2, :]]

        def row_mask(name):
            def f(h, tt):
                m = tab(name)[:, P:S] if tt == 0 else tab(name)
                n = P * (tt + 1)
                return m.unsqueeze(1).to_broadcast([P, 2, n])
            return f

        def head_bias(h, tt):
            return BIAS[:, h:h + 3:2, P:S] if tt == 0 else BIAS[:, h:h + 3:2, :]

        def into(buf, base, dv, heads, step=2):
            return lambda h, tt: (buf[:, tt, base:base + heads * dv].rearrange("p (h e) -> p h e", h=heads)
                                  [:, h:h + step + 1:step, :])

        A_DIL = Attention(8, HD ** -0.5, lambda h: pair_t(QT, 0, h), lambda h: pair_t(QT, 4, h),
                          lambda h, t: PROJ1[:, t, 1024 + HD * h:1024 + HD * (h + 1)], HD, row_mask("lnc"), into(MIX, 0, HD, 8))
        A_MLA = Attention(8, MLA_QK ** -0.5, lambda h: [QT[0:MLA_QK, h, :]], lambda h: [KT[0:MLA_QK, h, :]],
                          lambda h, t: KV[:, t, P * h + MLA_NOPE:P * (h + 1)], HD, row_mask("causal"), into(MIX, 0, HD, 8, 1),
                          step=1)
        OD8 = Y
        A_DIFF = Attention(8, HD ** -0.5, lambda h: pair_t(QT, 0, h), lambda h: pair_t(QT, 4, h),
                           lambda h, t: PROJ2[:, t, 1696 + P * (h // 2):1696 + P * (h // 2 + 1)], P, head_bias, into(OD8, 0, P, 8))
        A_MEM = Attention(4, 256 ** -0.5, lambda h: [QT[:, 2 * h, :], QT[:, 2 * h + 1, :]],
                          lambda h: [KT[:, 2 * h, :], KT[:, 2 * h + 1, :]],
                          lambda h, t: KVM[:, t, D + 256 * h:D + 256 * (h + 1)], 256, None, into(MIX, 0, 256, 4, 1), causal=False,
                          step=1)
        A_DSA = Attention(8, HD ** -0.5, lambda h: pair_t(QT, 0, h), lambda h: pair_t(QT, 4, h),
                          lambda h, t: PROJ3[:, t, 1024 + HD * h:1024 + HD * (h + 1)], HD, head_bias, into(MIX, 0, HD, 8),
                          extra=lambda tt: SEL[:, tt, 0:P * (tt + 1)].unsqueeze(1).to_broadcast([P, 2, P * (tt + 1)]))
        A_MOBA = Attention(8, HD ** -0.5, lambda h: pair_t(KT, 0, h), lambda h: pair_t(KT, 4, h),
                           lambda h, t: PROJ3[:, t, 2560 + HD * h:2560 + HD * (h + 1)], HD, head_bias, into(MIX, 512, HD, 8))

        LA = QT[:, 0:2, :]
        GB = QT[:, 2:6, :].rearrange("p (t a) b -> p t (a b)", t=2)
        QKD = H[:, :, 0:512]
        KL = H[:, :, 512:768]
        GT = KT[:, 2:6, :]
        ATTM = PR[:, 0:2, :]
        STATE = PT[:, :, :].rearrange("p a b -> p (a b)").rearrange("p (n m e) -> p n m e", n=4, m=2)
        OG = Y[:, :, 0:512]
        SR = Y[:, :, 512:1024]
        GSQ = H[:, :, 0:512]
        AN = MISC[:, 0:8].rearrange("p (m n) -> p m n", m=2)
        GLRT = QT[0:16, 6, :]

        MO = 6144
        XET = arena_at(MO, KD, CAP)
        GU = arena_at(MO + 1024, 2 * F_MOE)
        GL = arena_at(MO + 3072, F_MOE)
        SG = arena_at(MO + 4096, F_MOE)
        AV = arena_at(MO + 5120, F_MOE)
        AVT = Y[:, 0, :].rearrange("p (k c) -> p k c", k=KD)
        OUTE = Y[:, 1, :]
        PSEL = QT[:, 0, :].rearrange("p (t c) -> p t c", t=2)
        GSEL = QT[:, 1, :].rearrange("p (t c) -> p t c", t=2)
        GSELT = QT[:, 2, :]
        BROW = arena_at(0, 2 * F_MOE)[0:1, :]
        BB = MIX[:, :, :].rearrange("p a b -> p (a b)")
        MASKS = QT[:, 3, 0:64].rearrange("p (t e) -> p t e", t=2)
        GATES = QT[:, 3, 64:128].rearrange("p (t e) -> p t e", t=2)
        POS = [QT[:, 3, 128 + 32 * t:160 + 32 * t] for t in range(TT)]
        RT = QT[:, 4, 0:64].rearrange("p (t e) -> p t e", t=2)
        GATET = QT[0:32, 5, :]
        TMP32 = QT[:, 4, 64:96]
        BDOWN = KT[0:32, 0:4, :].rearrange("p a b -> p (a b)")
        glu_in = GU.rearrange("p (f two) -> p f two", two=2)

        CB = QT[:, 0:4, :].rearrange("p a b -> p (a b)").rearrange("p (k c) -> p k c", k=KD)
        BUCK = HT[0:32, 0:3, :].rearrange("p a b -> p (a b)")
        SMALLB = HT[0:32, 3, 0:24]
        RELS = HT[0:24, 4:6, :].rearrange("p a b -> p (a b)")[:, 0:384]
        CCOL = MISC[:, 0:8]
        KM = Y
        CTILE = QT
        KI2 = PT[:, :, 0:P]
        SQ = PR[:, :, :].rearrange("p a b -> p (a b)")[:, 0:D]

        m_landed = [sem(f"moe_landed{i}") for i in range(SLOTS)]
        m_used = sem("moe_chunk_used")
        m_read = sem("moe_block_read")
        m_sel = sem("moe_sel")
        m_gather = sem("moe_gather")
        m_x = sem("moe_x")
        m_gt = sem("moe_gate_turned")
        m_gtc = sem("moe_gate_copied")
        m_glu = sem("moe_glu")
        m_sig = sem("moe_sigmoid")
        m_act = sem("moe_act")
        m_tr = sem("moe_act_turned")
        m_at = sem("moe_act_copied")
        m_brow = sem("moe_bias_row")
        m_bias = sem("moe_bias")
        m_pass = sem("moe_pass")
        m_chain = sem("moe_dve_step")
        M_STEPS = 2

        block = ctx.enter_context(nc.Block())
        pows = {"n": 0}
        POWS_FIRST = 8
        UNIT_OF = {}

        @block.tensor
        def _(pe):
            unit = [0]
            group = [0]
            outs = [0]
            chunks_used = [0]
            att = [0]

            def gemm(name, lhs, tts=TT, kt0=0):
                for b in G[name]:
                    kt_all = sum(c.kts for c in b.chunks)
                    kt = 0
                    for c in b.chunks:
                        pe.wait_ge(landed[c.slot], c.landed)
                        last_chunk = c is b.chunks[-1]
                        for tt in range(tts):
                            u = unit[0] + tt
                            if kt == 0 and u >= GEMM_BANKS:
                                pe.wait_ge(unit_read, u - GEMM_BANKS + 1)
                            for j in range(c.kts):
                                mm = pe.matmul(bank[u % GEMM_BANKS][:, 0:c.cols], lhs(kt + j + kt0, tt),
                                               ring[:, c.slot, j, 0:c.cols], start=(kt + j == 0),
                                               stop=(kt + j == kt_all - 1))
                            if last_chunk:
                                mm.then_inc(unit_done, 1)
                        kt += c.kts
                        if last_chunk:
                            c.released = (unit_done, unit[0] + tts)
                        else:
                            mm.then_inc(chunk_used, 1)
                            chunks_used[0] += 1
                            c.released = (chunk_used, chunks_used[0])
                    unit[0] += tts

            def turn(tiles):
                for i in range(0, len(tiles), 4):
                    g = group[0]
                    if g >= 2:
                        pe.wait_ge(turned_read, g - 1)
                    for j, src in enumerate(tiles[i:i + 4]):
                        w = src.shape[1]
                        mm = pe.transpose(bank[4 + g % 2][0:w, P * j:P * (j + 1)], src, ident)
                    mm.then_inc(turned, 1)
                    group[0] += 1

            def turned_all():
                pe.wait_ge(turned_read, group[0])

            def turn_rows(buf, base=0, n=KD):
                turn([buf[:, tt, base + P * k:base + P * (k + 1)] for tt in range(TT) for k in range(n)])
                turned_all()

            def next_unit():
                u = unit[0]
                if u >= GEMM_BANKS:
                    pe.wait_ge(unit_read, u - GEMM_BANKS + 1)
                unit[0] += 1
                return bank[u % GEMM_BANKS]

            def attend(a):
                n = len(a.units)

                def scores(i):
                    h, tt = a.units[i]
                    nk = a.keys(tt)
                    b = next_unit()
                    for hh in range(2):
                        qs, ks = a.q(h + a.step * hh), a.k(h + a.step * hh)
                        for j in range(len(qs)):
                            mm = pe.matmul(b[:, hh * nk:(hh + 1) * nk], qs[j][:, tt * P:(tt + 1) * P], ks[j][:, 0:nk],
                                           start=(j == 0), stop=(j == len(qs) - 1))
                    mm.then_inc(unit_done, 1)

                def values(i):
                    h, tt = a.units[i]
                    nk = a.keys(tt)
                    k = att[0] + i
                    pe.wait_ge(att_exp, k + 1)
                    p = PR[:, k % 3, 0:2 * nk]
                    turn([p[:, P * j:P * (j + 1)] for j in range(2 * nk // P)])
                    turned_all()
                    o = outs[0]
                    if o >= 2:
                        pe.wait_ge(out_read, o - 1)
                    for hh in range(2):
                        for t in range(nk // P):
                            j = hh * (nk // P) + t
                            mm = pe.matmul(bank[6 + o % 2][:, hh * a.dv:(hh + 1) * a.dv], PT[:, k % 2, P * j:P * (j + 1)],
                                           a.v(h + a.step * hh, t), start=(t == 0), stop=(t == nk // P - 1))
                    mm.then_inc(out_done, 1)
                    outs[0] += 1

                for i in range(n + LOOKAHEAD):
                    if i < n:
                        scores(i)
                    if i >= LOOKAHEAD:
                        values(i - LOOKAHEAD)
                att[0] += n

            ht = lambda kt, tt: HT[:, kt, tt * P:(tt + 1) * P]

            pe.wait_ge(E("setup"), 16 * 4)
            b = next_unit()
            pe.matmul(b[0:24, 0:384], SMALLB[:, 0:24], BUCK[:, 0:384], start=True, stop=True).then_inc(unit_done, 1)
            pe.wait_ge(E("c_spread"), 1)
            for i in range(6):
                gemm(f"mod{i}", lambda kt, tt: CB[:, kt, :], tts=1)
            pe.wait_ge(E("h1"), 1)
            turn_rows(H)
            gemm("in1", ht)
            pe.wait_ge(E("rope1"), 1)
            turn_rows(Y)
            attend(A_DIL)
            pe.wait_ge(E("dil_out"), 1)
            turn([PROJ1[:, tt, 3072:3088] for tt in range(TT)])
            turned_all()
            pe.wait_ge(E("gate_lr"), 16)
            b = next_unit()
            for tt in range(TT):
                mm = pe.matmul(b[:, 256 * tt:256 * (tt + 1)], GLRT[:, tt * P:(tt + 1) * P], WGLR[:, :], start=True, stop=True)
            mm.then_inc(unit_done, 1)
            pe.wait_ge(E("log_a"), 1)
            for tt in range(TT):
                b = next_unit()
                pe.matmul(b[:, 0:256], tab("upto"), LA[:, tt, :], start=True, stop=True)
                pe.matmul(b[:, 256:512], tab("same"), LA[:, tt, :], start=True, stop=True).then_inc(unit_done, 1)
            b = next_unit()
            for m in range(2):
                for tt in range(TT):
                    mm = pe.matmul(b[:, 4 * m + 2 * tt:4 * m + 2 * tt + 2], LA[:, tt, m * P:(m + 1) * P], tab("chunk"),
                                   start=True, stop=True)
            mm.then_inc(unit_done, 1)
            pe.wait_ge(E("gla_qk"), 1)
            turn([QKD[:, tt, P * k:P * (k + 1)] for tt in range(TT) for k in range(4)])
            turned_all()
            for tt in range(TT):
                for par in range(2):
                    b = next_unit()
                    r = HD * par
                    for m in range(2):
                        mm = pe.matmul(b[:, P * m:P * (m + 1)], GT[r:r + HD, 2 + m, tt * P:(tt + 1) * P],
                                       GT[r:r + HD, m, tt * P:(tt + 1) * P], start=True, stop=True)
                    mm.then_inc(unit_done, 1)
            for some in ((0, 2), (1,)):
                b = next_unit()
                for c in some:
                    tt, r = c // 2, HD * (c % 2)
                    for h in range(4):
                        o = HD * (h % 2)
                        mm = pe.matmul(b[o:o + HD, 256 * tt + P * (h // 2):256 * tt + P * (h // 2 + 1)],
                                       KL[r:r + HD, tt, HD * h:HD * (h + 1)],
                                       PROJ1[r:r + HD, tt, 2048 + P * h:2048 + P * (h + 1)], start=True, stop=True)
                mm.then_inc(unit_done, 1)
            pe.wait_ge(E("gla_state"), 1)
            for tt in range(TT):
                b = next_unit()
                for h in range(4):
                    mm = pe.matmul(b[:, P * h:P * (h + 1)], ATTM[:, tt, P * h:P * (h + 1)],
                                   PROJ1[:, tt, 2048 + P * h:2048 + P * (h + 1)], start=True, stop=True)
                mm.then_inc(unit_done, 1)
                for par in range(2):
                    b = next_unit()
                    r = HD * par
                    for c in range(2):
                        n = 2 * tt + c
                        for m in range(2):
                            mm = pe.matmul(b[HD * c:HD * (c + 1), P * m:P * (m + 1)], GT[r:r + HD, m, n * HD:(n + 1) * HD],
                                           STATE[r:r + HD, n, m, :], start=True, stop=True)
                    mm.then_inc(unit_done, 1)
            pe.wait_ge(E("mix1"), 1)
            turn_rows(MIX)
            gemm("out1", ht)
            pe.wait_ge(E("h2"), 1)
            turn_rows(H)
            gemm("router", ht)
            pe.wait_ge(E("routed"), 1)
            b = next_unit()
            pe.matmul(b[:, 0:32], tab("before"), MASKS[:, 0, :], start=True, stop=True)
            pe.matmul(b[:, 32:64], tab("ones"), MASKS[:, 0, :], start=True, stop=False)
            pe.matmul(b[:, 32:64], tab("before"), MASKS[:, 1, :], start=False, stop=True)
            pe.matmul(b[:, 64:96], tab("ones"), MASKS[:, 0, :], start=True, stop=False)
            pe.matmul(b[:, 64:96], tab("ones"), MASKS[:, 1, :], start=False, stop=True).then_inc(unit_done, 1)
            turn([GATES[:, tt, :] for tt in range(TT)])
            turned_all()
            pe.wait_ge(unit_read, unit[0])
            pe.wait_ge(E("b_down"), 16)
            for tt in range(TT):
                for n in range(2):
                    pe.matmul(bank[2 * tt + n][:, :], GATET[:, tt * P:(tt + 1) * P], BDOWN[:, 512 * n:512 * (n + 1)],
                              start=True, stop=False, skip_group_check=True)
            pe.wait_ge(E("n_pass"), 1)
            n_pass = pe.value_load(NPASS[0:1, 0:1], min_val=1, max_val=2)
            with pe.Fori(0, n_pass) as ps:
                with pe.Fori(0, N_EXP) as ex:
                    it = ps * N_EXP + ex
                    pe.wait_ge(m_sel, it + 1)
                    for half in range(2):
                        for k in range(4):
                            for tt in range(TT):
                                kk = 4 * half + k
                                mm = pe.matmul(bank[6 + half][:, P * k:P * (k + 1)], H[:, tt, P * kk:P * (kk + 1)],
                                               PSEL[:, tt, :], start=(tt == 0), stop=(tt == TT - 1))
                        mm.then_inc(m_gather, 1)
                    pe.wait_ge(m_x, it * 2 + 2)

                    def moe_block(b, lhs):
                        pe.wait_ge(m_read, it * 6 + b + 1)
                        for j in range(2):
                            c = 2 * b + j
                            pe.wait_ge(m_landed[c % SLOTS], (it * 2 + c // SLOTS + 1) * 16)
                            for k in range(SLOT_K):
                                mm = pe.matmul(bank[4 + b % 2][:, :], lhs[:, SLOT_K * j + k, :], ring[:, c % SLOTS, k, :],
                                               start=(j == 0 and k == 0), stop=(j == 1 and k == SLOT_K - 1))
                            mm.then_inc(m_used, 1)

                    for b in range(4):
                        moe_block(b, XET)
                    for tt in range(TT):
                        mm = pe.transpose(bank[6][:, P * tt:P * (tt + 1)], GSEL[:, tt, :], ident)
                    mm.then_inc(m_gt, 1)
                    pe.wait_ge(m_act, it + 1)
                    for half in (1, 0):
                        if half == 0:
                            pe.wait_ge(m_gtc, it + 1)
                        for k in range(4):
                            kk = 4 * (1 - half) + k
                            mm = pe.transpose(bank[6 + half][:, P * k:P * (k + 1)], AV[:, P * kk:P * (kk + 1)], ident)
                        mm.then_inc(m_tr, 1)
                    pe.wait_ge(m_at, it * 2 + 2)
                    for b in range(4, 6):
                        moe_block(b, AVT)
                    pe.wait_ge(m_read, it * 6 + 8)
                    for tt in range(TT):
                        for n in range(2):
                            pe.matmul(bank[2 * tt + n][:, :], GSELT[:, tt * P:(tt + 1) * P], OUTE[:, 512 * n:512 * (n + 1)],
                                      start=False, stop=False, skip_group_check=True)
            for tt in range(TT):
                for n in range(2):
                    mm = pe.matmul(bank[2 * tt + n][:, :], ZERO[:, 0:P], ZERO[:, :], start=False, stop=True, skip_group_check=True)
            mm.then_inc(E("moe_over"), 1)
            pe.wait_ge(E("moe_sum"), 1)

            def ffn(name, src, ready):
                pe.wait_ge(E(ready), 1)
                turn_rows(src)
                for i, b in enumerate(G[name + "_up"]):
                    for tt in range(TT):
                        UNIT_OF[(name, b.col, tt)] = unit[0] + TT * i + tt
                gemm(name + "_up", ht)
                pe.wait_ge(E(name + "_act"), 1)
                turn([AF[:, tt, P * k:P * (k + 1)] for k in range(F_FFN // P) for tt in range(TT)])
                turned_all()
                gemm(name + "_down", lambda kt, tt: AFT[:, kt, tt * P:(tt + 1) * P])

            ffn("f1", X, "x1")
            pe.wait_ge(E("ln1"), 1)
            turn_rows(X)
            gemm("in2", ht)
            gemm("gate2", ht)
            pe.wait_ge(E("c_norm"), 1)
            turn([PROJ2[:, tt, P * k:P * (k + 1)] for k in range(5) for tt in range(TT)])
            turned_all()
            ct = lambda kt, tt: CTILE[:, kt, tt * P:(tt + 1) * P]
            gemm("q_b", ct)
            gemm("kv_b", ct, kt0=3)
            pe.wait_ge(E("mla_qk"), 1)
            turn([QM[:, tt, MLA_QK * h:MLA_QK * (h + 1)] for tt in range(TT) for h in range(MLA_H)])
            turn([KM[:, tt, MLA_QK * h:MLA_QK * (h + 1)] for tt in range(TT) for h in range(MLA_H)])
            turned_all()
            attend(A_MLA)
            turn_rows(PROJ2, base=672)
            pe.wait_ge(E("bias2"), 16)
            attend(A_DIFF)
            pe.wait_ge(E("mix2"), 1)
            turn_rows(MIX)
            gemm("up_mla", ht)
            gemm("up_diff", ht, kt0=4)
            pe.wait_ge(E("gated2"), 1)
            turn_rows(MIX)
            gemm("o2", ht)
            pe.wait_ge(E("ln2"), 1)
            turn_rows(X)
            gemm("mem_q", ht)
            pe.wait_ge(E("mem_in"), 16)
            turn_rows(H)
            gemm("mem_kv", ht)
            pe.wait_ge(E("mem_qkv"), 1)
            turn_rows(QMEM)
            turn_rows(KVM)
            attend(A_MEM)
            pe.wait_ge(E("mem_out"), 1)
            turn_rows(MIX)
            gemm("mem_o", ht)
            ffn("f2", X, "ln3")
            ffn("f3", H, "h3")
            pe.wait_ge(E("h4"), 1)
            turn_rows(H)
            gemm("in3", ht)
            pe.wait_ge(E("qk3"), 1)
            turn([PROJ3[:, tt, 3072 + P * k:3072 + P * (k + 1)] for k in range(2) for tt in range(TT)])
            turn([KI2[:, tt, :] for tt in range(TT)])
            turned_all()
            for tt in range(TT):
                nk = P * (tt + 1)
                for par in range(2):
                    b = next_unit()
                    r = HD * par
                    for hh in range(2):
                        mm = pe.matmul(b[:, hh * nk:(hh + 1) * nk], HT[r:r + HD, hh, tt * P:(tt + 1) * P],
                                       HT[r:r + HD, 2, 0:nk], start=True, stop=True)
                    mm.then_inc(unit_done, 1)
            turn_rows(PROJ3)
            turn_rows(PROJ3, base=1536)
            attend(A_DSA)
            attend(A_MOBA)
            pe.wait_ge(E("mix3"), 1)
            turn_rows(MIX)
            gemm("br_dsa", ht)
            gemm("br_moba", ht, kt0=4)
            pe.wait_ge(E("gated3"), 1)
            turn_rows(MIX)
            gemm("out3", ht)
            ffn("f4", H, "h5")


        @block.vector
        def _(dve):
            steps = [0]
            units = [0]
            outs = [0]
            npow = [0]
            vec_done = [0]
            att = [0]
            chain = sem("dve_step")

            def step(ins):
                steps[0] += 1
                ins.then_inc(chain, 1)
                dve.wait_ge(chain, steps[0])

            def mark(ins, name):
                ins.then_inc(E(name), 1)
                dve.wait_ge(E(name), 1)

            def signal(name):
                dve.sem_inc(E(name), 1)

            def unit():
                dve.wait_ge(unit_done, units[0] + 1)
                units[0] += 1
                return bank[(units[0] - 1) % GEMM_BANKS]

            def release(ins):
                ins.then_inc(unit_read, 1)
                dve.wait_ge(unit_read, units[0])

            def vec(name):
                i = vec_at[name]
                dve.wait_ge(vec_landed[i % 4], 16 * (i // 4 + 1))
                return VEC[:, i % 4, :]

            def vec_over(name):
                assert vec_at[name] == vec_done[0], name
                vec_done[0] += 1
                dve.sem_inc(vec_used, 1)

            def rsqrt(src, scale, eps, n=1):
                npow[0] += 1
                dve.tensor_scalar(st_in[:, 0:n], src, scale, eps, ALU.mult, ALU.add).then_inc(pow_in, 1)
                dve.wait_ge(pow_out, npow[0])
                return st_out

            def square_sum(x, col):
                w = x.shape[1]
                step(dve.tensor_tensor_reduce(SQ[:, 0:w], x, x, 1.0, 0.0, ALU.mult, ALU.add, col))

            ss = MISC[:, 32:33]

            def rms_rows(out, x, g):
                square_sum(x, ss)
                r = rsqrt(ss, 1.0 / x.shape[1], 1e-6)
                step(dve.scalar_tensor_tensor(out, x, r[:, 0:1], g, ALU.mult, ALU.mult))

            def rms_heads(x, heads, w, g, scale=1.0):
                sq = SQ[:, 0:heads * w].rearrange("p (h e) -> p h e", h=heads)
                step(dve.tensor_tensor(sq, x, x, ALU.mult))
                step(dve.tensor_reduce(MISC[:, 40:40 + heads], sq, AX, ALU.add))
                r = rsqrt(MISC[:, 40:40 + heads], 1.0 / w, 1e-6, heads)
                rb = r[:, 0:heads].unsqueeze(2).to_broadcast([P, heads, w])
                step(dve.tensor_tensor(x, x, rb, ALU.mult))
                gb = g.unsqueeze(1).to_broadcast([P, heads, w])
                if scale != 1.0:
                    step(dve.scalar_tensor_tensor(x, x, scale, gb, ALU.mult, ALU.mult))
                else:
                    step(dve.tensor_tensor(x, x, gb, ALU.mult))

            def copy_out(name, dst, tts=TT):
                for b in G[name]:
                    for tt in range(tts):
                        release(dve.tensor_copy(dst(tt, b.col, b.cols), unit()[:, 0:b.cols]))

            def layer_norm(n):
                g, b = vec(f"ln{n}_g"), vec(f"ln{n}_b")
                for tt in range(TT):
                    x = X[:, tt, :]
                    step(dve.tensor_reduce(MISC[:, 33:34], x, AX, ALU.add))
                    step(dve.tensor_scalar(MISC[:, 34:35], MISC[:, 33:34], -1.0 / D, None, ALU.mult))
                    step(dve.tensor_scalar(x, x, MISC[:, 34:35], None, ALU.add))
                    square_sum(x, ss)
                    r = rsqrt(ss, 1.0 / D, 1e-5)
                    step(dve.scalar_tensor_tensor(x, x, r[:, 0:1], g, ALU.mult, ALU.mult))
                    step(dve.tensor_tensor(x, x, b, ALU.add))
                vec_over(f"ln{n}_g")
                vec_over(f"ln{n}_b")
                signal(f"ln{n}")

            def add_scaled(name, scale):
                for b in G[name]:
                    for tt in range(TT):
                        y = Y[:, tt, b.col:b.col + b.cols]
                        x = X[:, tt, b.col:b.col + b.cols]
                        release(dve.tensor_scalar(y, unit()[:, 0:b.cols], scale, None, ALU.mult))
                        step(dve.scalar_tensor_tensor(x, x, ALPHA, y, ALU.mult, ALU.add))

            silu_n = [0]

            def ffn_act(name):
                for b in G[name + "_up"]:
                    for tt in range(TT):
                        psum = unit()
                        a = AF[:, tt, b.col:b.col + GLU]
                        silu_n[0] += 1
                        dve.wait_ge(E("silu"), silu_n[0])
                        release(dve.tensor_tensor(a, a, psum[:, GLU:2 * GLU], ALU.mult))
                signal(name + "_act")

            def attend(a):
                n = len(a.units)

                def soften(i):
                    h, tt = a.units[i]
                    nk = a.keys(tt)
                    k = att[0] + i
                    p = PR[:, k % 3, 0:2 * nk].rearrange("p (h n) -> p h n", h=2)
                    s = unit()[:, 0:2 * nk].rearrange("p (h n) -> p h n", h=2)
                    if a.bias is None:
                        release(dve.tensor_scalar(p, s, a.scale, None, ALU.mult))
                    else:
                        release(dve.scalar_tensor_tensor(p, s, a.scale, a.bias(h, tt), ALU.mult, ALU.add))
                    if a.extra is not None:
                        step(dve.tensor_tensor(p, p, a.extra(tt), ALU.add))
                    step(dve.tensor_reduce(MX[:, k % 3, :], p, AX, ALU.max))
                    dve.tensor_scalar(NM[:, k % 3, :], MX[:, k % 3, :], -1.0, None, ALU.mult).then_inc(att_shifted, 1)

                def put(i):
                    h, tt = a.units[i]
                    k = att[0] + i
                    dve.wait_ge(att_exp, k + 1)
                    step(dve.reciprocal(RL[:, :], LS[:, k % 3, :]))
                    dve.wait_ge(out_done, outs[0] + 1)
                    o = bank[6 + outs[0] % 2][:, 0:2 * a.dv].rearrange("p (h e) -> p h e", h=2)
                    outs[0] += 1
                    dve.tensor_tensor(a.put(h, tt), o, RL[:, :].unsqueeze(2).to_broadcast([P, 2, a.dv]),
                                      ALU.mult).then_inc(out_read, 1)
                    dve.wait_ge(out_read, outs[0])

                for i in range(n + LOOKAHEAD):
                    if i < n:
                        soften(i)
                    if i >= LOOKAHEAD:
                        put(i - LOOKAHEAD)
                att[0] += n

            def rotate(x1, x2, o1, o2, cos, sin, t):
                step(dve.tensor_tensor(t[0], x1, cos, ALU.mult))
                step(dve.tensor_tensor(t[1], x2, sin, ALU.mult))
                step(dve.tensor_tensor(t[2], x2, cos, ALU.mult))
                step(dve.tensor_tensor(t[3], x1, sin, ALU.mult))
                step(dve.tensor_tensor(o1, t[0], t[1], ALU.subtract))
                step(dve.tensor_tensor(o2, t[2], t[3], ALU.add))

            step(dve.memset(ZERO[:, :], 0.0))
            step(dve.memset(st_in[:, :], 1.0))
            dve.wait_ge(E("setup"), 64)
            mark(dve.tensor_tensor(RELS, unit()[0:24, 0:384], BUCK[0:24, 384:768], ALU.add), "rel_rows")
            dve.sem_inc(unit_read, 1)
            dve.wait_ge(E("c_act"), 1)
            mark(dve.tensor_copy(CB, CCOL.unsqueeze(2).to_broadcast([P, KD, P])), "c_spread")
            for i in range(6):
                v = vec(f"b_mod{i}")
                for b in G[f"mod{i}"]:
                    c = slice(b.col, b.col + b.cols)
                    release(dve.tensor_tensor(MOD[:, i, c], unit()[:, 0:b.cols], v[:, c], ALU.add))
                vec_over(f"b_mod{i}")
            shift1, scale1, gate1, shift2, scale2, gate2 = (MOD[:, i, :] for i in range(6))

            def gain(scale, name):
                v = vec(name)
                step(dve.scalar_tensor_tensor(scale, scale, 1.0, v, ALU.add, ALU.mult))
                vec_over(name)

            gain(scale1, "g_pre_mix")
            dve.wait_ge(E("x_in"), 16)
            for tt in range(TT):
                rms_rows(H[:, tt, :], X[:, tt, :], scale1)
                step(dve.tensor_tensor(H[:, tt, :], H[:, tt, :], shift1, ALU.add))
            signal("h1")
            copy_out("in1", lambda tt, c, n: PROJ1[:, tt, c:c + n])
            for tt in range(TT):
                x = PROJ1[:, tt, 0:1024].rearrange("p (h two e) -> p two h e", two=2, e=32)
                o = Y[:, tt, :].rearrange("p (h two e) -> p two h e", two=2, e=32)
                t = [H[:, 0, 512 * i:512 * (i + 1)].rearrange("p (h e) -> p h e", e=32) for i in range(2)]
                t += [H[:, 1, 512 * i:512 * (i + 1)].rearrange("p (h e) -> p h e", e=32) for i in range(2)]
                cos = tab("cos1")[:, 32 * tt:32 * (tt + 1)].unsqueeze(1).to_broadcast([P, 16, 32])
                sin = tab("sin1")[:, 32 * tt:32 * (tt + 1)].unsqueeze(1).to_broadcast([P, 16, 32])
                rotate(x[:, 0], x[:, 1], o[:, 0], o[:, 1], cos, sin, t)
            signal("rope1")
            attend(A_DIL)
            signal("dil_out")
            dve.wait_ge(E("small"), 16 * len(small_at))
            gb = small("b_gate", 256).unsqueeze(1).to_broadcast([P, TT, 256])
            az = H[:, :, 0:256]
            release(dve.tensor_tensor(LA, unit()[:, :].rearrange("p (t n) -> p t n", t=TT), gb, ALU.add))
            mark(dve.scalar_tensor_tensor(az, LA, -1.0, LA, ALU.mult, ALU.max), "z_abs")
            dve.wait_ge(E("z_log"), 1)
            step(dve.scalar_tensor_tensor(LA, LA, 0.0, az, ALU.min, ALU.subtract))
            mark(dve.tensor_scalar(LA, LA, 1.0 / 16.0, None, ALU.mult), "log_a")
            for tt in range(TT):
                release(dve.tensor_copy(GB[:, tt, :], unit()[:, :]))
            step(dve.tensor_tensor(GB[:, :, 256:512], GB[:, :, 256:512], GB[:, :, 0:256], ALU.subtract))
            release(dve.tensor_copy(MISC[:, 8:16], unit()[:, 0:8]))
            signal("gla_b")
            dve.wait_ge(E("gla_exp"), 1)
            qg, kg = PROJ1[:, :, 1536:1792], PROJ1[:, :, 1792:2048]
            step(dve.scalar_tensor_tensor(QKD[:, :, 0:256], qg, 64.0 ** -0.5, Y[:, :, 0:256], ALU.mult, ALU.mult))
            step(dve.tensor_tensor(QKD[:, :, 256:512], kg, Y[:, :, 256:512], ALU.mult))
            mark(dve.tensor_tensor(KL, kg, GB[:, :, 256:512], ALU.mult), "gla_qk")
            step(dve.memset(ATTM, 0.0))
            step(dve.memset(STATE[:, 0], 0.0))
            dve.wait_ge(E("gla_mask"), 16)
            for tt in range(TT):
                for par in range(2):
                    dst = ATTM[:, tt, :].rearrange("p (m two c) -> p two m c", m=2, two=2)[:, par]
                    release(dve.copy_predicated(dst, TMASK[:, 0:256].rearrange("p (m c) -> p m c", m=2),
                                                unit()[:, 0:256].rearrange("p (m c) -> p m c", m=2)))
            u02 = unit()[:, :].rearrange("p (n m e) -> p n m e", n=2, m=2)
            step(dve.tensor_copy(STATE[:, 1], u02[:, 0]))
            u1 = unit()[:, 0:256].rearrange("p (m e) -> p m e", m=2)
            for n, u in ((2, u1), (3, u02[:, 1])):
                for m in range(2):
                    step(dve.scalar_tensor_tensor(STATE[:, n, m], STATE[:, n - 1, m], AN[:, m, n - 1:n], u[:, m],
                                                  ALU.mult, ALU.add))
            dve.sem_inc(unit_read, 2)
            signal("gla_state")
            for tt in range(TT):
                release(dve.tensor_copy(OG[:, tt, :], unit()[:, :]))
                for par in range(2):
                    dst = OG[:, tt, :].rearrange("p (m two e) -> p two m e", m=2, two=2)[:, par]
                    release(dve.tensor_tensor(dst, dst, unit()[:, 0:256].rearrange("p (m e) -> p m e", m=2), ALU.add))
                rms_heads(OG[:, tt, :].rearrange("p (h e) -> p h e", h=4), 4, P, small("g_gla", 128))
                dve.wait_ge(E("silu_r"), 1)
                step(dve.tensor_tensor(MIX[:, tt, 512:1024], OG[:, tt, :], SR[:, tt, :], ALU.mult))
            signal("mix1")

            def gated_residual(gate, name):
                v = vec(name)
                step(dve.tensor_tensor(gate, gate, v, ALU.mult))
                vec_over(name)
                for tt in range(TT):
                    y = Y[:, tt, :]
                    rms_rows(y, y, gate)
                    step(dve.tensor_tensor(X[:, tt, :], X[:, tt, :], y, ALU.add))

            copy_out("out1", lambda tt, c, n: Y[:, tt, c:c + n])
            gated_residual(gate1, "g_post_mix")
            gain(scale2, "g_pre_ffn")
            for tt in range(TT):
                rms_rows(H[:, tt, :], X[:, tt, :], scale2)
                step(dve.tensor_tensor(H[:, tt, :], H[:, tt, :], shift2, ALU.add))
            signal("h2")
            for tt in range(TT):
                release(dve.tensor_tensor(RT[:, tt, :], unit()[:, 0:32], small("router_b", 32), ALU.add))
            for tt in range(TT):
                step(dve.max(TOPV[:, :], RT[:, tt, :]))
                step(dve.max_index(TOPI[:, :], TOPV[:, :], RT[:, tt, :]))
                step(dve.tensor_copy(TOPF[:, :], TOPI[:, :]))
                step(dve.tensor_scalar(MISC[:, 50:51], TOPV[:, 0:1], -1.0, None, ALU.mult))
                mark2 = f"top{tt}"
                signal(mark2)
                dve.wait_ge(E(f"top_exp{tt}"), 1)
                step(dve.reciprocal(MISC[:, 51:52], MISC[:, 52:53]))
                step(dve.tensor_scalar(MISC[:, 54:58], MISC[:, 58:62], MISC[:, 51:52], None, ALU.mult))
                for j in range(TOP_K):
                    dst = MASKS[:, tt, :] if j == 0 else TMP32
                    step(dve.tensor_scalar(dst, tab("ramp32"), TOPF[:, j:j + 1], None, ALU.is_equal))
                    if j == 0:
                        step(dve.tensor_scalar(GATES[:, tt, :], dst, MISC[:, 54:55], None, ALU.mult))
                    else:
                        step(dve.tensor_tensor(MASKS[:, tt, :], MASKS[:, tt, :], TMP32, ALU.add))
                        step(dve.scalar_tensor_tensor(GATES[:, tt, :], TMP32, MISC[:, 54 + j:55 + j], GATES[:, tt, :],
                                                      ALU.mult, ALU.add))
            signal("routed")
            b = unit()
            for tt in range(TT):
                step(dve.scalar_tensor_tensor(POS[tt], b[:, 32 * tt:32 * (tt + 1)], 1.0, MASKS[:, tt, :], ALU.add, ALU.mult))
                step(dve.tensor_scalar(POS[tt], POS[tt], -1.0, None, ALU.add))
            step(dve.tensor_reduce(MISC[:, 35:36], b[:, 64:96], AX, ALU.max))
            dve.sem_inc(unit_read, 1)
            mark(dve.tensor_scalar(NPASS[:, :], MISC[:, 35:36], float(CAP), 1.0, ALU.is_gt, ALU.add), "n_pass")
            n_pass = dve.value_load(NPASS[0:1, 0:1], min_val=1, max_val=2)
            dve.sem_inc(m_read, 2)
            with dve.Fori(0, n_pass) as ps:
                with dve.Fori(0, N_EXP) as ex:
                    it = ps * N_EXP + ex
                    for tt in range(TT):
                        ins = dve.tensor_scalar(PSEL[:, tt, :], tab("ramp"), POS[tt][:, bass.ds(ex, 1)], None, ALU.is_equal)
                    ins.then_inc(m_sel, 1)
                    dve.wait_ge(m_sel, it + 1)
                    for tt in range(TT):
                        dve.tensor_scalar(GSEL[:, tt, :], PSEL[:, tt, :], GATES[:, tt, bass.ds(ex, 1)], None, ALU.mult)
                    dve.wait_ge(m_bias, it + 1)
                    for b in range(4):
                        dve.wait_ge(m_used, it * 12 + 2 * b + 8)
                        c = slice(512 * b, 512 * (b + 1))
                        dve.tensor_tensor(GU[:, c], bank[4 + b % 2][:, :], BB[:, c], ALU.add).then_inc(m_read, 1)
                    dve.wait_ge(m_read, it * 6 + 6)
                    dve.tensor_scalar(GL, glu_in[:, :, 0], 7.0, None, ALU.min).then_inc(m_glu, 1)
                    dve.tensor_scalar(AV, glu_in[:, :, 1], 7.0, -7.0, ALU.min, ALU.max).then_inc(m_chain, 1)
                    dve.wait_ge(m_sig, it + 1)
                    dve.wait_ge(m_chain, it * M_STEPS + 1)
                    dve.tensor_tensor(GL, GL, SG, ALU.mult).then_inc(m_chain, 1)
                    dve.wait_ge(m_chain, it * M_STEPS + 2)
                    dve.scalar_tensor_tensor(AV, AV, 1.0, GL, ALU.add, ALU.mult).then_inc(m_act, 1)
                    for b in range(4, 6):
                        dve.wait_ge(m_used, it * 12 + 2 * b + 8)
                        dve.tensor_copy(OUTE[:, 512 * (b - 4):512 * (b - 3)], bank[4 + b % 2][:, :]).then_inc(m_read, 1)
                for tt in range(TT):
                    dve.tensor_scalar(POS[tt], POS[tt], -float(CAP), None, ALU.add).then_inc(m_pass, 1)
                dve.wait_ge(m_pass, ps * TT + TT)
            dve.wait_ge(E("moe_over"), 1)
            for i in range(4):
                step(dve.tensor_copy(Y[:, i // 2, 512 * (i % 2):512 * (i % 2 + 1)], bank[i][:, :]))
            signal("moe_sum")
            gated_residual(gate2, "g_post_ffn")
            signal("x1")

            ffn_act("f1")
            add_scaled("f1_down", 0.5)
            layer_norm(1)
            copy_out("in2", lambda tt, c, n: PROJ2[:, tt, c:c + n])
            for i in range(2):
                v = vec(f"b_gate2_{i}")
                for b in G["gate2"][2 * i:2 * i + 2]:
                    for tt in range(TT):
                        release(dve.tensor_tensor(GATE2[:, tt, b.col:b.col + b.cols], unit()[:, 0:b.cols],
                                                  v[:, b.col - D * i:b.col - D * i + b.cols], ALU.add))
                vec_over(f"b_gate2_{i}")
            signal("gate2_in")
            for tt in range(TT):
                cq, ckv = PROJ2[:, tt, 0:384], PROJ2[:, tt, 384:640]
                rms_rows(cq, cq, small("q_norm_g_2", 384))
                rms_rows(ckv, ckv, small("kv_norm_g_2", 256))
            signal("c_norm")
            for i in range(2):
                step(dve.tensor_tensor_reduce(SQ[:, 0:64], small(f"lam_q{i + 1}_2", 64), small(f"lam_k{i + 1}_2", 64),
                                              1.0, 0.0, ALU.mult, ALU.add, MISC[:, 16 + i:17 + i]))
            signal("lam_in")
            copy_out("q_b", lambda tt, c, n: QM[:, tt, c:c + n])
            copy_out("kv_b", lambda tt, c, n: KV[:, tt, c:c + n])
            dve.wait_ge(E("lam_exp"), 1)
            step(dve.tensor_tensor(MISC[:, 20:21], MISC[:, 19:20], MISC[:, 18:19], ALU.subtract))
            step(dve.tensor_scalar(MISC[:, 21:22], MISC[:, 20:21], -LAM_INIT, None, ALU.add))
            for tt in range(TT):
                cos = tab("cos2")[:, 16 * tt:16 * (tt + 1)]
                sin = tab("sin2")[:, 16 * tt:16 * (tt + 1)]
                t = [SQ[:, 128 * i:128 * (i + 1)].rearrange("p (h e) -> p h e", e=16) for i in range(4)]
                x = QM[:, tt, :].rearrange("p (h e) -> p h e", h=MLA_H)
                spread = lambda a: a.unsqueeze(1).to_broadcast([P, MLA_H, 16])
                rotate(x[:, :, 64:80], x[:, :, 80:96], x[:, :, 64:80], x[:, :, 80:96], spread(cos), spread(sin), t)
                r = PROJ2[:, tt, 640:672]
                t = [SQ[:, 16 * i:16 * (i + 1)] for i in range(4)]
                rotate(r[:, 0:16], r[:, 16:32], r[:, 0:16], r[:, 16:32], cos, sin, t)
                km = KM[:, tt, 0:MLA_H * MLA_QK].rearrange("p (h e) -> p h e", h=MLA_H)
                step(dve.tensor_copy(km[:, :, 0:MLA_NOPE], KV[:, tt, :].rearrange("p (h e) -> p h e", h=MLA_H)[:, :, 0:MLA_NOPE]))
                step(dve.tensor_copy(km[:, :, MLA_NOPE:], r.unsqueeze(1).to_broadcast([P, MLA_H, MLA_ROPE])))
            signal("mla_qk")
            attend(A_MLA)
            dve.wait_ge(E("bias2"), 16)
            attend(A_DIFF)
            signal("diff_done")
            for tt in range(TT):
                o = OD8[:, tt, :].rearrange("p (h two e) -> p two h e", two=2, e=P)
                d = MIX[:, tt, 512:1024].rearrange("p (h e) -> p h e", h=4)
                step(dve.scalar_tensor_tensor(d, o[:, 1], MISC[:, 21:22], o[:, 0], ALU.mult, ALU.add))
                rms_heads(d, 4, P, small("diff_norm_g_2", 128), 1.0 - LAM_INIT)
            signal("mix2")
            dve.wait_ge(E("gate2_sig"), 1)
            for b in G["up_mla"]:
                for tt in range(TT):
                    c = slice(b.col, b.col + b.cols)
                    release(dve.tensor_tensor(Y[:, tt, c], unit()[:, 0:b.cols], GATE2[:, tt, c], ALU.mult))
            for b in G["up_diff"]:
                for tt in range(TT):
                    c = slice(b.col, b.col + b.cols)
                    release(dve.tensor_tensor(MIX[:, tt, c], unit()[:, 0:b.cols],
                                              GATE2[:, tt, D + b.col:D + b.col + b.cols], ALU.mult))
                    step(dve.tensor_tensor(MIX[:, tt, c], MIX[:, tt, c], Y[:, tt, c], ALU.add))
            signal("gated2")
            add_scaled("o2", 1.0)
            layer_norm(2)
            copy_out("mem_q", lambda tt, c, n: QMEM[:, tt, c:c + n])
            copy_out("mem_kv", lambda tt, c, n: KVM[:, tt, c:c + n])
            signal("mem_qkv")
            attend(A_MEM)
            signal("mem_out")
            add_scaled("mem_o", 1.0)
            layer_norm(3)
            ffn_act("f2")
            add_scaled("f2_down", 0.5)
            layer_norm(4)

            def normed(name, ready):
                v = vec(name)
                for tt in range(TT):
                    rms_rows(H[:, tt, :], X[:, tt, :], v)
                vec_over(name)
                signal(ready)

            def add_half(name, scale=0.5):
                for b in G[name]:
                    for tt in range(TT):
                        x = X[:, tt, b.col:b.col + b.cols]
                        release(dve.scalar_tensor_tensor(x, unit()[:, 0:b.cols], scale, x, ALU.mult, ALU.add))

            normed("ffn1_norm", "h3")
            ffn_act("f3")
            add_half("f3_down")
            normed("mix_norm", "h4")
            copy_out("in3", lambda tt, c, n: PROJ3[:, tt, c:c + n])
            for i in range(2):
                v = vec(f"b_gate3_{i}")
                for tt in range(TT):
                    g = PROJ3[:, tt, 3396 + D * i:3396 + D * (i + 1)]
                    step(dve.tensor_tensor(g, g, v, ALU.add))
                vec_over(f"b_gate3_{i}")
            signal("gate3_in")
            for tt in range(TT):
                step(dve.tensor_copy(KI2[:, tt, :].rearrange("p (a e) -> p a e", a=2),
                                     PROJ3[:, tt, 3328:3392].unsqueeze(1).to_broadcast([P, 2, 64])))
                for c, g in ((0, "q_norm_dsa_3"), (512, "k_norm_dsa_3"), (1536, "q_norm_moba_3"), (2048, "k_norm_moba_3")):
                    rms_heads(PROJ3[:, tt, c:c + 512].rearrange("p (h e) -> p h e", h=8), 8, HD, small(g, 64))
                step(dve.tensor_scalar(MISC[:, 4 * tt:4 * tt + 4], PROJ3[:, tt, 3392:3396], 4.0 ** -0.5, None, ALU.mult))
            signal("qk3")
            for tt in range(TT):
                nk = P * (tt + 1)
                sc = SEL[:, tt, 0:nk]
                for i in range(4):
                    if i % 2 == 0:
                        b = unit()
                    h = 2 * (i % 2) + i // 2
                    w = MISC[:, 4 * tt + h:4 * tt + h + 1]
                    dots = SQ[:, 0:nk]
                    ins = dve.tensor_scalar(dots, b[:, (i % 2) * nk:(i % 2 + 1) * nk], 64.0 ** -0.5, 0.0, ALU.mult, ALU.max)
                    if i % 2 == 1:
                        release(ins)
                    else:
                        step(ins)
                    if i == 0:
                        step(dve.tensor_scalar(sc, dots, w, None, ALU.mult))
                    else:
                        step(dve.scalar_tensor_tensor(sc, dots, w, sc, ALU.mult, ALU.add))
                m = tab("causal")[:, P:S] if tt == 0 else tab("causal")
                step(dve.tensor_tensor(sc, sc, m, ALU.add))
                for r in range(DSA_TOPK // 8):
                    step(dve.max(TOPV[:, :], sc))
                    step(dve.match_replace(sc, TOPV[:, :], sc, TAKEN))
                step(dve.tensor_scalar(sc, sc, TAKEN / 2, NEG, ALU.is_gt, ALU.mult))
            dve.wait_ge(E("bias3a"), 16)
            attend(A_DSA)
            signal("dsa_done")
            dve.wait_ge(E("bias3b"), 16)
            attend(A_MOBA)
            signal("mix3")
            dve.wait_ge(E("gate3_sig"), 1)
            for b in G["br_dsa"]:
                for tt in range(TT):
                    c = slice(b.col, b.col + b.cols)
                    release(dve.tensor_tensor(Y[:, tt, c], unit()[:, 0:b.cols],
                                              PROJ3[:, tt, 3396 + b.col:3396 + b.col + b.cols], ALU.mult))
            for b in G["br_moba"]:
                for tt in range(TT):
                    c = slice(b.col, b.col + b.cols)
                    release(dve.tensor_tensor(MIX[:, tt, c], unit()[:, 0:b.cols],
                                              PROJ3[:, tt, 3396 + D + b.col:3396 + D + b.col + b.cols], ALU.mult))
                    step(dve.tensor_tensor(MIX[:, tt, c], MIX[:, tt, c], Y[:, tt, c], ALU.add))
            signal("gated3")
            add_half("out3", 1.0)
            normed("ffn2_norm", "h5")
            ffn_act("f4")
            add_half("f4_down")
            signal("result")
            pows["n"] = npow[0]

        @block.scalar
        def _(act):
            group = [0]
            att = [0]
            units = [0]

            def turned_to(dsts):
                for dst, rows, n in dsts:
                    g = group[0]
                    act.wait_ge(turned, g + 1)
                    src = bank[4 + g % 2][0:rows, 0:n]
                    if len(dst.shape) == 3:
                        src = src.rearrange("p (a b) -> p a b", a=dst.shape[1])
                    act.activation(dst, src, ACT.Copy).then_inc(turned_read, 1)
                    group[0] += 1

            def rows_to(dst):
                turned_to([(dst[:, 4 * k:4 * k + 4, tt * P:(tt + 1) * P], P, 512) for tt in range(TT) for k in range(2)])

            def attend(a):
                n = len(a.units)
                for i in range(n + LOOKAHEAD):
                    if i < n:
                        h, tt = a.units[i]
                        nk = a.keys(tt)
                        k = att[0] + i
                        act.wait_ge(att_shifted, k + 1)
                        for hh in range(2):
                            p = PR[:, k % 3, hh * nk:(hh + 1) * nk]
                            ins = act.activation(p, p, ACT.Exp, bias=NM[:, k % 3, hh:hh + 1],
                                                 accum_out=LS[:, k % 3, hh:hh + 1])
                        ins.then_inc(att_exp, 1)
                    if i >= LOOKAHEAD:
                        h, tt = a.units[i - LOOKAHEAD]
                        k = att[0] + i - LOOKAHEAD
                        turned_to([(PT[:, k % 2, 0:2 * a.keys(tt)], P, 2 * a.keys(tt))])
                att[0] += n

            unit_no = [0]

            def ffn_silu(name):
                for b in G[name + "_up"]:
                    for tt in range(TT):
                        u = UNIT_OF[(name, b.col, tt)]
                        act.wait_ge(unit_done, u + 1)
                        act.activation(AF[:, tt, b.col:b.col + GLU], bank[u % GEMM_BANKS][:, 0:GLU],
                                       ACT.Silu).then_inc(E("silu"), 1)

            def ffn(name):
                rows_to(HT)
                ffn_silu(name)
                turned_to([(AFT[:, k:k + 2, :], P, 512) for k in range(0, F_FFN // P, 2)])

            def one(wait, name, *ops):
                act.wait_ge(E(wait), 1)
                for o in ops:
                    ins = act.activation(*o[0:3], **o[3])
                ins.then_inc(E(name), 1)

            act.wait_ge(E("c_in"), 16)
            act.activation(CCOL, CCOL, ACT.Silu).then_inc(E("c_act"), 1)
            act.wait_ge(E("rel_stored"), 16)
            rows_to(HT)
            rows_to(QT)
            attend(A_DIL)
            turned_to([(GLRT, 16, 256)])
            az = H[:, :, 0:256]
            act.wait_ge(E("z_abs"), 1)
            act.activation(az, az, ACT.Exp, scale=-1.0).then_inc(E("z_exp"), 1)
            act.wait_ge(E("z_exp"), 1)
            act.activation(az, az, ACT.Ln, bias=1.0).then_inc(E("z_log"), 1)
            one("gla_b", "gla_exp", (Y[:, :, 0:256], GB[:, :, 0:256], ACT.Exp, {}),
                (Y[:, :, 256:512], GB[:, :, 0:256], ACT.Exp, {"scale": -1.0}),
                (AN.rearrange("p m n -> p (m n)"), MISC[:, 8:16], ACT.Exp, {}),
                (GB[:, :, 256:512], GB[:, :, 256:512], ACT.Exp, {}))
            act.activation(SR, PROJ1[:, :, 2560:3072], ACT.Silu).then_inc(E("silu_r"), 1)
            turned_to([(GT[:, 0:4, tt * P:(tt + 1) * P], P, 512) for tt in range(TT)])
            rows_to(HT)
            rows_to(HT)
            for tt in range(TT):
                act.wait_ge(E(f"top{tt}"), 1)
                act.activation(MISC[:, 58:62], TOPV[:, 0:4], ACT.Exp, bias=MISC[:, 50:51],
                               accum_out=MISC[:, 52:53]).then_inc(E(f"top_exp{tt}"), 1)
            turned_to([(GATET, 32, 256)])
            act.wait_ge(E("n_pass"), 1)
            n_pass = act.value_load(NPASS[0:1, 0:1], min_val=1, max_val=2)
            with act.Fori(0, n_pass) as ps:
                with act.Fori(0, N_EXP) as ex:
                    it = ps * N_EXP + ex
                    for half in range(2):
                        act.wait_ge(m_gather, it * 2 + half + 1)
                        act.activation(XET[:, 4 * half:4 * half + 4, :], bank[6 + half][:, :].rearrange("p (a b) -> p a b", a=4),
                                       ACT.Copy).then_inc(m_x, 1)
                    act.wait_ge(m_gt, it + 1)
                    act.activation(GSELT, bank[6][:, 0:2 * P], ACT.Copy).then_inc(m_gtc, 1)
                    act.wait_ge(m_glu, it + 1)
                    act.activation(SG, GL, ACT.Sigmoid, scale=1.702).then_inc(m_sig, 1)
                    for i, half in enumerate((1, 0)):
                        act.wait_ge(m_tr, it * 2 + i + 1)
                        act.activation(AVT[:, 4 * i:4 * i + 4, :], bank[6 + half][:, :].rearrange("p (a b) -> p a b", a=4),
                                       ACT.Copy).then_inc(m_at, 1)
            ffn("f1")
            rows_to(HT)
            turned_to([(CTILE[:, k:k + 2, :], P, 512) for k in (0, 2)] + [(CTILE[:, 4, :], P, 256)])
            act.wait_ge(E("gate2_in"), 1)
            act.activation(GATE2, GATE2, ACT.Sigmoid).then_inc(E("gate2_sig"), 1)
            act.wait_ge(E("lam_in"), 1)
            act.activation(MISC[:, 18:20], MISC[:, 16:18], ACT.Exp).then_inc(E("lam_exp"), 1)
            for dst in (QT, KT):
                turned_to([(dst[0:MLA_QK, 4 * k:4 * k + 4, tt * P:(tt + 1) * P], MLA_QK, 512)
                           for tt in range(TT) for k in range(2)])
            attend(A_MLA)
            rows_to(QT)
            attend(A_DIFF)
            rows_to(HT)
            rows_to(HT)
            rows_to(HT)
            rows_to(HT)
            rows_to(QT)
            rows_to(KT)
            attend(A_MEM)
            rows_to(HT)
            ffn("f2")
            ffn("f3")
            rows_to(HT)
            act.wait_ge(E("gate3_in"), 1)
            g3 = PROJ3[:, :, 3396:3396 + 2 * D]
            act.activation(g3, g3, ACT.Sigmoid).then_inc(E("gate3_sig"), 1)
            turned_to([(HT[:, 0:2, :], P, 512), (HT[:, 2, :], P, 256)])
            rows_to(QT)
            rows_to(KT)
            attend(A_DSA)
            attend(A_MOBA)
            rows_to(HT)
            rows_to(HT)
            ffn("f4")

        @block.gpsimd
        def _(pool):
            for name, (a, n, src) in small_at.items():
                pool.dma_start(SMALL[:, a:a + n], src[0:1, :].to_broadcast([P, n])).then_inc(E("small"), 16)
            pool.wait_ge(E("setup"), 64)

            def powers(first, last):
                with pool.Fori(first, last) as k:
                    pool.wait_ge(pow_in, k + 1)
                    pool.tensor_tensor(st_out[:, :], st_in[:, :], tab("half"), ALU.pow).then_inc(pow_out, 1)

            powers(0, POWS_FIRST)
            pool.wait_ge(E("n_pass"), 1)
            n_pass = pool.value_load(NPASS[0:1, 0:1], min_val=1, max_val=2)
            with pool.Fori(0, n_pass) as ps:
                with pool.Fori(0, N_EXP) as ex:
                    it = ps * N_EXP + ex
                    pool.wait_ge(m_read, it * 6 + 2)
                    pool.dma_start(BROW, I["b_gate_up"][0][bass.ds(ex, 1), :]).then_inc(m_brow, 16)
                    pool.wait_ge(m_brow, it * 16 + 16)
                    pool.sem_inc(E("moe_bias_row_seen"), 1)
                    pool.partition_broadcast(BB, BROW).then_inc(m_bias, 1)
            powers(POWS_FIRST, pows["n"])

        @block.sync
        def _(sp):
            sp.dma_start(CCOL, I["c"].rearrange("a (k p) -> p (a k)", p=P), allow_slow_non_contiguous=True).then_inc(E("c_in"), 16)
            sp.dma_start(TAB[:, :], I["table"]).then_inc(E("setup"), 16)
            sp.dma_start(BUCK, I["buckets"]).then_inc(E("setup"), 16)
            sp.dma_start(SMALLB[:, 0:8], I["rel_bias_2"]).then_inc(E("setup"), 16)
            sp.dma_start(SMALLB[:, 8:24], I["rel_bias_3"]).then_inc(E("setup"), 16)
            sp.dma_start(X[:, :, :], I["x"][0].rearrange("(t p) n -> p t n", p=P)).then_inc(E("x_in"), 16)
            sp.dma_start(TMASK, I["gla_mask"]).then_inc(E("gla_mask"), 16)
            sp.dma_start(WGLR[:, :], I["w_gate_lr"][0]).then_inc(E("gate_lr"), 16)

            def load_bias(first, name):
                src = bass.AP(tensor=skew_dram, offset=first * P * 384 + 127, ap=[[383, P], [P * 384, 8], [1, S]])
                sp.dma_start(BIAS[:, :, :], src).then_inc(E(name), 16)

            first_products = True
            for kind, c in order:
                if kind == "chunk":
                    if c.after == "moe":
                        sp.wait_ge(E("moe_over"), 1)
                    elif c.after is not None:
                        sp.wait_ge(*c.after.released)
                    for col, n, src in c.parts:
                        sp.dma_start(ring[:, c.slot, 0:c.kts, col:col + n], src).then_inc(landed[c.slot], 16)
                    if first_products and c.number == 5:
                        first_products = False
                        sp.wait_ge(E("rel_rows"), 1)
                        sp.dma_start(arr_dram.ap(), RELS).then_inc(E("rel_stored"), 16)
                        sp.wait_ge(E("rel_stored"), 16)
                        sp.dma_start(skew_dram.ap().rearrange("h (p n) -> h p n", p=P),
                                     arr_dram.ap().unsqueeze(1).to_broadcast([24, P, 384])).then_inc(E("rel_skewed"), 16)
                        sp.wait_ge(E("rel_skewed"), 16)
                        load_bias(0, "bias2")
                elif kind == "vec":
                    src, _ = vecs[c]
                    if c >= 4:
                        sp.wait_ge(vec_used, c - 3)
                    sp.dma_start(VEC[:, c % 4, :], src[0:1, :].to_broadcast([P, D])).then_inc(vec_landed[c % 4], 16)
                elif kind == "bias":
                    sp.wait_ge(E("diff_done" if c == 1 else "dsa_done"), 1)
                    load_bias(8 * c, "bias3a" if c == 1 else "bias3b")
                elif kind == "mem":
                    sp.wait_ge(E("moe_over"), 1)
                    sp.dma_start(H[:, :, :], I["mem_2"][0].rearrange("(t p) n -> p t n", p=P)).then_inc(E("mem_in"), 16)
                elif kind == "moe":
                    for c in before_moe:
                        sp.wait_ge(*c.released)
                    sp.wait_ge(E("mix1"), 1)
                    sp.dma_start(BDOWN, I["b_down"][0]).then_inc(E("b_down"), 16)
                    sp.sem_inc(m_used, SLOTS)
                    sp.wait_ge(E("n_pass"), 1)
                    n_pass = sp.value_load(NPASS[0:1, 0:1], min_val=1, max_val=2)
                    with sp.Fori(0, n_pass) as ps:
                        with sp.Fori(0, N_EXP) as ex:
                            it = ps * N_EXP + ex
                            wu = I["w_gate_up"][0].rearrange("e (k p) n -> e p k n", p=P)
                            wd = I["w_down"][0].rearrange("e (k p) n -> e p k n", p=P)
                            for j in range(12):
                                b, kk = j // 2, SLOT_K * (j % 2)
                                w, b = (wu, b) if b < 4 else (wd, b - 4)
                                sp.wait_ge(m_used, it * 12 + j + 1)
                                sp.dma_start(ring[:, j % SLOTS, :, :],
                                             w[bass.ds(ex, 1), :, kk:kk + SLOT_K, 512 * b:512 * (b + 1)]
                                             .rearrange("e p k n -> p (e k) n")).then_inc(m_landed[j % SLOTS], 16)
            sp.wait_ge(E("result"), 1)
            sp.dma_start(out[0].rearrange("(t p) n -> p t n", p=P), X[:, :, :]).then_inc(E("stored"), 16)
            sp.wait_ge(E("stored"), 16)


NAMES = """x c w_mod b_mod g_pre_mix w_in w_gate_lr b_gate g_gla w_out g_post_mix g_pre_ffn router_w router_b w_gate_up
b_gate_up w_down b_down g_post_ffn mem_2 rel_bias_2 ffn1_w1_2 ffn1_w3_2 ffn1_w2_2 ln1_g_2 ln1_b_2 w_in_2 q_norm_g_2
kv_norm_g_2 w_q_b_2 w_kv_b_2 lam_q1_2 lam_k1_2 lam_q2_2 lam_k2_2 diff_norm_g_2 w_gate_2 b_gate_2 w_up_mla_2
w_up_diff_2 w_o_2 ln2_g_2 ln2_b_2 mem_w_q_2 mem_w_kv_2 mem_w_o_2 ln3_g_2 ln3_b_2 ffn2_w1_2 ffn2_w3_2 ffn2_w2_2 ln4_g_2
ln4_b_2 ffn1_norm_3 ffn1_w_gu_3 ffn1_w_down_3 mix_norm_3 w_in_3 b_gate_3 q_norm_dsa_3 k_norm_dsa_3 q_norm_moba_3
k_norm_moba_3 w_branch_dsa_3 w_branch_moba_3 w_out_3 ffn2_norm_3 ffn2_w_gu_3 ffn2_w_down_3 rel_bias_3""".split()


def kernel(**inputs):
    import concourse.bacc as bacc
    from concourse.bass_utils import run_bass_kernel_spmd

    nc = bacc.Bacc("TRN2", target_bir_lowering=False, num_devices=1)
    arrays = {name: np.ascontiguousarray(inputs[name]) for name in NAMES}
    arrays.update(table=TABLE, buckets=BUCKETS, gla_mask=GLA_MASK)
    I = {name: nc.dram_tensor(f"in_{name}", a.shape, mybir.dt.from_np(a.dtype), kind="ExternalInput").ap()
         for name, a in arrays.items()}
    out = nc.dram_tensor("result", (1, S, D), F32, kind="ExternalOutput").ap()
    build(nc, I, out)
    got = run_bass_kernel_spmd(nc, [{f"in_{k}": a for k, a in arrays.items()}], core_ids=[0])
    return got.results[0]["result"]
```

```python
import math
from contextlib import ExitStack

import numpy as np

import concourse.bass as bass
from concourse import mybir

P = 128
D = 1024
S = 256
TT = S // P
KD = D // P
NEG = -1.0e30
TAKEN = -3.0e38

N_EXP, TOP_K, F_MOE = 32, 4, 1024
CAP = P
F_FFN = 2816
GLU = 256
ATT_W, HD = 512, 64
IN1 = 3088
IN2 = 2208
IN3 = 5444
MLA_H, MLA_NOPE, MLA_ROPE = 8, 64, 32
MLA_QK = MLA_NOPE + MLA_ROPE
DSA_TOPK = 64
ALPHA = 2.0 ** 0.25
LAM_INIT = 0.8 - 0.6 * math.exp(-0.3 * 0)
RAW = 4
MOE_RAW = 6
PARTS = 4
VECS = 3
AHEAD = 2
TILE = 1024
FFN_TILES = 6
FFN_STEPS = F_FFN // GLU
FFN_PAIRS = (FFN_STEPS - 1) // 2
MOE_TILES = 24
POOL_EVERY = 4
GEMM_BANKS = 4
LOOKAHEAD = 2

ALU = mybir.AluOpType
ACT = mybir.ActivationFunctionType
AX = mybir.AxisListType.X
F32 = mybir.dt.float32
F32R = mybir.dt.float32r
I32 = mybir.dt.int32
U32 = mybir.dt.uint32


def shape_constants():
    t = np.arange(P)
    q, k = P + t[:, None], np.arange(S)[None, :]
    dist = q - k
    count = ((dist >= 0) & (dist <= 128)).astype(np.float64)
    count += (dist >= 0) & (dist % 4 == 0)
    count += (dist >= 0) & (dist % 16 == 0)
    lnc = np.where(count > 0, np.log(np.maximum(count, 1)), NEG)
    causal = np.where(dist >= 0, 0.0, NEG)
    same = (t[:, None] // 64) == (t[None, :] // 64)
    upto = same & (t[:, None] <= t[None, :])
    chunk = np.stack([t // 64 == 0, t // 64 == 1], 1)
    before = t[:, None] < t[None, :]

    def angles(inv):
        a = np.arange(S, dtype=np.float32)[:, None] * inv[None, :].astype(np.float32)
        a = a.reshape(TT, P, -1).transpose(1, 0, 2).reshape(P, -1)
        return np.cos(a), np.sin(a)

    half1 = np.float32(10000.0) ** (-np.arange(32, dtype=np.float32) / np.float32(32))
    half2 = np.float32(10000.0) ** (-np.arange(0, 32, 2, dtype=np.float32) / np.float32(32))
    cos1, sin1 = angles(half1)
    cos2, sin2 = angles(half2)
    parts = {
        "ident": np.eye(P), "lnc": lnc, "causal": causal, "upto": upto, "same": same, "chunk": chunk,
        "before": before, "ones": np.ones((P, P)), "ramp": np.tile(np.arange(P), (P, 1)),
        "ramp32": np.tile(np.arange(N_EXP), (P, 1)), "cos1": cos1, "sin1": sin1, "cos2": cos2, "sin2": sin2,
        "half": np.full((P, 16), -0.5),
    }
    at, n = {}, 0
    for name, a in parts.items():
        at[name] = (n, a.shape[1])
        n += a.shape[1]
    table = np.concatenate([np.asarray(a, np.float32) for a in parts.values()], 1)
    d = (S - 1) - np.arange(384)
    n_ = np.maximum(d, 1).astype(np.float32)
    large = 16 + (np.log(n_ / np.float32(16)) / np.float32(math.log(8.0)) * np.float32(16)).astype(np.int32)
    bucket = np.where(np.maximum(d, 0) < 16, np.maximum(d, 0), np.minimum(large, 31))
    onehot = (np.arange(32)[:, None] == bucket[None, :]) & (d >= 0)[None, :]
    ahead = np.tile(np.where(d >= 0, 0.0, NEG)[None, :], (32, 1))
    buckets = np.concatenate([onehot, ahead], 1).astype(np.float32)
    mask = np.tile(upto.astype(np.int32), (1, 4))
    return table, at, buckets, mask


TABLE, TABLE_AT, BUCKETS, GLA_MASK = shape_constants()


class Tile:

    def __init__(self, n, kts, cols, loads, landed):
        self.n, self.kts, self.cols, self.loads, self.landed = n, kts, cols, loads, landed


class Block:

    def __init__(self, col, cols, tiles):
        self.col, self.cols, self.tiles = col, cols, tiles


def build(nc, I, out):
    ctx = ExitStack()
    with ctx:
        sb = lambda name, shape, dt=F32: ctx.enter_context(nc.sbuf_tensor(name, shape, dt))
        sems = {}

        def sem(name):
            if name not in sems:
                sems[name] = ctx.enter_context(nc.semaphore(name))
            return sems[name]

        raw = sb("raw", [P, RAW, TILE])
        w_hi = sb("w_hi", [P, PARTS, TILE], F32R)
        w_lo = sb("w_lo", [P, PARTS, TILE], F32R)
        arena = sb("arena", [P, 10888])
        X = sb("X", [P, TT, D])
        HTh = sb("HTh", [P, KD, S], F32R)
        HTl = sb("HTl", [P, KD, S], F32R)
        AFTh = sb("AFTh", [P, 2, S], F32R)
        AFTl = sb("AFTl", [P, 2, S], F32R)
        Y = sb("Y", [P, TT, D])
        H = sb("H", [P, TT, D])
        QT = sb("QT", [P, KD, S])
        KT = sb("KT", [P, KD, S])
        MIX = sb("MIX", [P, TT, D])
        BIAS = sb("BIAS", [P, 8, S])
        VEC = sb("VEC", [P, VECS, D])
        PR = sb("PR", [P, 3, 512])
        PT = sb("PT", [P, 2, 512])
        SMALL = sb("SMALL", [P, 1696])
        TAB = sb("TAB", [P, TABLE.shape[1]])
        TMASK = KT[:, 0:2, :].rearrange("p a b -> p (a b)").bitcast(I32)
        st_in = sb("st_in", [P, 16])
        st_out = sb("st_out", [P, 16])
        MX = sb("MX", [P, 3, 2])
        NM = sb("NM", [P, 3, 2])
        LS = sb("LS", [P, 3, 2])
        RL = sb("RL", [P, 2])
        MISC = sb("MISC", [P, 64])
        TOPV = sb("TOPV", [P, 8])
        TOPI = sb("TOPI", [P, 8], U32)
        NPASS = sb("NPASS", [P, 1], I32)
        TOPF = sb("TOPF", [P, 8])
        WGLR = sb("WGLR", [16, 256])
        ZERO = sb("ZERO", [P, P], F32R)
        bank = [ctx.enter_context(nc.psum_tensor(f"bank{i}", [P, 512], F32)) for i in range(8)]

        def tab(name):
            a, n = TABLE_AT[name]
            return TAB[:, a:a + n]

        ident = tab("ident")
        arr_dram = nc.dram_tensor("rel_rows", [24, 384], F32)
        skew_dram = nc.dram_tensor("rel_skew", [24, P * 384], F32)

        def bias_rows(first):
            return bass.AP(tensor=skew_dram, offset=first * P * 384 + 127, ap=[[383, P], [P * 384, 8], [1, S]])

        def arena_at(a, *shape):
            n = int(np.prod(shape))
            v = arena[:, a:a + n]
            if len(shape) == 2:
                return v.rearrange("p (a b) -> p a b", a=shape[0])
            if len(shape) == 3:
                return v.rearrange("p (a b c) -> p a b c", a=shape[0], b=shape[1])
            return v

        tiles = []
        landings = [0] * RAW

        def tile(kts, cols, loads):
            n = len(tiles)
            landings[n % RAW] += 16 * len(loads)
            tiles.append(Tile(n, kts, cols, loads, landings[n % RAW]))
            return tiles[-1]

        def product(w, inner, cols, block=512):
            kts = inner // P
            blocks = []
            for c in range(0, cols, block):
                n = min(block, cols - c)
                most = min(kts, TILE // n)
                mine = []
                for k in range(0, kts, most):
                    m = min(most, kts - k)
                    src = w[k * P:(k + m) * P, c:c + n].rearrange("(k p) n -> p k n", p=P)
                    mine.append(tile(m, n, [(0, n, src)]))
                blocks.append(Block(c, n, mine))
            return blocks

        class FeedForward:

            def __init__(self, w1, w3, w2):
                self.up_src = [w.rearrange("(k p) n -> p k n", p=P) for w in (w1, w3)]
                self.down_src = w2.rearrange("(j k p) n -> j k p n", k=2, p=P)
                self.n0 = len(tiles)
                self.tiles = [tile(2, 512, [None, None]) for _ in range(FFN_TILES * FFN_STEPS)]

            def up(self, i, col):
                return [(GLU * h, GLU, w[:, 2 * i:2 * i + 2, col]) for h, w in enumerate(self.up_src)]

        FFN = {}
        G = {}
        vecs = []
        vec_at = {}
        order = []

        def plan_product(name, blocks):
            G[name] = blocks
            for b in blocks:
                order.extend(("tile", t) for t in b.tiles)

        def plan_vec(name, src, users):
            vec_at[name] = len(vecs)
            order.append(("vec", len(vecs)))
            vecs.append((src, users))

        for i in range(6):
            plan_vec(f"b_mod{i}", I["b_mod"][0:1, i * D:(i + 1) * D], 1)
            plan_product(f"mod{i}", product(I["w_mod"][0][:, i * D:(i + 1) * D], D, D))
        plan_vec("g_pre_mix", I["g_pre_mix"], 1)
        plan_product("in1", product(I["w_in"][0], D, IN1))
        plan_vec("g_post_mix", I["g_post_mix"], 1)
        plan_product("out1", product(I["w_out"][0], D, D))
        plan_vec("g_pre_ffn", I["g_pre_ffn"], 1)
        plan_product("router", product(I["router_w"][0], D, N_EXP))
        moe_at = len(tiles)
        order.append(("moe", None))
        plan_vec("g_post_ffn", I["g_post_ffn"], 1)

        def plan_ffn(name, w1, w3, w2):
            FFN[name] = FeedForward(w1, w3, w2)
            order.append(("ffn", FFN[name]))

        def plan_ln(n):
            plan_vec(f"ln{n}_g", I[f"ln{n}_g_2"], 1)
            plan_vec(f"ln{n}_b", I[f"ln{n}_b_2"], 1)

        plan_ffn("f1", I["ffn1_w1_2"][0], I["ffn1_w3_2"][0], I["ffn1_w2_2"][0])
        plan_ln(1)
        plan_product("in2", product(I["w_in_2"][0], D, IN2))
        for i in range(2):
            plan_vec(f"b_gate2_{i}", I["b_gate_2"][0:1, i * D:(i + 1) * D], 1)
        plan_product("gate2", product(I["w_gate_2"][0], D, 2 * D))
        plan_product("q_b", product(I["w_q_b_2"][0], 384, MLA_H * MLA_QK))
        plan_product("kv_b", product(I["w_kv_b_2"][0], 256, D))
        plan_product("up_mla", product(I["w_up_mla_2"][0], 512, D))
        plan_product("up_diff", product(I["w_up_diff_2"][0], 512, D))
        plan_product("o2", product(I["w_o_2"][0], D, D))
        order.append(("mem", None))
        plan_ln(2)
        plan_product("mem_q", product(I["mem_w_q_2"][0], D, D))
        plan_product("mem_kv", product(I["mem_w_kv_2"][0], D, 2 * D))
        plan_product("mem_o", product(I["mem_w_o_2"][0], D, D))
        plan_ln(3)
        plan_ffn("f2", I["ffn2_w1_2"][0], I["ffn2_w3_2"][0], I["ffn2_w2_2"][0])
        plan_ln(4)
        plan_vec("ffn1_norm", I["ffn1_norm_3"], 1)
        plan_ffn("f3", I["ffn1_w_gu_3"][0][:, 0:F_FFN], I["ffn1_w_gu_3"][0][:, F_FFN:2 * F_FFN], I["ffn1_w_down_3"][0])
        plan_vec("mix_norm", I["mix_norm_3"], 1)
        for i in range(2):
            plan_vec(f"b_gate3_{i}", I["b_gate_3"][0:1, i * D:(i + 1) * D], 1)
        plan_product("in3", product(I["w_in_3"][0], D, IN3))
        plan_product("br_dsa", product(I["w_branch_dsa_3"][0], 512, D))
        plan_product("br_moba", product(I["w_branch_moba_3"][0], 512, D))
        plan_product("out3", product(I["w_out_3"][0], D, D))
        plan_vec("ffn2_norm", I["ffn2_norm_3"], 1)
        plan_ffn("f4", I["ffn2_w_gu_3"][0][:, 0:F_FFN], I["ffn2_w_gu_3"][0][:, F_FFN:2 * F_FFN], I["ffn2_w_down_3"][0])

        raw_landed = [sem(f"raw_landed{i}") for i in range(RAW)]
        hi_done = sem("hi_done")
        lo_done = sem("lo_done")
        tile_used = sem("tile_used")
        unit_done = sem("unit_done")
        unit_read = sem("unit_read")
        turned = sem("turned")
        turned_read = sem("turned_read")
        rows_turned = sem("rows_turned")
        rows_hi = sem("rows_hi")
        rows_read = sem("rows_read")
        att_shifted = sem("att_shifted")
        att_exp = sem("att_exp")
        out_done = sem("out_done")
        out_read = sem("out_read")
        pow_in = sem("pow_in")
        pow_out = sem("pow_out")
        vec_landed = [sem(f"vec_landed{i}") for i in range(VECS)]
        vec_used = sem("vec_used")
        E = sem

        MOD = [MIX[:, 0, :], MIX[:, 1, :]] + [arena_at(D * i, D) for i in range(4)]
        PROJ1 = arena_at(4 * D, TT, IN1)
        PROJ2 = arena_at(0, TT, IN2)
        GATE2 = arena_at(4416, TT, 2 * D)
        KV = arena_at(8512, TT, D)
        QM = H[:, :, 0:MLA_H * MLA_QK]
        KVM = arena_at(0, TT, 2 * D)
        QMEM = arena_at(4096, TT, D)
        PROJ3 = arena_at(0, TT, IN3)
        SEL = H[:, :, 0:S]

        small_at = {}

        def small(name, n, src=None):
            if name not in small_at:
                a = sum(m for _, m, _ in small_at.values())
                small_at[name] = (a, n, src)
            a, n, _ = small_at[name]
            return SMALL[:, a:a + n]

        for name, n in (("g_gla", 128), ("b_gate", 256), ("q_norm_g_2", 384), ("kv_norm_g_2", 256), ("lam_q1_2", 64),
                        ("lam_k1_2", 64), ("lam_q2_2", 64), ("lam_k2_2", 64), ("diff_norm_g_2", 128),
                        ("q_norm_dsa_3", 64), ("k_norm_dsa_3", 64), ("q_norm_moba_3", 64), ("k_norm_moba_3", 64),
                        ("router_b", 32)):
            small(name, n, I[name])

        class Attention:

            def __init__(self, heads, scale, q, k, v, dv, bias, put, causal=True, extra=None, step=2):
                self.heads, self.scale, self.q, self.k, self.v, self.dv = heads, scale, q, k, v, dv
                self.bias, self.put, self.causal, self.extra = bias, put, causal, extra
                self.step = step
                self.units = [(h, tt) for h in range(heads) if h % (2 * step) < step for tt in range(TT)]

            def keys(self, tt):
                return P * (tt + 1) if self.causal else S

        def pair_t(t, base, h):
            r = HD * (h % 2)
            return [t[r:r + HD, base + h // 2, :]]

        def row_mask(name):
            def f(h, tt):
                m = tab(name)[:, P:S] if tt == 0 else tab(name)
                n = P * (tt + 1)
                return m.unsqueeze(1).to_broadcast([P, 2, n])
            return f

        def head_bias(h, tt):
            return BIAS[:, h:h + 3:2, P:S] if tt == 0 else BIAS[:, h:h + 3:2, :]

        def into(buf, base, dv, heads, step=2):
            return lambda h, tt: (buf[:, tt, base:base + heads * dv].rearrange("p (h e) -> p h e", h=heads)
                                  [:, h:h + step + 1:step, :])

        A_DIL = Attention(8, HD ** -0.5, lambda h: pair_t(QT, 0, h), lambda h: pair_t(QT, 4, h),
                          lambda h, t: PROJ1[:, t, 1024 + HD * h:1024 + HD * (h + 1)], HD, row_mask("lnc"), into(MIX, 0, HD, 8))
        A_MLA = Attention(8, MLA_QK ** -0.5, lambda h: [QT[0:MLA_QK, h, :]], lambda h: [KT[0:MLA_QK, h, :]],
                          lambda h, t: KV[:, t, P * h + MLA_NOPE:P * (h + 1)], HD, row_mask("causal"), into(MIX, 0, HD, 8, 1),
                          step=1)
        OD8 = Y
        A_DIFF = Attention(8, HD ** -0.5, lambda h: pair_t(QT, 0, h), lambda h: pair_t(QT, 4, h),
                           lambda h, t: PROJ2[:, t, 1696 + P * (h // 2):1696 + P * (h // 2 + 1)], P, head_bias, into(OD8, 0, P, 8))
        A_MEM = Attention(4, 256 ** -0.5, lambda h: [QT[:, 2 * h, :], QT[:, 2 * h + 1, :]],
                          lambda h: [KT[:, 2 * h, :], KT[:, 2 * h + 1, :]],
                          lambda h, t: KVM[:, t, D + 256 * h:D + 256 * (h + 1)], 256, None, into(MIX, 0, 256, 4, 1), causal=False,
                          step=1)
        A_DSA = Attention(8, HD ** -0.5, lambda h: pair_t(QT, 0, h), lambda h: pair_t(QT, 4, h),
                          lambda h, t: PROJ3[:, t, 1024 + HD * h:1024 + HD * (h + 1)], HD, head_bias, into(MIX, 0, HD, 8),
                          extra=lambda tt: SEL[:, tt, 0:P * (tt + 1)].unsqueeze(1).to_broadcast([P, 2, P * (tt + 1)]))
        A_MOBA = Attention(8, HD ** -0.5, lambda h: pair_t(KT, 0, h), lambda h: pair_t(KT, 4, h),
                           lambda h, t: PROJ3[:, t, 2560 + HD * h:2560 + HD * (h + 1)], HD, head_bias, into(MIX, 512, HD, 8))

        LA = QT[:, 0:2, :]
        GB = QT[:, 2:6, :].rearrange("p (t a) b -> p t (a b)", t=2)
        QKD = H[:, :, 0:512]
        KL = H[:, :, 512:768]
        GT = KT[:, 2:6, :]
        ATTM = PR[:, 0:2, :]
        STATE = PT[:, :, :].rearrange("p a b -> p (a b)").rearrange("p (n m e) -> p n m e", n=4, m=2)
        OG = Y[:, :, 0:512]
        SR = Y[:, :, 512:1024]
        GSQ = H[:, :, 0:512]
        AN = MISC[:, 0:8].rearrange("p (m n) -> p m n", m=2)
        GLRT = QT[0:16, 6, :]

        MO = 4 * D
        XETh, XETl = HTh[:, :, 0:CAP], HTl[:, :, 0:CAP]
        AVTh, AVTl = HTh[:, :, CAP:2 * CAP], HTl[:, :, CAP:2 * CAP]
        GU = arena_at(MO, 2 * F_MOE)
        GL = arena_at(MO + 2048, F_MOE)
        SG = arena_at(MO + 3072, F_MOE)
        AV = arena_at(MO + 4096, F_MOE)
        OUTE = Y[:, 1, :]
        PSEL = QT[:, 0, :].rearrange("p (t c) -> p t c", t=2)
        GSEL = QT[:, 1, :].rearrange("p (t c) -> p t c", t=2)
        GSELT = QT[:, 2, :]
        BROW = BIAS[0:1, :, :].rearrange("p a b -> p (a b)")
        BB = MIX[:, :, :].rearrange("p a b -> p (a b)")
        MASKS = QT[:, 3, 0:64].rearrange("p (t e) -> p t e", t=2)
        GATES = QT[:, 3, 64:128].rearrange("p (t e) -> p t e", t=2)
        POS = [QT[:, 3, 128 + 40 * t:128 + 40 * t + N_EXP + 1] for t in range(TT)]
        RT = QT[:, 4, 0:64].rearrange("p (t e) -> p t e", t=2)
        GATET = QT[0:32, 5, :]
        TMP32 = QT[:, 4, 64:96]
        BDOWN = KT[0:32, 0:4, :].rearrange("p a b -> p (a b)")
        glu_in = GU.rearrange("p (f two) -> p f two", two=2)

        BUCK = KT[0:32, 2:5, :].rearrange("p a b -> p (a b)")
        SMALLB = KT[0:32, 5, 0:24]
        RELS = KT[0:24, 6:8, :].rearrange("p a b -> p (a b)")[:, 0:384]
        CCOL = MISC[:, 0:8]
        FA = arena_at(0, TT, GLU)
        KM = Y
        KI2 = PT[:, :, 0:P]
        SQ = PR[:, :, :].rearrange("p a b -> p (a b)")[:, 0:D]

        m_landed = [sem(f"moe_landed{i}") for i in range(MOE_RAW)]
        m_hi = sem("moe_hi")
        m_lo = [sem("moe_lo_vector"), sem("moe_lo_pool")]
        m_used = sem("moe_tile_used")
        m_up_read = sem("moe_up_read")
        m_down_read = sem("moe_down_read")
        m_sel = sem("moe_sel")
        m_gather = sem("moe_gather")
        m_xhi = sem("moe_x_hi")
        m_xlo = sem("moe_x_lo")
        m_gt = sem("moe_gate_turned")
        m_gtc = sem("moe_gate_copied")
        m_glu = sem("moe_glu")
        m_sig = sem("moe_sigmoid")
        m_act = sem("moe_act")
        m_tr = sem("moe_act_turned")
        m_ahi = sem("moe_act_hi")
        m_alo = sem("moe_act_lo")
        m_brow = sem("moe_bias_row")
        m_bias = sem("moe_bias")
        m_pass = sem("moe_pass")
        m_chain = sem("moe_dve_step")
        M_STEPS = 3
        pool_tile = lambda t: t % POOL_EVERY == POOL_EVERY - 1
        lo_per = [sum(not pool_tile(t) for t in range(MOE_TILES)), sum(pool_tile(t) for t in range(MOE_TILES))]

        def moe_raw(t):
            i = t % MOE_RAW
            return raw[:, i, :] if i < RAW else arena_at((i - RAW) * TILE, TILE)

        def moe_lo(it, t):
            back, t = (1, t + MOE_TILES) if t < 0 else (0, t)
            e = int(pool_tile(t))
            nth = sum(pool_tile(i) == pool_tile(t) for i in range(t + 1))
            return m_lo[e], it * lo_per[e] + (1 - back) * lo_per[e] + nth

        def moe_used(it, t):
            return it * MOE_TILES + MOE_TILES + t + 1

        block = ctx.enter_context(nc.Block())
        pows = {"n": 0}
        POWS_FIRST = 8
        UNIT_OF = {}

        @block.tensor
        def _(pe):
            unit = [0]
            group = [0]
            outs = [0]
            rows = [0]
            att = [0]

            def three(acc, xh, xl, wh, wl, start, stop):
                pe.matmul(acc, xh, wh, start=start, stop=False)
                pe.matmul(acc, xh, wl, start=False, stop=False)
                return pe.matmul(acc, xl, wh, start=False, stop=stop)

            def parts(n, j, cols):
                c = slice(j * cols, (j + 1) * cols)
                return w_hi[:, n % PARTS, c], w_lo[:, n % PARTS, c]

            def gemm(name, tts=TT, kt0=0):
                for b in G[name]:
                    kt_all = sum(t.kts for t in b.tiles)
                    kt = 0
                    for t in b.tiles:
                        pe.wait_ge(lo_done, t.n + 1)
                        for tt in range(tts):
                            u = unit[0] + tt
                            if kt == 0 and u >= GEMM_BANKS:
                                pe.wait_ge(unit_read, u - GEMM_BANKS + 1)
                            c = slice(tt * P, (tt + 1) * P)
                            for j in range(t.kts):
                                k = kt + j + kt0
                                mm = three(bank[u % GEMM_BANKS][:, 0:t.cols], HTh[:, k, c], HTl[:, k, c],
                                           *parts(t.n, j, t.cols), kt + j == 0, kt + j == kt_all - 1)
                        mm.then_inc(tile_used, 1)
                        kt += t.kts
                    unit[0] += tts

            def turn(tiles):
                for i in range(0, len(tiles), 4):
                    g = group[0]
                    if g >= 2:
                        pe.wait_ge(turned_read, g - 1)
                    for j, src in enumerate(tiles[i:i + 4]):
                        w = src.shape[1]
                        mm = pe.transpose(bank[4 + g % 2][0:w, P * j:P * (j + 1)], src, ident)
                    mm.then_inc(turned, 1)
                    group[0] += 1

            def turned_all():
                pe.wait_ge(turned_read, group[0])

            def turn_rows(buf, base=0, n=KD):
                turn([buf[:, tt, base + P * k:base + P * (k + 1)] for tt in range(TT) for k in range(n)])
                turned_all()

            def turn_split(srcs):
                for i in range(0, len(srcs), 4):
                    g = rows[0]
                    if g >= 2:
                        pe.wait_ge(rows_read, g - 1)
                    for j, src in enumerate(srcs[i:i + 4]):
                        mm = pe.transpose(bank[4 + g % 2][:, P * j:P * (j + 1)], src, ident)
                    mm.then_inc(rows_turned, 1)
                    rows[0] += 1
                pe.wait_ge(rows_read, rows[0])

            def split_rows(buf):
                turn_split([buf[:, tt, P * k:P * (k + 1)] for tt in range(TT) for k in range(KD)])

            def next_unit():
                u = unit[0]
                if u >= GEMM_BANKS:
                    pe.wait_ge(unit_read, u - GEMM_BANKS + 1)
                unit[0] += 1
                return bank[u % GEMM_BANKS]

            def attend(a):
                n = len(a.units)

                def scores(i):
                    h, tt = a.units[i]
                    nk = a.keys(tt)
                    b = next_unit()
                    for hh in range(2):
                        qs, ks = a.q(h + a.step * hh), a.k(h + a.step * hh)
                        for j in range(len(qs)):
                            mm = pe.matmul(b[:, hh * nk:(hh + 1) * nk], qs[j][:, tt * P:(tt + 1) * P], ks[j][:, 0:nk],
                                           start=(j == 0), stop=(j == len(qs) - 1))
                    mm.then_inc(unit_done, 1)

                def values(i):
                    h, tt = a.units[i]
                    nk = a.keys(tt)
                    k = att[0] + i
                    pe.wait_ge(att_exp, k + 1)
                    p = PR[:, k % 3, 0:2 * nk]
                    turn([p[:, P * j:P * (j + 1)] for j in range(2 * nk // P)])
                    turned_all()
                    o = outs[0]
                    if o >= 2:
                        pe.wait_ge(out_read, o - 1)
                    for hh in range(2):
                        for t in range(nk // P):
                            j = hh * (nk // P) + t
                            mm = pe.matmul(bank[6 + o % 2][:, hh * a.dv:(hh + 1) * a.dv], PT[:, k % 2, P * j:P * (j + 1)],
                                           a.v(h + a.step * hh, t), start=(t == 0), stop=(t == nk // P - 1))
                    mm.then_inc(out_done, 1)
                    outs[0] += 1

                for i in range(n + LOOKAHEAD):
                    if i < n:
                        scores(i)
                    if i >= LOOKAHEAD:
                        values(i - LOOKAHEAD)
                att[0] += n

            pe.wait_ge(E("setup"), 16 * 4)
            b = next_unit()
            pe.matmul(b[0:24, 0:384], SMALLB[:, 0:24], BUCK[:, 0:384], start=True, stop=True).then_inc(unit_done, 1)
            pe.wait_ge(E("c_spread"), 1)
            for i in range(6):
                gemm(f"mod{i}", tts=1)
            pe.wait_ge(E("h1"), 1)
            split_rows(H)
            gemm("in1")
            pe.wait_ge(E("rope1"), 1)
            turn_rows(Y)
            attend(A_DIL)
            pe.wait_ge(E("dil_out"), 1)
            turn([PROJ1[:, tt, 3072:3088] for tt in range(TT)])
            turned_all()
            pe.wait_ge(E("gate_lr"), 16)
            b = next_unit()
            for tt in range(TT):
                mm = pe.matmul(b[:, 256 * tt:256 * (tt + 1)], GLRT[:, tt * P:(tt + 1) * P], WGLR[:, :], start=True, stop=True)
            mm.then_inc(unit_done, 1)
            pe.wait_ge(E("log_a"), 1)
            for tt in range(TT):
                b = next_unit()
                pe.matmul(b[:, 0:256], tab("upto"), LA[:, tt, :], start=True, stop=True)
                pe.matmul(b[:, 256:512], tab("same"), LA[:, tt, :], start=True, stop=True).then_inc(unit_done, 1)
            b = next_unit()
            for m in range(2):
                for tt in range(TT):
                    mm = pe.matmul(b[:, 4 * m + 2 * tt:4 * m + 2 * tt + 2], LA[:, tt, m * P:(m + 1) * P], tab("chunk"),
                                   start=True, stop=True)
            mm.then_inc(unit_done, 1)
            pe.wait_ge(E("gla_qk"), 1)
            turn([QKD[:, tt, P * k:P * (k + 1)] for tt in range(TT) for k in range(4)])
            turned_all()
            for tt in range(TT):
                for par in range(2):
                    b = next_unit()
                    r = HD * par
                    for m in range(2):
                        mm = pe.matmul(b[:, P * m:P * (m + 1)], GT[r:r + HD, 2 + m, tt * P:(tt + 1) * P],
                                       GT[r:r + HD, m, tt * P:(tt + 1) * P], start=True, stop=True)
                    mm.then_inc(unit_done, 1)
            for some in ((0, 2), (1,)):
                b = next_unit()
                for c in some:
                    tt, r = c // 2, HD * (c % 2)
                    for h in range(4):
                        o = HD * (h % 2)
                        mm = pe.matmul(b[o:o + HD, 256 * tt + P * (h // 2):256 * tt + P * (h // 2 + 1)],
                                       KL[r:r + HD, tt, HD * h:HD * (h + 1)],
                                       PROJ1[r:r + HD, tt, 2048 + P * h:2048 + P * (h + 1)], start=True, stop=True)
                mm.then_inc(unit_done, 1)
            pe.wait_ge(E("gla_state"), 1)
            for tt in range(TT):
                b = next_unit()
                for h in range(4):
                    mm = pe.matmul(b[:, P * h:P * (h + 1)], ATTM[:, tt, P * h:P * (h + 1)],
                                   PROJ1[:, tt, 2048 + P * h:2048 + P * (h + 1)], start=True, stop=True)
                mm.then_inc(unit_done, 1)
                for par in range(2):
                    b = next_unit()
                    r = HD * par
                    for c in range(2):
                        n = 2 * tt + c
                        for m in range(2):
                            mm = pe.matmul(b[HD * c:HD * (c + 1), P * m:P * (m + 1)], GT[r:r + HD, m, n * HD:(n + 1) * HD],
                                           STATE[r:r + HD, n, m, :], start=True, stop=True)
                    mm.then_inc(unit_done, 1)
            pe.wait_ge(E("mix1"), 1)
            split_rows(MIX)
            gemm("out1")
            pe.wait_ge(E("h2"), 1)
            split_rows(H)
            gemm("router")
            pe.wait_ge(E("routed"), 1)
            b = next_unit()
            pe.matmul(b[:, 0:32], tab("before"), MASKS[:, 0, :], start=True, stop=True)
            pe.matmul(b[:, 32:64], tab("ones"), MASKS[:, 0, :], start=True, stop=False)
            pe.matmul(b[:, 32:64], tab("before"), MASKS[:, 1, :], start=False, stop=True)
            pe.matmul(b[:, 64:96], tab("ones"), MASKS[:, 0, :], start=True, stop=False)
            pe.matmul(b[:, 64:96], tab("ones"), MASKS[:, 1, :], start=False, stop=True).then_inc(unit_done, 1)
            turn([GATES[:, tt, :] for tt in range(TT)])
            turned_all()
            pe.wait_ge(unit_read, unit[0])
            pe.wait_ge(E("b_down"), 16)
            for tt in range(TT):
                for n in range(2):
                    pe.matmul(bank[2 * tt + n][:, :], GATET[:, tt * P:(tt + 1) * P], BDOWN[:, 512 * n:512 * (n + 1)],
                              start=True, stop=False, skip_group_check=True)

            def zero_bank(b, start, stop):
                for i in range(4):
                    mm = pe.matmul(b[:, P * i:P * (i + 1)], ZERO[:, :], ZERO[:, :], start=start, stop=stop, skip_group_check=True)
                return mm

            def gather(done):
                pe.wait_ge(m_sel, done)
                for half in range(2):
                    for k in range(4):
                        for tt in range(TT):
                            kk = 4 * half + k
                            mm = pe.matmul(bank[6 + half][:, P * k:P * (k + 1)], H[:, tt, P * kk:P * (kk + 1)],
                                           PSEL[:, tt, :], start=(tt == 0), stop=(tt == TT - 1))
                    mm.then_inc(m_gather, 1)

            def scatter():
                for tt in range(TT):
                    for n in range(2):
                        mm = pe.matmul(bank[2 * tt + n][:, :], GSELT[:, tt * P:(tt + 1) * P],
                                       OUTE[:, 512 * n:512 * (n + 1)], start=False, stop=False, skip_group_check=True)
                return mm

            pe.wait_ge(E("zeroed"), 1)
            zero_bank(bank[5], True, True).then_inc(E("moe_begun"), 1)
            gather(1)
            pe.sem_inc(m_used, MOE_TILES)
            pe.wait_ge(E("moe_zero"), 1)
            pe.wait_ge(E("n_pass"), 1)
            n_pass = pe.value_load(NPASS[0:1, 0:1], min_val=1, max_val=2)
            with pe.Fori(0, n_pass) as ps:
                with pe.Fori(0, N_EXP) as ex:
                    it = ps * N_EXP + ex

                    def moe_block(b, xh, xl, free):
                        for w in free:
                            pe.wait_ge(*w)
                        for i in range(4):
                            t = 4 * b + i
                            if b >= 4 and i in (0, 2):
                                pe.wait_ge(m_alo, it * 2 + 1 + i // 2)
                            pe.wait_ge(*moe_lo(it, t))
                            for j in range(2):
                                k = 2 * i + j
                                mm = three(bank[4 + b % 2][:, :], xh[:, k, :], xl[:, k, :], *parts(t, j, 512), k == 0, k == KD - 1)
                            mm.then_inc(m_used, 1)

                    pe.wait_ge(m_xlo, it * 2 + 2)
                    moe_block(0, XETh, XETl, [(m_down_read, it * 2 + 2)])
                    moe_block(1, XETh, XETl, [(m_down_read, it * 2 + 3)])
                    moe_block(2, XETh, XETl, [(m_up_read, it * 4 + 5)])
                    moe_block(3, XETh, XETl, [(m_up_read, it * 4 + 6)])
                    gather(it + 2)
                    pe.wait_ge(m_down_read, it * 2 + 3)
                    pe.wait_ge(m_gtc, it + 1)
                    scatter()
                    pe.wait_ge(m_act, it + 1)
                    pe.wait_ge(m_up_read, it * 4 + 8)
                    for half in range(2):
                        pe.wait_ge(m_xlo, it * 2 + 3 + half)
                        for k in range(4):
                            kk = 4 * half + k
                            mm = pe.transpose(bank[6 + half][:, P * k:P * (k + 1)], AV[:, P * kk:P * (kk + 1)], ident)
                        mm.then_inc(m_tr, 1)
                    for tt in range(TT):
                        mm = pe.transpose(bank[5][:, P * tt:P * (tt + 1)], GSEL[:, tt, :], ident)
                    mm.then_inc(m_gt, 1)
                    moe_block(4, AVTh, AVTl, [(m_up_read, it * 4 + 7)])
                    moe_block(5, AVTh, AVTl, [(m_gtc, it + 2)])
            pe.wait_ge(m_down_read, n_pass * (2 * N_EXP) + 3)
            pe.wait_ge(m_gtc, n_pass * N_EXP + 1)
            scatter()
            for i in range(4):
                mm = zero_bank(bank[i], False, True)
            mm.then_inc(E("moe_over"), 1)
            pe.wait_ge(E("moe_sum"), 1)

            def ffn(name, src, ready):
                f = FFN[name]
                pe.wait_ge(E(ready), 1)
                split_rows(src)
                u = unit[0]
                pe.wait_ge(unit_read, u)
                for i in range(4):
                    zero_bank(bank[(u + i) % GEMM_BANKS], True, False)
                acted, turned_f, read_f = E(name + "_acted"), E(name + "_turned"), E(name + "_turned_lo")

                def up(n, pair):
                    for i in range(4):
                        pe.wait_ge(lo_done, pair * (2 * FFN_TILES) + n + i + 1)
                        for tt in range(TT):
                            c = slice(tt * P, (tt + 1) * P)
                            for j in range(2):
                                k = 2 * i + j
                                mm = three(bank[6 + tt][:, :], HTh[:, k, c], HTl[:, k, c], *parts(n + i, j, 512),
                                           k == 0, k == KD - 1)
                        mm.then_inc(tile_used, 1)

                def turn_act(jj):
                    pe.wait_ge(acted, jj * TT + TT)
                    for k in range(2):
                        for tt in range(TT):
                            mm = pe.transpose(bank[5][:, S * k + P * tt:S * k + P * (tt + 1)], FA[:, tt, P * k:P * (k + 1)], ident)
                    mm.then_inc(turned_f, 1)

                def down(n, pair, two):
                    last = pair is None
                    pe.wait_ge(read_f, FFN_STEPS if last else pair * 2 + two + 1)
                    for i in range(2):
                        pe.wait_ge(lo_done, n + i + 1 if last else pair * (2 * FFN_TILES) + n + i + 1)
                        for tt in range(TT):
                            c = slice(tt * P, (tt + 1) * P)
                            for k in range(2):
                                wh, wl = parts(n + i, k, 512)
                                acc = bank[(u + 2 * tt + i) % GEMM_BANKS][:, :]
                                pe.matmul(acc, AFTh[:, k, c], wh, start=False, stop=False, skip_group_check=True)
                                pe.matmul(acc, AFTh[:, k, c], wl, start=False, stop=False, skip_group_check=True)
                                mm = pe.matmul(acc, AFTl[:, k, c], wh, start=False, stop=last and k == 1, skip_group_check=True)
                        mm.then_inc(tile_used, 1)

                up(f.n0, 0)
                with pe.Fori(0, FFN_PAIRS) as pair:
                    for two in range(2):
                        turn_act(pair * 2 + two)
                        up(f.n0 + 4 + FFN_TILES * two, pair)
                        down(f.n0 + 8 + FFN_TILES * two, pair, two)
                turn_act(FFN_STEPS - 1)
                down(f.n0 + 4 + FFN_TILES * (FFN_STEPS - 1), None, None)
                unit[0] += 4

            ffn("f1", X, "x1")
            pe.wait_ge(E("ln1"), 1)
            split_rows(X)
            gemm("in2")
            gemm("gate2")
            pe.wait_ge(E("c_norm"), 1)
            turn_split([PROJ2[:, tt, P * k:P * (k + 1)] for k in range(5) for tt in range(TT)])
            gemm("q_b")
            gemm("kv_b", kt0=3)
            pe.wait_ge(E("mla_qk"), 1)
            turn([QM[:, tt, MLA_QK * h:MLA_QK * (h + 1)] for tt in range(TT) for h in range(MLA_H)])
            turn([KM[:, tt, MLA_QK * h:MLA_QK * (h + 1)] for tt in range(TT) for h in range(MLA_H)])
            turned_all()
            attend(A_MLA)
            turn_rows(PROJ2, base=672)
            pe.wait_ge(E("bias2"), 16)
            attend(A_DIFF)
            pe.wait_ge(E("mix2"), 1)
            split_rows(MIX)
            gemm("up_mla")
            gemm("up_diff", kt0=4)
            pe.wait_ge(E("gated2"), 1)
            split_rows(MIX)
            gemm("o2")
            pe.wait_ge(E("ln2"), 1)
            split_rows(X)
            gemm("mem_q")
            pe.wait_ge(E("mem_in"), 16)
            split_rows(H)
            gemm("mem_kv")
            pe.wait_ge(E("mem_qkv"), 1)
            turn_rows(QMEM)
            turn_rows(KVM)
            attend(A_MEM)
            pe.wait_ge(E("mem_out"), 1)
            split_rows(MIX)
            gemm("mem_o")
            ffn("f2", X, "ln3")
            ffn("f3", H, "h3")
            pe.wait_ge(E("h4"), 1)
            split_rows(H)
            gemm("in3")
            pe.wait_ge(E("qk3"), 1)
            turn([PROJ3[:, tt, 3072 + P * k:3072 + P * (k + 1)] for k in range(2) for tt in range(TT)])
            turn([KI2[:, tt, :] for tt in range(TT)])
            turned_all()
            for tt in range(TT):
                nk = P * (tt + 1)
                for par in range(2):
                    b = next_unit()
                    r = HD * par
                    for hh in range(2):
                        mm = pe.matmul(b[:, hh * nk:(hh + 1) * nk], QT[r:r + HD, hh, tt * P:(tt + 1) * P],
                                       QT[r:r + HD, 2, 0:nk], start=True, stop=True)
                    mm.then_inc(unit_done, 1)
            turn_rows(PROJ3)
            turn_rows(PROJ3, base=1536)
            attend(A_DSA)
            attend(A_MOBA)
            pe.wait_ge(E("mix3"), 1)
            split_rows(MIX)
            gemm("br_dsa")
            gemm("br_moba", kt0=4)
            pe.wait_ge(E("gated3"), 1)
            split_rows(MIX)
            gemm("out3")
            ffn("f4", H, "h5")


        @block.vector
        def _(dve):
            steps = [0]
            units = [0]
            alone = [0]
            split = [0]
            rows = [0]
            outs = [0]
            npow = [0]
            vec_done = [0]
            att = [0]
            chain = sem("dve_step")

            def step(ins):
                steps[0] += 1
                ins.then_inc(chain, 1)
                dve.wait_ge(chain, steps[0])

            def mark(ins, name):
                ins.then_inc(E(name), 1)
                dve.wait_ge(E(name), 1)

            def signal(name):
                dve.sem_inc(E(name), 1)

            def unit():
                alone[0] += 1
                dve.wait_ge(unit_done, alone[0])
                units[0] += 1
                return bank[(units[0] - 1) % GEMM_BANKS]

            def low(n, hi_count):
                m = tiles[n].kts * tiles[n].cols
                dve.wait_ge(hi_done, hi_count)
                dve.tensor_tensor(w_lo[:, n % PARTS, 0:m], raw[:, n % RAW, 0:m], w_hi[:, n % PARTS, 0:m].bitcast(F32),
                                  ALU.subtract).then_inc(lo_done, 1)

            def split_to(n):
                for i in range(split[0], n):
                    low(i, i + 1)
                split[0] = max(split[0], n)

            def ahead(n):
                split_to(min(n + AHEAD, moe_at if n <= moe_at else len(tiles)))

            def gemm(name, put, tts=TT):
                def read(b):
                    dve.wait_ge(tile_used, b.tiles[-1].n + 1)
                    for tt in range(tts):
                        units[0] += 1
                        put(bank[(units[0] - 1) % GEMM_BANKS][:, 0:b.cols], tt, b)
                last = None
                for b in G[name]:
                    split_to(b.tiles[-1].n + 1)
                    if last is not None:
                        read(last)
                    last = b
                read(last)
                ahead(last.tiles[-1].n + 1)

            def rows_lo(dsts):
                for lo, hi in dsts:
                    g = rows[0]
                    dve.wait_ge(rows_hi, g + 1)
                    n = hi.shape[1] * hi.shape[2]
                    src = bank[4 + g % 2][:, 0:n].rearrange("p (a b) -> p a b", a=hi.shape[1])
                    dve.tensor_tensor(lo, src, hi.bitcast(F32), ALU.subtract).then_inc(rows_read, 1)
                    rows[0] += 1

            def split_rows():
                rows_lo([(HTl[:, 4 * k:4 * k + 4, tt * P:(tt + 1) * P], HTh[:, 4 * k:4 * k + 4, tt * P:(tt + 1) * P])
                         for tt in range(TT) for k in range(2)])

            def release(ins):
                ins.then_inc(unit_read, 1)
                dve.wait_ge(unit_read, units[0])

            def vec(name):
                i = vec_at[name]
                dve.wait_ge(vec_landed[i % VECS], 16 * (i // VECS + 1))
                return VEC[:, i % VECS, :]

            def vec_over(name):
                assert vec_at[name] == vec_done[0], name
                vec_done[0] += 1
                dve.sem_inc(vec_used, 1)

            def rsqrt(src, scale, eps, n=1):
                npow[0] += 1
                dve.tensor_scalar(st_in[:, 0:n], src, scale, eps, ALU.mult, ALU.add).then_inc(pow_in, 1)
                dve.wait_ge(pow_out, npow[0])
                return st_out

            def square_sum(x, col):
                w = x.shape[1]
                step(dve.tensor_tensor_reduce(SQ[:, 0:w], x, x, 1.0, 0.0, ALU.mult, ALU.add, col))

            ss = MISC[:, 32:33]

            def rms_rows(out, x, g):
                square_sum(x, ss)
                r = rsqrt(ss, 1.0 / x.shape[1], 1e-6)
                step(dve.scalar_tensor_tensor(out, x, r[:, 0:1], g, ALU.mult, ALU.mult))

            def rms_heads(x, heads, w, g, scale=1.0):
                sq = SQ[:, 0:heads * w].rearrange("p (h e) -> p h e", h=heads)
                step(dve.tensor_tensor(sq, x, x, ALU.mult))
                step(dve.tensor_reduce(MISC[:, 40:40 + heads], sq, AX, ALU.add))
                r = rsqrt(MISC[:, 40:40 + heads], 1.0 / w, 1e-6, heads)
                rb = r[:, 0:heads].unsqueeze(2).to_broadcast([P, heads, w])
                step(dve.tensor_tensor(x, x, rb, ALU.mult))
                gb = g.unsqueeze(1).to_broadcast([P, heads, w])
                if scale != 1.0:
                    step(dve.scalar_tensor_tensor(x, x, scale, gb, ALU.mult, ALU.mult))
                else:
                    step(dve.tensor_tensor(x, x, gb, ALU.mult))

            def copy_out(name, dst, tts=TT):
                gemm(name, lambda s, tt, b: release(dve.tensor_copy(dst(tt, b.col, b.cols), s)), tts)

            def layer_norm(n):
                g, b = vec(f"ln{n}_g"), vec(f"ln{n}_b")
                for tt in range(TT):
                    x = X[:, tt, :]
                    step(dve.tensor_reduce(MISC[:, 33:34], x, AX, ALU.add))
                    step(dve.tensor_scalar(MISC[:, 34:35], MISC[:, 33:34], -1.0 / D, None, ALU.mult))
                    step(dve.tensor_scalar(x, x, MISC[:, 34:35], None, ALU.add))
                    square_sum(x, ss)
                    r = rsqrt(ss, 1.0 / D, 1e-5)
                    step(dve.scalar_tensor_tensor(x, x, r[:, 0:1], g, ALU.mult, ALU.mult))
                    step(dve.tensor_tensor(x, x, b, ALU.add))
                vec_over(f"ln{n}_g")
                vec_over(f"ln{n}_b")
                signal(f"ln{n}")

            def scaled(scale):
                def put(s, tt, b):
                    c = slice(b.col, b.col + b.cols)
                    release(dve.tensor_scalar(Y[:, tt, c], s, scale, None, ALU.mult))
                    step(dve.scalar_tensor_tensor(X[:, tt, c], X[:, tt, c], ALPHA, Y[:, tt, c], ALU.mult, ALU.add))
                return put

            def halved(scale):
                def put(s, tt, b):
                    x = X[:, tt, b.col:b.col + b.cols]
                    release(dve.scalar_tensor_tensor(x, s, scale, x, ALU.mult, ALU.add))
                return put

            def ffn(name, put):
                f = FFN[name]
                n0, last = f.n0, FFN_STEPS - 1
                acted, silued = E(name + "_acted"), E(name + "_silu")
                turned_hi, turned_lo = E(name + "_turned_hi"), E(name + "_turned_lo")

                def product_of_halves(first):
                    for tt in range(TT):
                        dve.wait_ge(silued, first + tt + 1)
                        dve.tensor_tensor(FA[:, tt, :], FA[:, tt, :], bank[6 + tt][:, GLU:2 * GLU], ALU.mult).then_inc(acted, 1)

                def turned_low(turn):
                    dve.wait_ge(turned_hi, turn)
                    dve.tensor_tensor(AFTl[:, :, :], bank[5][:, :].rearrange("p (a b) -> p a b", a=2),
                                      AFTh[:, :, :].bitcast(F32), ALU.subtract).then_inc(turned_lo, 1)

                split_rows()
                split_to(n0 + 4)
                product_of_halves(0)
                with dve.Fori(0, FFN_PAIRS) as pair:
                    for two in range(2):
                        for i in range(FFN_TILES):
                            n = n0 + 4 + FFN_TILES * two + i
                            if i == 4:
                                turned_low(pair * 2 + two + 1)
                            low(n, pair * (2 * FFN_TILES) + n + 1)
                        product_of_halves(pair * (2 * TT) + TT * two + TT)
                turned_low(FFN_STEPS)
                n = n0 + 4 + FFN_TILES * last
                split[0] = n
                split_to(n + 2)
                dve.wait_ge(tile_used, n + 2)
                u = units[0]
                units[0] += 4
                done = [0]
                for tt in range(TT):
                    for i in range(2):
                        done[0] += 1
                        units[0] = u + done[0]
                        put(bank[(u + 2 * tt + i) % GEMM_BANKS][:, :], tt, Block(512 * i, 512, None))
                ahead(n + 2)

            def attend(a):
                n = len(a.units)

                def soften(i):
                    h, tt = a.units[i]
                    nk = a.keys(tt)
                    k = att[0] + i
                    p = PR[:, k % 3, 0:2 * nk].rearrange("p (h n) -> p h n", h=2)
                    s = unit()[:, 0:2 * nk].rearrange("p (h n) -> p h n", h=2)
                    if a.bias is None:
                        release(dve.tensor_scalar(p, s, a.scale, None, ALU.mult))
                    else:
                        release(dve.scalar_tensor_tensor(p, s, a.scale, a.bias(h, tt), ALU.mult, ALU.add))
                    if a.extra is not None:
                        step(dve.tensor_tensor(p, p, a.extra(tt), ALU.add))
                    step(dve.tensor_reduce(MX[:, k % 3, :], p, AX, ALU.max))
                    dve.tensor_scalar(NM[:, k % 3, :], MX[:, k % 3, :], -1.0, None, ALU.mult).then_inc(att_shifted, 1)

                def put(i):
                    h, tt = a.units[i]
                    k = att[0] + i
                    dve.wait_ge(att_exp, k + 1)
                    step(dve.reciprocal(RL[:, :], LS[:, k % 3, :]))
                    dve.wait_ge(out_done, outs[0] + 1)
                    o = bank[6 + outs[0] % 2][:, 0:2 * a.dv].rearrange("p (h e) -> p h e", h=2)
                    outs[0] += 1
                    dve.tensor_tensor(a.put(h, tt), o, RL[:, :].unsqueeze(2).to_broadcast([P, 2, a.dv]),
                                      ALU.mult).then_inc(out_read, 1)
                    dve.wait_ge(out_read, outs[0])

                for i in range(n + LOOKAHEAD):
                    if i < n:
                        soften(i)
                    if i >= LOOKAHEAD:
                        put(i - LOOKAHEAD)
                att[0] += n

            def rotate(x1, x2, o1, o2, cos, sin, t):
                step(dve.tensor_tensor(t[0], x1, cos, ALU.mult))
                step(dve.tensor_tensor(t[1], x2, sin, ALU.mult))
                step(dve.tensor_tensor(t[2], x2, cos, ALU.mult))
                step(dve.tensor_tensor(t[3], x1, sin, ALU.mult))
                step(dve.tensor_tensor(o1, t[0], t[1], ALU.subtract))
                step(dve.tensor_tensor(o2, t[2], t[3], ALU.add))

            mark(dve.memset(ZERO[:, :].bitcast(F32), 0.0), "zeroed")
            step(dve.memset(st_in[:, :], 1.0))
            dve.wait_ge(E("setup"), 64)
            mark(dve.tensor_tensor(RELS, unit()[0:24, 0:384], BUCK[0:24, 384:768], ALU.add), "rel_rows")
            dve.sem_inc(unit_read, 1)
            dve.wait_ge(E("c_hi"), 1)
            dve.tensor_tensor(HTl[:, :, 0:P], CCOL.unsqueeze(2).to_broadcast([P, KD, P]), HTh[:, :, 0:P].bitcast(F32),
                              ALU.subtract).then_inc(E("c_spread"), 1)
            for i in range(6):
                v = vec(f"b_mod{i}")

                def modulation(s, tt, b, i=i, v=v):
                    c = slice(b.col, b.col + b.cols)
                    release(dve.tensor_tensor(MOD[i][:, c], s, v[:, c], ALU.add))

                gemm(f"mod{i}", modulation, 1)
                vec_over(f"b_mod{i}")
            shift1, scale1, gate1, shift2, scale2, gate2 = MOD

            def gain(scale, name):
                v = vec(name)
                step(dve.scalar_tensor_tensor(scale, scale, 1.0, v, ALU.add, ALU.mult))
                vec_over(name)

            gain(scale1, "g_pre_mix")
            dve.wait_ge(E("x_in"), 16)
            for tt in range(TT):
                rms_rows(H[:, tt, :], X[:, tt, :], scale1)
                step(dve.tensor_tensor(H[:, tt, :], H[:, tt, :], shift1, ALU.add))
            signal("h1")
            split_rows()
            copy_out("in1", lambda tt, c, n: PROJ1[:, tt, c:c + n])
            for tt in range(TT):
                x = PROJ1[:, tt, 0:1024].rearrange("p (h two e) -> p two h e", two=2, e=32)
                o = Y[:, tt, :].rearrange("p (h two e) -> p two h e", two=2, e=32)
                t = [H[:, 0, 512 * i:512 * (i + 1)].rearrange("p (h e) -> p h e", e=32) for i in range(2)]
                t += [H[:, 1, 512 * i:512 * (i + 1)].rearrange("p (h e) -> p h e", e=32) for i in range(2)]
                cos = tab("cos1")[:, 32 * tt:32 * (tt + 1)].unsqueeze(1).to_broadcast([P, 16, 32])
                sin = tab("sin1")[:, 32 * tt:32 * (tt + 1)].unsqueeze(1).to_broadcast([P, 16, 32])
                rotate(x[:, 0], x[:, 1], o[:, 0], o[:, 1], cos, sin, t)
            signal("rope1")
            attend(A_DIL)
            signal("dil_out")
            dve.wait_ge(E("small"), 16 * len(small_at))
            gb = small("b_gate", 256).unsqueeze(1).to_broadcast([P, TT, 256])
            az = H[:, :, 0:256]
            release(dve.tensor_tensor(LA, unit()[:, :].rearrange("p (t n) -> p t n", t=TT), gb, ALU.add))
            mark(dve.scalar_tensor_tensor(az, LA, -1.0, LA, ALU.mult, ALU.max), "z_abs")
            dve.wait_ge(E("z_log"), 1)
            step(dve.scalar_tensor_tensor(LA, LA, 0.0, az, ALU.min, ALU.subtract))
            mark(dve.tensor_scalar(LA, LA, 1.0 / 16.0, None, ALU.mult), "log_a")
            for tt in range(TT):
                release(dve.tensor_copy(GB[:, tt, :], unit()[:, :]))
            step(dve.tensor_tensor(GB[:, :, 256:512], GB[:, :, 256:512], GB[:, :, 0:256], ALU.subtract))
            release(dve.tensor_copy(MISC[:, 8:16], unit()[:, 0:8]))
            signal("gla_b")
            dve.wait_ge(E("gla_exp"), 1)
            qg, kg = PROJ1[:, :, 1536:1792], PROJ1[:, :, 1792:2048]
            step(dve.scalar_tensor_tensor(QKD[:, :, 0:256], qg, 64.0 ** -0.5, Y[:, :, 0:256], ALU.mult, ALU.mult))
            step(dve.tensor_tensor(QKD[:, :, 256:512], kg, Y[:, :, 256:512], ALU.mult))
            mark(dve.tensor_tensor(KL, kg, GB[:, :, 256:512], ALU.mult), "gla_qk")
            step(dve.memset(ATTM, 0.0))
            step(dve.memset(STATE[:, 0], 0.0))
            dve.wait_ge(E("gla_mask"), 16)
            for tt in range(TT):
                for par in range(2):
                    dst = ATTM[:, tt, :].rearrange("p (m two c) -> p two m c", m=2, two=2)[:, par]
                    release(dve.copy_predicated(dst, TMASK[:, 0:256].rearrange("p (m c) -> p m c", m=2),
                                                unit()[:, 0:256].rearrange("p (m c) -> p m c", m=2)))
            u02 = unit()[:, :].rearrange("p (n m e) -> p n m e", n=2, m=2)
            step(dve.tensor_copy(STATE[:, 1], u02[:, 0]))
            u1 = unit()[:, 0:256].rearrange("p (m e) -> p m e", m=2)
            for n, u in ((2, u1), (3, u02[:, 1])):
                for m in range(2):
                    step(dve.scalar_tensor_tensor(STATE[:, n, m], STATE[:, n - 1, m], AN[:, m, n - 1:n], u[:, m],
                                                  ALU.mult, ALU.add))
            dve.sem_inc(unit_read, 2)
            signal("gla_state")
            for tt in range(TT):
                release(dve.tensor_copy(OG[:, tt, :], unit()[:, :]))
                for par in range(2):
                    dst = OG[:, tt, :].rearrange("p (m two e) -> p two m e", m=2, two=2)[:, par]
                    release(dve.tensor_tensor(dst, dst, unit()[:, 0:256].rearrange("p (m e) -> p m e", m=2), ALU.add))
                rms_heads(OG[:, tt, :].rearrange("p (h e) -> p h e", h=4), 4, P, small("g_gla", 128))
                dve.wait_ge(E("silu_r"), 1)
                step(dve.tensor_tensor(MIX[:, tt, 512:1024], OG[:, tt, :], SR[:, tt, :], ALU.mult))
            signal("mix1")

            def gated_residual(gate, name):
                v = vec(name)
                step(dve.tensor_tensor(gate, gate, v, ALU.mult))
                vec_over(name)
                for tt in range(TT):
                    y = Y[:, tt, :]
                    rms_rows(y, y, gate)
                    step(dve.tensor_tensor(X[:, tt, :], X[:, tt, :], y, ALU.add))

            split_rows()
            copy_out("out1", lambda tt, c, n: Y[:, tt, c:c + n])
            gated_residual(gate1, "g_post_mix")
            gain(scale2, "g_pre_ffn")
            for tt in range(TT):
                rms_rows(H[:, tt, :], X[:, tt, :], scale2)
                step(dve.tensor_tensor(H[:, tt, :], H[:, tt, :], shift2, ALU.add))
            signal("h2")
            split_rows()
            gemm("router", lambda s, tt, b: release(dve.tensor_tensor(RT[:, tt, :], s, small("router_b", 32), ALU.add)))
            for tt in range(TT):
                step(dve.max(TOPV[:, :], RT[:, tt, :]))
                step(dve.max_index(TOPI[:, :], TOPV[:, :], RT[:, tt, :]))
                step(dve.tensor_copy(TOPF[:, :], TOPI[:, :]))
                step(dve.tensor_scalar(MISC[:, 50:51], TOPV[:, 0:1], -1.0, None, ALU.mult))
                mark2 = f"top{tt}"
                signal(mark2)
                dve.wait_ge(E(f"top_exp{tt}"), 1)
                step(dve.reciprocal(MISC[:, 51:52], MISC[:, 52:53]))
                step(dve.tensor_scalar(MISC[:, 54:58], MISC[:, 58:62], MISC[:, 51:52], None, ALU.mult))
                for j in range(TOP_K):
                    dst = MASKS[:, tt, :] if j == 0 else TMP32
                    step(dve.tensor_scalar(dst, tab("ramp32"), TOPF[:, j:j + 1], None, ALU.is_equal))
                    if j == 0:
                        step(dve.tensor_scalar(GATES[:, tt, :], dst, MISC[:, 54:55], None, ALU.mult))
                    else:
                        step(dve.tensor_tensor(MASKS[:, tt, :], MASKS[:, tt, :], TMP32, ALU.add))
                        step(dve.scalar_tensor_tensor(GATES[:, tt, :], TMP32, MISC[:, 54 + j:55 + j], GATES[:, tt, :],
                                                      ALU.mult, ALU.add))
            signal("routed")
            b = unit()
            for tt in range(TT):
                p = POS[tt][:, 0:N_EXP]
                step(dve.scalar_tensor_tensor(p, b[:, 32 * tt:32 * (tt + 1)], 1.0, MASKS[:, tt, :], ALU.add, ALU.mult))
                step(dve.tensor_scalar(p, p, -1.0, None, ALU.add))
                step(dve.tensor_scalar(POS[tt][:, N_EXP:N_EXP + 1], POS[tt][:, 0:1], -float(CAP), None, ALU.add))
            step(dve.tensor_reduce(MISC[:, 35:36], b[:, 64:96], AX, ALU.max))
            dve.sem_inc(unit_read, 1)
            mark(dve.tensor_scalar(NPASS[:, :], MISC[:, 35:36], float(CAP), 1.0, ALU.is_gt, ALU.add), "n_pass")
            n_pass = dve.value_load(NPASS[0:1, 0:1], min_val=1, max_val=2)
            step(dve.memset(GSELT, 0.0))
            mark(dve.memset(OUTE[:, 0:512], 0.0), "moe_zero")
            dve.sem_inc(m_up_read, 4)
            dve.sem_inc(m_lo[0], lo_per[0])

            def choose(col):
                for tt in range(TT):
                    ins = dve.tensor_scalar(PSEL[:, tt, :], tab("ramp"), POS[tt][:, col], None, ALU.is_equal)
                ins.then_inc(m_sel, 1)

            def tokens_low(done):
                for half in range(2):
                    k = slice(4 * half, 4 * half + 4)
                    dve.wait_ge(m_xhi, done + half)
                    dve.tensor_tensor(XETl[:, k, :], bank[6 + half][:, :].rearrange("p (a b) -> p a b", a=4),
                                      XETh[:, k, :].bitcast(F32), ALU.subtract).then_inc(m_xlo, 1)

            choose(slice(0, 1))
            tokens_low(1)
            with dve.Fori(0, n_pass) as ps:
                with dve.Fori(0, N_EXP) as ex:
                    it = ps * N_EXP + ex

                    def lows(first, last):
                        for t in range(first, last):
                            if not pool_tile(t):
                                dve.wait_ge(m_hi, it * MOE_TILES + t + 1)
                                dve.tensor_tensor(w_lo[:, t % PARTS, :], moe_raw(t), w_hi[:, t % PARTS, :].bitcast(F32),
                                                  ALU.subtract).then_inc(m_lo[0], 1)

                    def add_bias(b):
                        c = slice(512 * b, 512 * (b + 1))
                        dve.wait_ge(m_used, moe_used(it, 4 * b + 3))
                        dve.tensor_tensor(GU[:, c], bank[4 + b % 2][:, :], BB[:, c], ALU.add).then_inc(m_up_read, 1)

                    lows(0, 8)
                    dve.wait_ge(m_bias, it + 1)
                    add_bias(0)
                    lows(8, 12)
                    add_bias(1)
                    lows(12, 16)
                    add_bias(2)
                    lows(16, 18)
                    dve.wait_ge(m_gather, it * 2 + 2)
                    choose(bass.ds(ex + 1, 1))
                    add_bias(3)
                    dve.wait_ge(m_up_read, it * 4 + 8)
                    dve.tensor_scalar(GL, glu_in[:, :, 0], 7.0, None, ALU.min).then_inc(m_glu, 1)
                    dve.tensor_scalar(AV, glu_in[:, :, 1], 7.0, -7.0, ALU.min, ALU.max).then_inc(m_chain, 1)
                    for tt in range(TT):
                        ins = dve.tensor_scalar(GSEL[:, tt, :], tab("ramp"), POS[tt][:, bass.ds(ex, 1)],
                                                GATES[:, tt, bass.ds(ex, 1)], ALU.is_equal, ALU.mult)
                    ins.then_inc(m_chain, 1)
                    dve.wait_ge(m_sig, it + 1)
                    dve.wait_ge(m_chain, it * M_STEPS + 2)
                    dve.tensor_tensor(GL, GL, SG, ALU.mult).then_inc(m_chain, 1)
                    dve.wait_ge(m_chain, it * M_STEPS + 3)
                    dve.scalar_tensor_tensor(AV, AV, 1.0, GL, ALU.add, ALU.mult).then_inc(m_act, 1)
                    tokens_low(it * 2 + 3)
                    for half in range(2):
                        k = slice(4 * half, 4 * half + 4)
                        dve.wait_ge(m_ahi, it * 2 + 1 + half)
                        dve.tensor_tensor(AVTl[:, k, :], bank[6 + half][:, :].rearrange("p (a b) -> p a b", a=4),
                                          AVTh[:, k, :].bitcast(F32), ALU.subtract).then_inc(m_alo, 1)
                    lows(18, MOE_TILES)
                for tt in range(TT):
                    dve.tensor_scalar(POS[tt], POS[tt], -float(CAP), None, ALU.add).then_inc(m_pass, 1)
                dve.wait_ge(m_pass, ps * TT + TT)
            dve.wait_ge(E("moe_over"), 1)
            for i in range(4):
                step(dve.tensor_copy(Y[:, i // 2, 512 * (i % 2):512 * (i % 2 + 1)], bank[i][:, :]))
            signal("moe_sum")
            gated_residual(gate2, "g_post_ffn")
            signal("x1")

            ffn("f1", scaled(0.5))
            layer_norm(1)
            split_rows()
            copy_out("in2", lambda tt, c, n: PROJ2[:, tt, c:c + n])
            gate_bias = [vec(f"b_gate2_{i}") for i in range(2)]

            def gate(s, tt, b):
                v = gate_bias[b.col // D]
                release(dve.tensor_tensor(GATE2[:, tt, b.col:b.col + b.cols], s, v[:, b.col % D:b.col % D + b.cols], ALU.add))

            gemm("gate2", gate)
            for i in range(2):
                vec_over(f"b_gate2_{i}")
            signal("gate2_in")
            for tt in range(TT):
                cq, ckv = PROJ2[:, tt, 0:384], PROJ2[:, tt, 384:640]
                rms_rows(cq, cq, small("q_norm_g_2", 384))
                rms_rows(ckv, ckv, small("kv_norm_g_2", 256))
            signal("c_norm")
            rows_lo([(HTl[:, k:k + n, :], HTh[:, k:k + n, :]) for k, n in ((0, 2), (2, 2), (4, 1))])
            for i in range(2):
                step(dve.tensor_tensor_reduce(SQ[:, 0:64], small(f"lam_q{i + 1}_2", 64), small(f"lam_k{i + 1}_2", 64),
                                              1.0, 0.0, ALU.mult, ALU.add, MISC[:, 16 + i:17 + i]))
            signal("lam_in")
            copy_out("q_b", lambda tt, c, n: QM[:, tt, c:c + n])
            copy_out("kv_b", lambda tt, c, n: KV[:, tt, c:c + n])
            dve.wait_ge(E("lam_exp"), 1)
            step(dve.tensor_tensor(MISC[:, 20:21], MISC[:, 19:20], MISC[:, 18:19], ALU.subtract))
            step(dve.tensor_scalar(MISC[:, 21:22], MISC[:, 20:21], -LAM_INIT, None, ALU.add))
            for tt in range(TT):
                cos = tab("cos2")[:, 16 * tt:16 * (tt + 1)]
                sin = tab("sin2")[:, 16 * tt:16 * (tt + 1)]
                t = [SQ[:, 128 * i:128 * (i + 1)].rearrange("p (h e) -> p h e", e=16) for i in range(4)]
                x = QM[:, tt, :].rearrange("p (h e) -> p h e", h=MLA_H)
                spread = lambda a: a.unsqueeze(1).to_broadcast([P, MLA_H, 16])
                rotate(x[:, :, 64:80], x[:, :, 80:96], x[:, :, 64:80], x[:, :, 80:96], spread(cos), spread(sin), t)
                r = PROJ2[:, tt, 640:672]
                t = [SQ[:, 16 * i:16 * (i + 1)] for i in range(4)]
                rotate(r[:, 0:16], r[:, 16:32], r[:, 0:16], r[:, 16:32], cos, sin, t)
                km = KM[:, tt, 0:MLA_H * MLA_QK].rearrange("p (h e) -> p h e", h=MLA_H)
                step(dve.tensor_copy(km[:, :, 0:MLA_NOPE], KV[:, tt, :].rearrange("p (h e) -> p h e", h=MLA_H)[:, :, 0:MLA_NOPE]))
                step(dve.tensor_copy(km[:, :, MLA_NOPE:], r.unsqueeze(1).to_broadcast([P, MLA_H, MLA_ROPE])))
            signal("mla_qk")
            attend(A_MLA)
            dve.wait_ge(E("bias2"), 16)
            attend(A_DIFF)
            signal("diff_done")
            for tt in range(TT):
                o = OD8[:, tt, :].rearrange("p (h two e) -> p two h e", two=2, e=P)
                d = MIX[:, tt, 512:1024].rearrange("p (h e) -> p h e", h=4)
                step(dve.scalar_tensor_tensor(d, o[:, 1], MISC[:, 21:22], o[:, 0], ALU.mult, ALU.add))
                rms_heads(d, 4, P, small("diff_norm_g_2", 128), 1.0 - LAM_INIT)
            signal("mix2")
            split_rows()
            dve.wait_ge(E("gate2_sig"), 1)

            def gated_pair(first, second, gates, at):
                def put_first(s, tt, b):
                    release(dve.tensor_tensor(Y[:, tt, b.col:b.col + b.cols], s,
                                              gates[:, tt, at + b.col:at + b.col + b.cols], ALU.mult))

                def put_second(s, tt, b):
                    c = slice(b.col, b.col + b.cols)
                    release(dve.tensor_tensor(MIX[:, tt, c], s, gates[:, tt, at + D + b.col:at + D + b.col + b.cols], ALU.mult))
                    step(dve.tensor_tensor(MIX[:, tt, c], MIX[:, tt, c], Y[:, tt, c], ALU.add))

                gemm(first, put_first)
                gemm(second, put_second)

            gated_pair("up_mla", "up_diff", GATE2, 0)
            signal("gated2")
            split_rows()
            gemm("o2", scaled(1.0))
            layer_norm(2)
            split_rows()
            copy_out("mem_q", lambda tt, c, n: QMEM[:, tt, c:c + n])
            split_rows()
            copy_out("mem_kv", lambda tt, c, n: KVM[:, tt, c:c + n])
            signal("mem_qkv")
            attend(A_MEM)
            signal("mem_out")
            split_rows()
            gemm("mem_o", scaled(1.0))
            layer_norm(3)
            ffn("f2", scaled(0.5))
            layer_norm(4)

            def normed(name, ready):
                v = vec(name)
                for tt in range(TT):
                    rms_rows(H[:, tt, :], X[:, tt, :], v)
                vec_over(name)
                signal(ready)

            normed("ffn1_norm", "h3")
            ffn("f3", halved(0.5))
            normed("mix_norm", "h4")
            split_rows()
            copy_out("in3", lambda tt, c, n: PROJ3[:, tt, c:c + n])
            for i in range(2):
                v = vec(f"b_gate3_{i}")
                for tt in range(TT):
                    g = PROJ3[:, tt, 3396 + D * i:3396 + D * (i + 1)]
                    step(dve.tensor_tensor(g, g, v, ALU.add))
                vec_over(f"b_gate3_{i}")
            signal("gate3_in")
            for tt in range(TT):
                step(dve.tensor_copy(KI2[:, tt, :].rearrange("p (a e) -> p a e", a=2),
                                     PROJ3[:, tt, 3328:3392].unsqueeze(1).to_broadcast([P, 2, 64])))
                for c, g in ((0, "q_norm_dsa_3"), (512, "k_norm_dsa_3"), (1536, "q_norm_moba_3"), (2048, "k_norm_moba_3")):
                    rms_heads(PROJ3[:, tt, c:c + 512].rearrange("p (h e) -> p h e", h=8), 8, HD, small(g, 64))
                step(dve.tensor_scalar(MISC[:, 4 * tt:4 * tt + 4], PROJ3[:, tt, 3392:3396], 4.0 ** -0.5, None, ALU.mult))
            signal("qk3")
            for tt in range(TT):
                nk = P * (tt + 1)
                sc = SEL[:, tt, 0:nk]
                for i in range(4):
                    if i % 2 == 0:
                        b = unit()
                    h = 2 * (i % 2) + i // 2
                    w = MISC[:, 4 * tt + h:4 * tt + h + 1]
                    dots = SQ[:, 0:nk]
                    ins = dve.tensor_scalar(dots, b[:, (i % 2) * nk:(i % 2 + 1) * nk], 64.0 ** -0.5, 0.0, ALU.mult, ALU.max)
                    if i % 2 == 1:
                        release(ins)
                    else:
                        step(ins)
                    if i == 0:
                        step(dve.tensor_scalar(sc, dots, w, None, ALU.mult))
                    else:
                        step(dve.scalar_tensor_tensor(sc, dots, w, sc, ALU.mult, ALU.add))
                m = tab("causal")[:, P:S] if tt == 0 else tab("causal")
                step(dve.tensor_tensor(sc, sc, m, ALU.add))
                for r in range(DSA_TOPK // 8):
                    step(dve.max(TOPV[:, :], sc))
                    step(dve.match_replace(sc, TOPV[:, :], sc, TAKEN))
                step(dve.tensor_scalar(sc, sc, TAKEN / 2, NEG, ALU.is_gt, ALU.mult))
            dve.wait_ge(E("bias3a"), 16)
            attend(A_DSA)
            signal("dsa_done")
            dve.wait_ge(E("bias3b"), 16)
            attend(A_MOBA)
            signal("mix3")
            split_rows()
            dve.wait_ge(E("gate3_sig"), 1)
            gated_pair("br_dsa", "br_moba", PROJ3, 3396)
            signal("gated3")
            split_rows()
            gemm("out3", halved(1.0))
            normed("ffn2_norm", "h5")
            ffn("f4", halved(0.5))
            signal("result")
            pows["n"] = npow[0]

        @block.scalar
        def _(act):
            group = [0]
            att = [0]
            split = [0]
            rows = [0]

            def high(n, landed, used):
                m = tiles[n].kts * tiles[n].cols
                act.wait_ge(raw_landed[n % RAW], landed)
                if used is not None:
                    act.wait_ge(tile_used, used)
                act.activation(w_hi[:, n % PARTS, 0:m], raw[:, n % RAW, 0:m], ACT.Copy).then_inc(hi_done, 1)

            def split_to(n):
                for i in range(split[0], n):
                    high(i, tiles[i].landed, i - PARTS + 1 if i >= PARTS else None)
                split[0] = max(split[0], n)

            def gemm(*names):
                n = G[names[-1]][-1].tiles[-1].n + 1
                split_to(min(n + AHEAD, moe_at if n <= moe_at else len(tiles)))

            def rows_hi_to(dsts):
                for dst in dsts:
                    g = rows[0]
                    act.wait_ge(rows_turned, g + 1)
                    n = dst.shape[1] * dst.shape[2]
                    act.activation(dst, bank[4 + g % 2][:, 0:n].rearrange("p (a b) -> p a b", a=dst.shape[1]),
                                   ACT.Copy).then_inc(rows_hi, 1)
                    rows[0] += 1

            def split_rows():
                rows_hi_to([HTh[:, 4 * k:4 * k + 4, tt * P:(tt + 1) * P] for tt in range(TT) for k in range(2)])

            def turned_to(dsts):
                for dst, rows, n in dsts:
                    g = group[0]
                    act.wait_ge(turned, g + 1)
                    src = bank[4 + g % 2][0:rows, 0:n]
                    if len(dst.shape) == 3:
                        src = src.rearrange("p (a b) -> p a b", a=dst.shape[1])
                    act.activation(dst, src, ACT.Copy).then_inc(turned_read, 1)
                    group[0] += 1

            def rows_to(dst):
                turned_to([(dst[:, 4 * k:4 * k + 4, tt * P:(tt + 1) * P], P, 512) for tt in range(TT) for k in range(2)])

            def attend(a):
                n = len(a.units)
                for i in range(n + LOOKAHEAD):
                    if i < n:
                        h, tt = a.units[i]
                        nk = a.keys(tt)
                        k = att[0] + i
                        act.wait_ge(att_shifted, k + 1)
                        for hh in range(2):
                            p = PR[:, k % 3, hh * nk:(hh + 1) * nk]
                            ins = act.activation(p, p, ACT.Exp, bias=NM[:, k % 3, hh:hh + 1],
                                                 accum_out=LS[:, k % 3, hh:hh + 1])
                        ins.then_inc(att_exp, 1)
                    if i >= LOOKAHEAD:
                        h, tt = a.units[i - LOOKAHEAD]
                        k = att[0] + i - LOOKAHEAD
                        turned_to([(PT[:, k % 2, 0:2 * a.keys(tt)], P, 2 * a.keys(tt))])
                att[0] += n

            def ffn(name):
                f = FFN[name]
                n0, last = f.n0, FFN_STEPS - 1

                def silu(used):
                    act.wait_ge(tile_used, used)
                    for tt in range(TT):
                        act.activation(FA[:, tt, :], bank[6 + tt][:, 0:GLU], ACT.Silu).then_inc(E(name + "_silu"), 1)

                def turned_high(turn):
                    act.wait_ge(E(name + "_turned"), turn)
                    act.activation(AFTh[:, :, :], bank[5][:, :].rearrange("p (a b) -> p a b", a=2),
                                   ACT.Copy).then_inc(E(name + "_turned_hi"), 1)

                split_rows()
                split_to(n0 + 4)
                silu(n0 + 4)
                with act.Fori(0, FFN_PAIRS) as pair:
                    for two in range(2):
                        for i in range(FFN_TILES):
                            n = n0 + 4 + FFN_TILES * two + i
                            if i == 4:
                                turned_high(pair * 2 + two + 1)
                            high(n, pair * (32 * 2 * FFN_TILES // RAW) + tiles[n].landed, pair * (2 * FFN_TILES) + n - PARTS + 1)
                        silu(pair * (2 * FFN_TILES) + n0 + 8 + FFN_TILES * two)
                turned_high(FFN_STEPS)
                n = n0 + 4 + FFN_TILES * last
                split[0] = n
                split_to(min(n + 2 + AHEAD, len(tiles)))

            def one(wait, name, *ops):
                act.wait_ge(E(wait), 1)
                for o in ops:
                    ins = act.activation(*o[0:3], **o[3])
                ins.then_inc(E(name), 1)

            act.wait_ge(E("c_in"), 16)
            act.activation(CCOL, CCOL, ACT.Silu).then_inc(E("c_act"), 1)
            act.wait_ge(E("c_act"), 1)
            act.activation(HTh[:, :, 0:P], CCOL.unsqueeze(2).to_broadcast([P, KD, P]), ACT.Copy).then_inc(E("c_hi"), 1)
            gemm("mod5")
            split_rows()
            gemm("in1")
            rows_to(QT)
            attend(A_DIL)
            turned_to([(GLRT, 16, 256)])
            az = H[:, :, 0:256]
            act.wait_ge(E("z_abs"), 1)
            act.activation(az, az, ACT.Exp, scale=-1.0).then_inc(E("z_exp"), 1)
            act.wait_ge(E("z_exp"), 1)
            act.activation(az, az, ACT.Ln, bias=1.0).then_inc(E("z_log"), 1)
            one("gla_b", "gla_exp", (Y[:, :, 0:256], GB[:, :, 0:256], ACT.Exp, {}),
                (Y[:, :, 256:512], GB[:, :, 0:256], ACT.Exp, {"scale": -1.0}),
                (AN.rearrange("p m n -> p (m n)"), MISC[:, 8:16], ACT.Exp, {}),
                (GB[:, :, 256:512], GB[:, :, 256:512], ACT.Exp, {}))
            act.activation(SR, PROJ1[:, :, 2560:3072], ACT.Silu).then_inc(E("silu_r"), 1)
            act.wait_ge(E("rel_stored"), 16)
            turned_to([(GT[:, 0:4, tt * P:(tt + 1) * P], P, 512) for tt in range(TT)])
            split_rows()
            gemm("out1")
            split_rows()
            gemm("router")
            for tt in range(TT):
                act.wait_ge(E(f"top{tt}"), 1)
                act.activation(MISC[:, 58:62], TOPV[:, 0:4], ACT.Exp, bias=MISC[:, 50:51],
                               accum_out=MISC[:, 52:53]).then_inc(E(f"top_exp{tt}"), 1)
            turned_to([(GATET, 32, 256)])
            act.wait_ge(E("n_pass"), 1)
            n_pass = act.value_load(NPASS[0:1, 0:1], min_val=1, max_val=2)

            def tokens_high(done):
                for half in range(2):
                    act.wait_ge(m_gather, done + half)
                    act.activation(XETh[:, 4 * half:4 * half + 4, :], bank[6 + half][:, :].rearrange("p (a b) -> p a b", a=4),
                                   ACT.Copy).then_inc(m_xhi, 1)

            def out_half(n, used):
                act.wait_ge(m_used, used)
                act.activation(OUTE[:, 512 * n:512 * (n + 1)], bank[4 + n][:, :], ACT.Copy).then_inc(m_down_read, 1)

            act.wait_ge(E("moe_begun"), 1)
            act.wait_ge(E("moe_zero"), 1)
            act.sem_inc(m_down_read, 2)
            act.sem_inc(m_gtc, 1)
            tokens_high(1)
            with act.Fori(0, n_pass) as ps:
                with act.Fori(0, N_EXP) as ex:
                    it = ps * N_EXP + ex

                    def highs(first, last):
                        for t in range(first, last):
                            act.wait_ge(m_landed[t % MOE_RAW], it * (16 * MOE_TILES // MOE_RAW) + 16 * (t // MOE_RAW + 1))
                            act.wait_ge(m_used, moe_used(it, t - PARTS))
                            act.activation(w_hi[:, t % PARTS, :], moe_raw(t), ACT.Copy).then_inc(m_hi, 1)

                    highs(0, 2)
                    out_half(1, moe_used(it, -1))
                    highs(2, 18)
                    act.wait_ge(m_glu, it + 1)
                    act.activation(SG, GL, ACT.Sigmoid, scale=1.702).then_inc(m_sig, 1)
                    tokens_high(it * 2 + 3)
                    for half in range(2):
                        act.wait_ge(m_tr, it * 2 + 1 + half)
                        act.activation(AVTh[:, 4 * half:4 * half + 4, :], bank[6 + half][:, :].rearrange("p (a b) -> p a b", a=4),
                                       ACT.Copy).then_inc(m_ahi, 1)
                    act.wait_ge(m_gt, it + 1)
                    act.activation(GSELT, bank[5][:, 0:2 * P], ACT.Copy).then_inc(m_gtc, 1)
                    highs(18, 22)
                    out_half(0, moe_used(it, 19))
                    highs(22, MOE_TILES)
            out_half(1, n_pass * (N_EXP * MOE_TILES) + MOE_TILES)
            act.wait_ge(E("moe_over"), 1)
            ffn("f1")
            split_rows()
            gemm("in2", "gate2")
            act.wait_ge(E("gate2_in"), 1)
            act.activation(GATE2, GATE2, ACT.Sigmoid).then_inc(E("gate2_sig"), 1)
            rows_hi_to([HTh[:, k:k + n, :] for k, n in ((0, 2), (2, 2), (4, 1))])
            act.wait_ge(E("lam_in"), 1)
            act.activation(MISC[:, 18:20], MISC[:, 16:18], ACT.Exp).then_inc(E("lam_exp"), 1)
            gemm("q_b", "kv_b")
            for dst in (QT, KT):
                turned_to([(dst[0:MLA_QK, 4 * k:4 * k + 4, tt * P:(tt + 1) * P], MLA_QK, 512)
                           for tt in range(TT) for k in range(2)])
            attend(A_MLA)
            rows_to(QT)
            attend(A_DIFF)
            split_rows()
            gemm("up_mla", "up_diff")
            split_rows()
            gemm("o2")
            split_rows()
            gemm("mem_q")
            split_rows()
            gemm("mem_kv")
            rows_to(QT)
            rows_to(KT)
            attend(A_MEM)
            split_rows()
            gemm("mem_o")
            ffn("f2")
            ffn("f3")
            split_rows()
            gemm("in3")
            act.wait_ge(E("gate3_in"), 1)
            g3 = PROJ3[:, :, 3396:3396 + 2 * D]
            act.activation(g3, g3, ACT.Sigmoid).then_inc(E("gate3_sig"), 1)
            turned_to([(QT[:, 0:2, :], P, 512), (QT[:, 2, :], P, 256)])
            rows_to(QT)
            rows_to(KT)
            attend(A_DSA)
            act.wait_ge(E("dsa_done"), 1)
            act.dma_start(BIAS[:, :, :], bias_rows(16)).then_inc(E("bias3b"), 16)
            attend(A_MOBA)
            split_rows()
            gemm("br_dsa", "br_moba")
            split_rows()
            gemm("out3")
            ffn("f4")

        @block.gpsimd
        def _(pool):
            for name, (a, n, src) in small_at.items():
                pool.dma_start(SMALL[:, a:a + n], src[0:1, :].to_broadcast([P, n])).then_inc(E("small"), 16)
            pool.wait_ge(E("setup"), 64)

            def powers(first, last):
                with pool.Fori(first, last) as k:
                    pool.wait_ge(pow_in, k + 1)
                    pool.tensor_tensor(st_out[:, :], st_in[:, :], tab("half"), ALU.pow).then_inc(pow_out, 1)

            powers(0, POWS_FIRST)
            pool.wait_ge(E("n_pass"), 1)
            n_pass = pool.value_load(NPASS[0:1, 0:1], min_val=1, max_val=2)
            pool.sem_inc(m_lo[1], lo_per[1])
            with pool.Fori(0, n_pass) as ps:
                with pool.Fori(0, N_EXP) as ex:
                    it = ps * N_EXP + ex
                    pool.wait_ge(m_up_read, it * 4 + 4)
                    pool.dma_start(BROW, I["b_gate_up"][0][bass.ds(ex, 1), :]).then_inc(m_brow, 16)
                    pool.wait_ge(m_brow, it * 16 + 16)
                    pool.sem_inc(E("moe_bias_row_seen"), 1)
                    pool.partition_broadcast(BB, BROW).then_inc(m_bias, 1)
                    for t in range(MOE_TILES):
                        if pool_tile(t):
                            pool.wait_ge(m_hi, it * MOE_TILES + t + 1)
                            pool.tensor_tensor(w_lo[:, t % PARTS, :], moe_raw(t), w_hi[:, t % PARTS, :].bitcast(F32),
                                               ALU.subtract).then_inc(m_lo[1], 1)
            powers(POWS_FIRST, pows["n"])

        @block.sync
        def _(sp):
            sp.dma_start(CCOL, I["c"].rearrange("a (k p) -> p (a k)", p=P), allow_slow_non_contiguous=True).then_inc(E("c_in"), 16)
            sp.dma_start(TAB[:, :], I["table"]).then_inc(E("setup"), 16)
            sp.dma_start(BUCK, I["buckets"]).then_inc(E("setup"), 16)
            sp.dma_start(SMALLB[:, 0:8], I["rel_bias_2"]).then_inc(E("setup"), 16)
            sp.dma_start(SMALLB[:, 8:24], I["rel_bias_3"]).then_inc(E("setup"), 16)
            sp.dma_start(X[:, :, :], I["x"][0].rearrange("(t p) n -> p t n", p=P)).then_inc(E("x_in"), 16)
            sp.dma_start(TMASK, I["gla_mask"]).then_inc(E("gla_mask"), 16)
            sp.dma_start(WGLR[:, :], I["w_gate_lr"][0]).then_inc(E("gate_lr"), 16)

            def load(n, loads, freed):
                if freed is not None:
                    sp.wait_ge(lo_done, freed)
                t = tiles[n]
                dst = raw[:, n % RAW, 0:t.kts * t.cols].rearrange("p (k n) -> p k n", k=t.kts)
                for part, src in loads(dst):
                    sp.dma_start(part, src).then_inc(raw_landed[n % RAW], 16)

            def load_ffn(f):
                def up(n, col, freed):
                    for i in range(4):
                        load(n + i, lambda dst: [(dst[:, :, c:c + m], src) for c, m, src in f.up(i, col)], freed + i)

                def down(n, j, freed):
                    for i in range(2):
                        load(n + i, lambda dst: [(dst[:, k:k + 1, :], f.down_src[j, k:k + 1, :, 512 * i:512 * (i + 1)]
                                                  .rearrange("j k p n -> p (j k) n")) for k in range(2)], freed + i)

                n0, last = f.n0, FFN_STEPS - 1
                up(n0, slice(0, GLU), n0 - RAW + 1)
                with sp.Fori(0, FFN_PAIRS) as pair:
                    for two in range(2):
                        n = n0 + 4 + FFN_TILES * two
                        freed = pair * (2 * FFN_TILES) + n + 1 - RAW
                        up(n, bass.ds(pair * (2 * GLU) + GLU * (two + 1), GLU), freed)
                        down(n + 4, bass.ds(pair * 2 + two, 1), freed + 4)
                n = n0 + 4 + FFN_TILES * last
                down(n, slice(last, last + 1), n + 1 - RAW)

            for kind, c in order:
                if kind == "tile":
                    load(c.n, lambda dst: [(dst[:, :, a:a + m], src) for a, m, src in c.loads],
                         c.n - RAW + 1 if c.n >= RAW else None)
                    if c.n == RAW - 1:
                        sp.wait_ge(E("rel_rows"), 1)
                        sp.dma_start(arr_dram.ap(), RELS).then_inc(E("rel_stored"), 16)
                        sp.wait_ge(E("rel_stored"), 16)
                        sp.dma_start(skew_dram.ap().rearrange("h (p n) -> h p n", p=P),
                                     arr_dram.ap().unsqueeze(1).to_broadcast([24, P, 384])).then_inc(E("rel_skewed"), 16)
                elif kind == "vec":
                    src, _ = vecs[c]
                    if c >= VECS:
                        sp.wait_ge(vec_used, c - VECS + 1)
                    sp.dma_start(VEC[:, c % VECS, :], src[0:1, :].to_broadcast([P, D])).then_inc(vec_landed[c % VECS], 16)
                elif kind == "mem":
                    sp.wait_ge(E("diff_done"), 1)
                    sp.dma_start(H[:, :, :], I["mem_2"][0].rearrange("(t p) n -> p t n", p=P)).then_inc(E("mem_in"), 16)
                    sp.dma_start(BIAS[:, :, :], bias_rows(8)).then_inc(E("bias3a"), 16)
                elif kind == "ffn":
                    load_ffn(c)
                elif kind == "moe":
                    sp.wait_ge(lo_done, moe_at)
                    sp.wait_ge(E("mix1"), 1)
                    sp.dma_start(BDOWN, I["b_down"][0]).then_inc(E("b_down"), 16)
                    sp.wait_ge(E("n_pass"), 1)
                    n_pass = sp.value_load(NPASS[0:1, 0:1], min_val=1, max_val=2)
                    wu = I["w_gate_up"][0].rearrange("e (k p) n -> e p k n", p=P)
                    wd = I["w_down"][0].rearrange("e (k p) n -> e p k n", p=P)
                    with sp.Fori(0, n_pass) as ps:
                        with sp.Fori(0, N_EXP) as ex:
                            it = ps * N_EXP + ex
                            for t in range(MOE_TILES):
                                b, k = t // 4, 2 * (t % 4)
                                w, b = (wu, b) if b < 4 else (wd, b - 4)
                                sp.wait_ge(*moe_lo(it, t - MOE_RAW))
                                sp.dma_start(moe_raw(t).rearrange("p (k n) -> p k n", k=2),
                                             w[bass.ds(ex, 1), :, k:k + 2, 512 * b:512 * (b + 1)]
                                             .rearrange("e p k n -> p (e k) n")).then_inc(m_landed[t % MOE_RAW], 16)
                    sp.wait_ge(E("moe_over"), 1)
                    sp.wait_ge(E("rel_skewed"), 16)
                    sp.dma_start(BIAS[:, :, :], bias_rows(0)).then_inc(E("bias2"), 16)
            sp.wait_ge(E("result"), 1)
            sp.dma_start(out[0].rearrange("(t p) n -> p t n", p=P), X[:, :, :]).then_inc(E("stored"), 16)
            sp.wait_ge(E("stored"), 16)


NAMES = """x c w_mod b_mod g_pre_mix w_in w_gate_lr b_gate g_gla w_out g_post_mix g_pre_ffn router_w router_b w_gate_up
b_gate_up w_down b_down g_post_ffn mem_2 rel_bias_2 ffn1_w1_2 ffn1_w3_2 ffn1_w2_2 ln1_g_2 ln1_b_2 w_in_2 q_norm_g_2
kv_norm_g_2 w_q_b_2 w_kv_b_2 lam_q1_2 lam_k1_2 lam_q2_2 lam_k2_2 diff_norm_g_2 w_gate_2 b_gate_2 w_up_mla_2
w_up_diff_2 w_o_2 ln2_g_2 ln2_b_2 mem_w_q_2 mem_w_kv_2 mem_w_o_2 ln3_g_2 ln3_b_2 ffn2_w1_2 ffn2_w3_2 ffn2_w2_2 ln4_g_2
ln4_b_2 ffn1_norm_3 ffn1_w_gu_3 ffn1_w_down_3 mix_norm_3 w_in_3 b_gate_3 q_norm_dsa_3 k_norm_dsa_3 q_norm_moba_3
k_norm_moba_3 w_branch_dsa_3 w_branch_moba_3 w_out_3 ffn2_norm_3 ffn2_w_gu_3 ffn2_w_down_3 rel_bias_3""".split()


def kernel(**inputs):
    import concourse.bacc as bacc
    from concourse.bass_utils import run_bass_kernel_spmd

    nc = bacc.Bacc("TRN2", target_bir_lowering=False, num_devices=1)
    arrays = {name: np.ascontiguousarray(inputs[name]) for name in NAMES}
    arrays.update(table=TABLE, buckets=BUCKETS, gla_mask=GLA_MASK)
    I = {name: nc.dram_tensor(f"in_{name}", a.shape, mybir.dt.from_np(a.dtype), kind="ExternalInput").ap()
         for name, a in arrays.items()}
    out = nc.dram_tensor("result", (1, S, D), F32, kind="ExternalOutput").ap()
    build(nc, I, out)
    got = run_bass_kernel_spmd(nc, [{f"in_{k}": a for k, a in arrays.items()}], core_ids=[0])
    return got.results[0]["result"]
```

```python
import math
from contextlib import ExitStack

import numpy as np

import concourse.bass as bass
from concourse import mybir

P = 128
D = 1024
S = 256
TT = S // P
KD = D // P
NEG = -1.0e30
TAKEN = -3.0e38

N_EXP, TOP_K, F_MOE = 32, 4, 1024
CAP = P
F_FFN = 2816
GLU = 256
HD = 64
IN1 = 3088
IN2 = 2208
IN3 = 5444
MLA_H, MLA_NOPE, MLA_ROPE = 8, 64, 32
MLA_QK = MLA_NOPE + MLA_ROPE
DSA_TOPK = 64
ALPHA = 2.0 ** 0.25
LAM_INIT = 0.8 - 0.6 * math.exp(-0.3 * 0)
RAW = 4
MOE_RAW = 8
PARTS = 4
VECS = 3
LOW_AHEAD = 1
TILE = 1024
FFN_TILES = 6
FFN_STEPS = F_FFN // GLU
FFN_PAIRS = (FFN_STEPS - 1) // 2
MOE_TILES = 24
POOL_TILES = (7, 11, 15, 19, 23)
GEMM_BANKS = 4
LOOKAHEAD = 2

ALU = mybir.AluOpType
ACT = mybir.ActivationFunctionType
AX = mybir.AxisListType.X
F32 = mybir.dt.float32
F32R = mybir.dt.float32r
I32 = mybir.dt.int32
U32 = mybir.dt.uint32


def shape_constants():
    t = np.arange(P)
    q, k = P + t[:, None], np.arange(S)[None, :]
    dist = q - k
    count = ((dist >= 0) & (dist <= 128)).astype(np.float64)
    count += (dist >= 0) & (dist % 4 == 0)
    count += (dist >= 0) & (dist % 16 == 0)
    lnc = np.where(count > 0, np.log(np.maximum(count, 1)), NEG)
    causal = np.where(dist >= 0, 0.0, NEG)
    same = (t[:, None] // 64) == (t[None, :] // 64)
    upto = same & (t[:, None] <= t[None, :])
    chunk = np.stack([t // 64 == 0, t // 64 == 1], 1)
    before = t[:, None] < t[None, :]

    def angles(inv):
        a = np.arange(S, dtype=np.float32)[:, None] * inv[None, :].astype(np.float32)
        a = a.reshape(TT, P, -1).transpose(1, 0, 2).reshape(P, -1)
        return np.cos(a), np.sin(a)

    half1 = np.float32(10000.0) ** (-np.arange(32, dtype=np.float32) / np.float32(32))
    half2 = np.float32(10000.0) ** (-np.arange(0, 32, 2, dtype=np.float32) / np.float32(32))
    cos1, sin1 = angles(half1)
    cos2, sin2 = angles(half2)
    parts = {
        "ident": np.eye(P), "lnc": lnc, "causal": causal, "upto": upto, "same": same, "chunk": chunk,
        "before": before, "ones": np.ones((P, P)), "ramp": np.tile(np.arange(P), (P, 1)),
        "ramp32": np.tile(np.arange(N_EXP), (P, 1)), "cos1": cos1, "sin1": sin1, "cos2": cos2, "sin2": sin2,
        "half": np.full((P, 1), -0.5),
    }
    at, n = {}, 0
    for name, a in parts.items():
        at[name] = (n, a.shape[1])
        n += a.shape[1]
    table = np.concatenate([np.asarray(a, np.float32) for a in parts.values()], 1)
    d = (S - 1) - np.arange(384)
    n_ = np.maximum(d, 1).astype(np.float32)
    large = 16 + (np.log(n_ / np.float32(16)) / np.float32(math.log(8.0)) * np.float32(16)).astype(np.int32)
    bucket = np.where(np.maximum(d, 0) < 16, np.maximum(d, 0), np.minimum(large, 31))
    onehot = (np.arange(32)[:, None] == bucket[None, :]) & (d >= 0)[None, :]
    ahead = np.tile(np.where(d >= 0, 0.0, NEG)[None, :], (32, 1))
    buckets = np.concatenate([onehot, ahead], 1).astype(np.float32)
    mask = np.tile(upto.astype(np.int32), (1, 4))
    return table, at, buckets, mask


TABLE, TABLE_AT, BUCKETS, GLA_MASK = shape_constants()


class Tile:

    def __init__(self, n, kts, cols, loads, landed):
        self.n, self.kts, self.cols, self.loads, self.landed = n, kts, cols, loads, landed


class Block:

    def __init__(self, col, cols, tiles):
        self.col, self.cols, self.tiles = col, cols, tiles


def build(nc, I, out):
    ctx = ExitStack()
    with ctx:
        sb = lambda name, shape, dt=F32: ctx.enter_context(nc.sbuf_tensor(name, shape, dt))
        sems = {}

        def sem(name):
            if name not in sems:
                sems[name] = ctx.enter_context(nc.semaphore(name))
            return sems[name]

        raw = sb("raw", [P, RAW, TILE])
        w_hi = sb("w_hi", [P, PARTS, TILE], F32R)
        w_lo = sb("w_lo", [P, PARTS, TILE], F32R)
        arena = sb("arena", [P, 10888])
        X = sb("X", [P, TT, D])
        HTh = sb("HTh", [P, KD, S], F32R)
        HTl = sb("HTl", [P, KD, S], F32R)
        AFTh = sb("AFTh", [P, 2, S], F32R)
        AFTl = sb("AFTl", [P, 2, S], F32R)
        Y = sb("Y", [P, TT, D])
        H = sb("H", [P, TT, D])
        QT = sb("QT", [P, KD, S])
        KT = sb("KT", [P, KD, S])
        MIX = sb("MIX", [P, TT, D])
        BIAS = sb("BIAS", [P, 8, S])
        VEC = sb("VEC", [P, VECS, D])
        PR = sb("PR", [P, 3, 512])
        PT = sb("PT", [P, 2, 512])
        SMALL = sb("SMALL", [P, 1696])
        TAB = sb("TAB", [P, TABLE.shape[1]])
        TMASK = KT[:, 0:2, :].rearrange("p a b -> p (a b)").bitcast(I32)
        st_in = sb("st_in", [P, 2, 32])
        st_out = sb("st_out", [P, 2, 32])
        SUMS = sb("SUMS", [P, 2, 32])
        STATS = sb("STATS", [P, 8])
        NEG_MEAN = sb("NEG_MEAN", [P, TT])
        MX = sb("MX", [P, 4, 2])
        NM = sb("NM", [P, 4, 2])
        LS = sb("LS", [P, 4, 2])
        RL = sb("RL", [P, 2])
        MISC = sb("MISC", [P, 64])
        TOPV = sb("TOPV", [P, 8])
        TOPI = sb("TOPI", [P, 8], U32)
        NPASS = sb("NPASS", [P, 1], I32)
        TOPF = sb("TOPF", [P, 8])
        WGLR = sb("WGLR", [16, 256])
        ZERO = sb("ZERO", [P, P], F32R)
        bank = [ctx.enter_context(nc.psum_tensor(f"bank{i}", [P, 512], F32)) for i in range(8)]

        def tab(name):
            a, n = TABLE_AT[name]
            return TAB[:, a:a + n]

        ident = tab("ident")
        arr_dram = nc.dram_tensor("rel_rows", [24, 384], F32)
        skew_dram = nc.dram_tensor("rel_skew", [24, P * 384], F32)

        def bias_rows(first):
            return bass.AP(tensor=skew_dram, offset=first * P * 384 + 127, ap=[[383, P], [P * 384, 8], [1, S]])

        def arena_at(a, *shape):
            n = int(np.prod(shape))
            v = arena[:, a:a + n]
            if len(shape) == 2:
                return v.rearrange("p (a b) -> p a b", a=shape[0])
            if len(shape) == 3:
                return v.rearrange("p (a b c) -> p a b c", a=shape[0], b=shape[1])
            return v

        tiles = []
        landings = [0] * RAW

        def tile(kts, cols, loads):
            n = len(tiles)
            landings[n % RAW] += 16 * len(loads)
            tiles.append(Tile(n, kts, cols, loads, landings[n % RAW]))
            return tiles[-1]

        def product(w, inner, cols, block=512):
            kts = inner // P
            blocks = []
            for c in range(0, cols, block):
                n = min(block, cols - c)
                most = min(kts, TILE // n)
                mine = []
                for k in range(0, kts, most):
                    m = min(most, kts - k)
                    src = w[k * P:(k + m) * P, c:c + n].rearrange("(k p) n -> p k n", p=P)
                    mine.append(tile(m, n, [(0, n, src)]))
                blocks.append(Block(c, n, mine))
            return blocks

        class FeedForward:

            def __init__(self, w1, w3, w2):
                self.up_src = [w.rearrange("(k p) n -> p k n", p=P) for w in (w1, w3)]
                self.down_src = w2.rearrange("(j k p) n -> j k p n", k=2, p=P)
                self.n0 = len(tiles)
                self.tiles = [tile(2, 512, [None, None]) for _ in range(FFN_TILES * FFN_STEPS)]

            def up(self, i, col):
                return [(GLU * h, GLU, w[:, 2 * i:2 * i + 2, col]) for h, w in enumerate(self.up_src)]

        FFN = {}
        G = {}
        vecs = []
        vec_at = {}
        order = []

        def plan_product(name, blocks):
            G[name] = blocks
            for b in blocks:
                order.extend(("tile", t) for t in b.tiles)

        def plan_vec(name, src):
            vec_at[name] = len(vecs)
            order.append(("vec", len(vecs)))
            vecs.append(src)

        for i in range(6):
            plan_vec(f"b_mod{i}", I["b_mod"][0:1, i * D:(i + 1) * D])
            plan_product(f"mod{i}", product(I["w_mod"][0][:, i * D:(i + 1) * D], D, D))
            if i == 1:
                plan_vec("g_pre_mix", I["g_pre_mix"])
        plan_product("in1", product(I["w_in"][0], D, IN1))
        for name in ("g_post_mix", "g_pre_ffn", "g_post_ffn"):
            plan_vec(name, I[name])
        plan_product("out1", product(I["w_out"][0], D, D))
        plan_product("router", product(I["router_w"][0], D, N_EXP))
        moe_at = len(tiles)
        order.append(("moe", None))

        def plan_ffn(name, w1, w3, w2):
            FFN[name] = FeedForward(w1, w3, w2)
            order.append(("ffn", FFN[name]))

        def plan_ln(n):
            plan_vec(f"ln{n}_g", I[f"ln{n}_g_2"])
            plan_vec(f"ln{n}_b", I[f"ln{n}_b_2"])

        plan_ffn("f1", I["ffn1_w1_2"][0], I["ffn1_w3_2"][0], I["ffn1_w2_2"][0])
        plan_ln(1)
        plan_product("in2", product(I["w_in_2"][0], D, IN2))
        for i in range(2):
            plan_vec(f"b_gate2_{i}", I["b_gate_2"][0:1, i * D:(i + 1) * D])
        plan_product("gate2", product(I["w_gate_2"][0], D, 2 * D))
        plan_product("q_b", product(I["w_q_b_2"][0], 384, MLA_H * MLA_QK))
        plan_product("kv_b", product(I["w_kv_b_2"][0], 256, D))
        plan_product("up_mla", product(I["w_up_mla_2"][0], 512, D))
        plan_product("up_diff", product(I["w_up_diff_2"][0], 512, D))
        plan_product("o2", product(I["w_o_2"][0], D, D))
        order.append(("mem", None))
        plan_ln(2)
        plan_product("mem_q", product(I["mem_w_q_2"][0], D, D))
        plan_product("mem_kv", product(I["mem_w_kv_2"][0], D, 2 * D))
        plan_product("mem_o", product(I["mem_w_o_2"][0], D, D))
        plan_ln(3)
        plan_ffn("f2", I["ffn2_w1_2"][0], I["ffn2_w3_2"][0], I["ffn2_w2_2"][0])
        plan_ln(4)
        plan_vec("ffn1_norm", I["ffn1_norm_3"])
        plan_ffn("f3", I["ffn1_w_gu_3"][0][:, 0:F_FFN], I["ffn1_w_gu_3"][0][:, F_FFN:2 * F_FFN], I["ffn1_w_down_3"][0])
        plan_vec("mix_norm", I["mix_norm_3"])
        for i in range(2):
            plan_vec(f"b_gate3_{i}", I["b_gate_3"][0:1, i * D:(i + 1) * D])
        plan_product("in3", product(I["w_in_3"][0], D, IN3))
        plan_product("br_dsa", product(I["w_branch_dsa_3"][0], 512, D))
        plan_product("br_moba", product(I["w_branch_moba_3"][0], 512, D))
        plan_product("out3", product(I["w_out_3"][0], D, D))
        plan_vec("ffn2_norm", I["ffn2_norm_3"])
        plan_ffn("f4", I["ffn2_w_gu_3"][0][:, 0:F_FFN], I["ffn2_w_gu_3"][0][:, F_FFN:2 * F_FFN], I["ffn2_w_down_3"][0])

        raw_landed = [sem(f"raw_landed{i}") for i in range(RAW)]
        hi_done = sem("hi_done")
        lo_done = sem("lo_done")
        tile_used = sem("tile_used")
        unit_done = sem("unit_done")
        unit_read = sem("unit_read")
        turned = sem("turned")
        turned_read = sem("turned_read")
        rows_turned = sem("rows_turned")
        rows_hi = sem("rows_hi")
        rows_read = sem("rows_read")
        att_shifted = sem("att_shifted")
        att_exp = sem("att_exp")
        out_done = sem("out_done")
        out_read = sem("out_read")
        pow_in = sem("pow_in")
        pow_out = sem("pow_out")
        vec_landed = [sem(f"vec_landed{i}") for i in range(VECS)]
        vec_used = sem("vec_used")
        stat_in = sem("stat_in")
        stat_out = sem("stat_out")
        E = sem

        MOD = [MIX[:, 0, :], MIX[:, 1, :]] + [arena_at(D * i, D) for i in range(4)]
        PROJ1 = arena_at(4 * D, TT, IN1)
        PROJ2 = arena_at(0, TT, IN2)
        GATE2 = arena_at(4416, TT, 2 * D)
        KV = arena_at(8512, TT, D)
        QM = H[:, :, 0:MLA_H * MLA_QK]
        KVM = arena_at(0, TT, 2 * D)
        QMEM = arena_at(4096, TT, D)
        PROJ3 = arena_at(0, TT, IN3)
        SEL = H[:, :, 0:S]

        small_at = {}

        def small(name, n, src=None):
            if name not in small_at:
                a = sum(m for _, m, _ in small_at.values())
                small_at[name] = (a, n, src)
            a, n, _ = small_at[name]
            return SMALL[:, a:a + n]

        for name, n in (("g_gla", 128), ("b_gate", 256), ("q_norm_g_2", 384), ("kv_norm_g_2", 256), ("lam_q1_2", 64),
                        ("lam_k1_2", 64), ("lam_q2_2", 64), ("lam_k2_2", 64), ("diff_norm_g_2", 128),
                        ("q_norm_dsa_3", 64), ("k_norm_dsa_3", 64), ("q_norm_moba_3", 64), ("k_norm_moba_3", 64),
                        ("router_b", 32)):
            small(name, n, I[name])

        class Attention:

            def __init__(self, heads, scale, q, k, v, dv, bias, put, causal=True, extra=None, step=2):
                self.heads, self.scale, self.q, self.k, self.v, self.dv = heads, scale, q, k, v, dv
                self.bias, self.put, self.causal, self.extra = bias, put, causal, extra
                self.step = step
                self.units = [(h, tt) for h in range(heads) if h % (2 * step) < step for tt in range(TT)]

            def keys(self, tt):
                return P * (tt + 1) if self.causal else S

        def pair_t(t, base, h):
            r = HD * (h % 2)
            return [t[r:r + HD, base + h // 2, :]]

        def row_mask(name):
            def f(h, tt):
                m = tab(name)[:, P:S] if tt == 0 else tab(name)
                n = P * (tt + 1)
                return m.unsqueeze(1).to_broadcast([P, 2, n])
            return f

        def head_bias(h, tt):
            return BIAS[:, h:h + 3:2, P:S] if tt == 0 else BIAS[:, h:h + 3:2, :]

        def into(buf, base, dv, heads, step=2):
            return lambda h, tt: (buf[:, tt, base:base + heads * dv].rearrange("p (h e) -> p h e", h=heads)
                                  [:, h:h + step + 1:step, :])

        A_DIL = Attention(8, HD ** -0.5, lambda h: pair_t(QT, 0, h), lambda h: pair_t(QT, 4, h),
                          lambda h, t: PROJ1[:, t, 1024 + HD * h:1024 + HD * (h + 1)], HD, row_mask("lnc"), into(MIX, 0, HD, 8))
        A_MLA = Attention(8, MLA_QK ** -0.5, lambda h: [QT[0:MLA_QK, h, :]], lambda h: [KT[0:MLA_QK, h, :]],
                          lambda h, t: KV[:, t, P * h + MLA_NOPE:P * (h + 1)], HD, row_mask("causal"), into(MIX, 0, HD, 8, 1),
                          step=1)
        OD8 = Y
        A_DIFF = Attention(8, HD ** -0.5, lambda h: pair_t(QT, 0, h), lambda h: pair_t(QT, 4, h),
                           lambda h, t: PROJ2[:, t, 1696 + P * (h // 2):1696 + P * (h // 2 + 1)], P, head_bias, into(OD8, 0, P, 8))
        A_MEM = Attention(4, 256 ** -0.5, lambda h: [QT[:, 2 * h, :], QT[:, 2 * h + 1, :]],
                          lambda h: [KT[:, 2 * h, :], KT[:, 2 * h + 1, :]],
                          lambda h, t: KVM[:, t, D + 256 * h:D + 256 * (h + 1)], 256, None, into(MIX, 0, 256, 4, 1), causal=False,
                          step=1)
        A_DSA = Attention(8, HD ** -0.5, lambda h: pair_t(QT, 0, h), lambda h: pair_t(QT, 4, h),
                          lambda h, t: PROJ3[:, t, 1024 + HD * h:1024 + HD * (h + 1)], HD, head_bias, into(MIX, 0, HD, 8),
                          extra=lambda tt: SEL[:, tt, 0:P * (tt + 1)].unsqueeze(1).to_broadcast([P, 2, P * (tt + 1)]))
        A_MOBA = Attention(8, HD ** -0.5, lambda h: pair_t(KT, 0, h), lambda h: pair_t(KT, 4, h),
                           lambda h, t: PROJ3[:, t, 2560 + HD * h:2560 + HD * (h + 1)], HD, head_bias, into(MIX, 512, HD, 8))

        LA = QT[:, 0:2, :]
        GB = QT[:, 2:6, :].rearrange("p (t a) b -> p t (a b)", t=2)
        QKD = H[:, :, 0:512]
        KL = H[:, :, 512:768]
        GT = KT[:, 2:6, :]
        ATTM = PR[:, 0:2, :]
        STATE = PT[:, :, :].rearrange("p a b -> p (a b)").rearrange("p (n m e) -> p n m e", n=4, m=2)
        OG = Y[:, :, 0:512]
        SR = Y[:, :, 512:1024]
        AN = MISC[:, 0:8].rearrange("p (m n) -> p m n", m=2)
        GLRT = QT[0:16, 6, :]

        MO = 4 * D
        XETh, XETl = HTh[:, :, 0:CAP], HTl[:, :, 0:CAP]
        AVTh, AVTl = HTh[:, :, CAP:2 * CAP], HTl[:, :, CAP:2 * CAP]
        GU = arena_at(MO, 2 * F_MOE)
        GL = arena_at(MO + 2048, F_MOE)
        SG = arena_at(MO + 3072, F_MOE)
        AV = arena_at(MO + 4096, F_MOE)
        OUTE = Y[:, 1, :]
        PSEL = QT[:, 0, :].rearrange("p (t c) -> p t c", t=2)
        GSEL = QT[:, 1, :].rearrange("p (t c) -> p t c", t=2)
        GSELT = QT[:, 2, :]
        BROW = BIAS[0:1, :, :].rearrange("p a b -> p (a b)")
        BB = MIX[:, :, :].rearrange("p a b -> p (a b)")
        MASKS = QT[:, 3, 0:64].rearrange("p (t e) -> p t e", t=2)
        GATES = QT[:, 3, 64:128].rearrange("p (t e) -> p t e", t=2)
        POS = [QT[:, 3, 128 + 40 * t:128 + 40 * t + N_EXP + 1] for t in range(TT)]
        RT = QT[:, 4, 0:64].rearrange("p (t e) -> p t e", t=2)
        GATET = QT[0:32, 5, :]
        TMP32 = QT[:, 4, 64:96]
        BDOWN = KT[0:32, 0:4, :].rearrange("p a b -> p (a b)")
        glu_in = GU.rearrange("p (f two) -> p f two", two=2)

        BUCK = KT[0:32, 2:5, :].rearrange("p a b -> p (a b)")
        SMALLB = KT[0:32, 5, 0:24]
        RELS = KT[0:24, 6:8, :].rearrange("p a b -> p (a b)")[:, 0:384]
        CCOL = MISC[:, 0:8]
        FA = arena_at(0, TT, GLU)
        KM = Y
        KI2 = PT[:, :, 0:P]
        SQ = PR[:, :, :].rearrange("p a b -> p (a b)")[:, 0:D]

        m_landed = [sem(f"moe_landed{i}") for i in range(MOE_RAW)]
        m_hi = sem("moe_hi")
        m_lo = [sem("moe_lo_vector"), sem("moe_lo_pool")]
        m_used = sem("moe_tile_used")
        m_up_read = sem("moe_up_read")
        m_down_read = sem("moe_down_read")
        m_sel = sem("moe_sel")
        m_gather = sem("moe_gather")
        m_xhi = sem("moe_x_hi")
        m_xlo = sem("moe_x_lo")
        m_gt = sem("moe_gate_turned")
        m_gtc = sem("moe_gate_copied")
        m_glu = sem("moe_glu")
        m_sig = sem("moe_sigmoid")
        m_act = sem("moe_act")
        m_tr = sem("moe_act_turned")
        m_ahi = sem("moe_act_hi")
        m_alo = sem("moe_act_lo")
        m_brow = sem("moe_bias_row")
        m_bias = sem("moe_bias")
        m_pass = sem("moe_pass")
        m_chain = sem("moe_dve_step")
        M_STEPS = 4
        pool_tile = lambda t: t in POOL_TILES
        lo_per = [sum(not pool_tile(t) for t in range(MOE_TILES)), sum(pool_tile(t) for t in range(MOE_TILES))]

        def moe_raw(t):
            i = t % MOE_RAW
            return raw[:, i, :] if i < RAW else arena_at((0, D, 2 * D, MO + 5 * F_MOE)[i - RAW], TILE)

        def moe_lo(it, t):
            back, t = (1, t + MOE_TILES) if t < 0 else (0, t)
            e = int(pool_tile(t))
            nth = sum(pool_tile(i) == pool_tile(t) for i in range(t + 1))
            return m_lo[e], it * lo_per[e] + (1 - back) * lo_per[e] + nth

        def moe_used(it, t):
            return it * MOE_TILES + MOE_TILES + t + 1

        block = ctx.enter_context(nc.Block())
        pow_widths = []
        pows_before = []
        group_of = []

        @block.tensor
        def _(pe):
            unit = [0]
            group = [0]
            outs = [0]
            rows = [0]
            att = [0]

            def three(acc, xh, xl, wh, wl, start, stop):
                pe.matmul(acc, xh, wh, start=start, stop=False)
                pe.matmul(acc, xh, wl, start=False, stop=False)
                return pe.matmul(acc, xl, wh, start=False, stop=stop)

            def parts(n, j, cols):
                c = slice(j * cols, (j + 1) * cols)
                return w_hi[:, n % PARTS, c], w_lo[:, n % PARTS, c]

            def gemm(name, tts=TT, kt0=0):
                for b in G[name]:
                    kt_all = sum(t.kts for t in b.tiles)
                    kt = 0
                    for t in b.tiles:
                        pe.wait_ge(lo_done, t.n + 1)
                        for tt in range(tts):
                            u = unit[0] + tt
                            if kt == 0 and u >= GEMM_BANKS:
                                pe.wait_ge(unit_read, u - GEMM_BANKS + 1)
                            c = slice(tt * P, (tt + 1) * P)
                            for j in range(t.kts):
                                k = kt + j + kt0
                                mm = three(bank[u % GEMM_BANKS][:, 0:t.cols], HTh[:, k, c], HTl[:, k, c],
                                           *parts(t.n, j, t.cols), kt + j == 0, kt + j == kt_all - 1)
                        mm.then_inc(tile_used, 1)
                        kt += t.kts
                    unit[0] += tts

            def turn(tiles):
                for i in range(0, len(tiles), 4):
                    g = group[0]
                    if g >= 2:
                        pe.wait_ge(turned_read, g - 1)
                    for j, src in enumerate(tiles[i:i + 4]):
                        w = src.shape[1]
                        mm = pe.transpose(bank[4 + g % 2][0:w, P * j:P * (j + 1)], src, ident)
                    mm.then_inc(turned, 1)
                    group[0] += 1

            def turned_all():
                pe.wait_ge(turned_read, group[0])

            def turn_rows(buf, base=0, n=KD):
                turn([buf[:, tt, base + P * k:base + P * (k + 1)] for tt in range(TT) for k in range(n)])
                turned_all()

            def turn_split(srcs, last=True):
                for i in range(0, len(srcs), 4):
                    g = rows[0]
                    if g >= 2:
                        pe.wait_ge(rows_read, g - 1)
                    for j, src in enumerate(srcs[i:i + 4]):
                        mm = pe.transpose(bank[4 + g % 2][:, P * j:P * (j + 1)], src, ident)
                    mm.then_inc(rows_turned, 1)
                    rows[0] += 1
                if last:
                    pe.wait_ge(rows_read, rows[0])

            def split_rows(buf, ready=None):
                for tt in range(TT):
                    if ready is not None:
                        pe.wait_ge(E(ready), tt + 1)
                    turn_split([buf[:, tt, P * k:P * (k + 1)] for k in range(KD)], tt == TT - 1)

            def next_unit():
                u = unit[0]
                if u >= GEMM_BANKS:
                    pe.wait_ge(unit_read, u - GEMM_BANKS + 1)
                unit[0] += 1
                return bank[u % GEMM_BANKS]

            def attend(a):
                n = len(a.units)

                def scores(i):
                    h, tt = a.units[i]
                    nk = a.keys(tt)
                    b = next_unit()
                    for hh in range(2):
                        qs, ks = a.q(h + a.step * hh), a.k(h + a.step * hh)
                        for j in range(len(qs)):
                            mm = pe.matmul(b[:, hh * nk:(hh + 1) * nk], qs[j][:, tt * P:(tt + 1) * P], ks[j][:, 0:nk],
                                           start=(j == 0), stop=(j == len(qs) - 1))
                    mm.then_inc(unit_done, 1)

                def turn_probs(i):
                    h, tt = a.units[i]
                    nk = a.keys(tt)
                    k = att[0] + i
                    pe.wait_ge(att_exp, k + 1)
                    p = PR[:, k % 3, 0:2 * nk]
                    group_of.append(group[0])
                    turn([p[:, P * j:P * (j + 1)] for j in range(2 * nk // P)])

                def values(i):
                    h, tt = a.units[i]
                    nk = a.keys(tt)
                    k = att[0] + i
                    pe.wait_ge(turned_read, group_of[k] + 1)
                    o = outs[0]
                    if o >= 2:
                        pe.wait_ge(out_read, o - 1)
                    for hh in range(2):
                        for t in range(nk // P):
                            j = hh * (nk // P) + t
                            mm = pe.matmul(bank[6 + o % 2][:, hh * a.dv:(hh + 1) * a.dv], PT[:, k % 2, P * j:P * (j + 1)],
                                           a.v(h + a.step * hh, t), start=(t == 0), stop=(t == nk // P - 1))
                    mm.then_inc(out_done, 1)
                    outs[0] += 1

                for i in range(n + LOOKAHEAD + 1):
                    if i < n:
                        scores(i)
                    if LOOKAHEAD <= i < n + LOOKAHEAD:
                        turn_probs(i - LOOKAHEAD)
                    if i > LOOKAHEAD:
                        values(i - LOOKAHEAD - 1)
                att[0] += n

            pe.wait_ge(E("c_spread"), 1)
            for i in range(6):
                gemm(f"mod{i}", tts=1)
            pe.wait_ge(E("setup"), 16 * 4)
            b = next_unit()
            pe.matmul(b[0:24, 0:384], SMALLB[:, 0:24], BUCK[:, 0:384], start=True, stop=True).then_inc(unit_done, 1)
            split_rows(H, "h1")
            gemm("in1")
            pe.wait_ge(E("rope1"), 1)
            turn_rows(Y)
            attend(A_DIL)
            pe.wait_ge(E("dil_out"), 1)
            turn([PROJ1[:, tt, 3072:3088] for tt in range(TT)])
            turned_all()
            pe.wait_ge(E("gate_lr"), 16)
            b = next_unit()
            for tt in range(TT):
                mm = pe.matmul(b[:, 256 * tt:256 * (tt + 1)], GLRT[:, tt * P:(tt + 1) * P], WGLR[:, :], start=True, stop=True)
            mm.then_inc(unit_done, 1)
            pe.wait_ge(E("log_a"), 1)
            for tt in range(TT):
                b = next_unit()
                pe.matmul(b[:, 0:256], tab("upto"), LA[:, tt, :], start=True, stop=True)
                pe.matmul(b[:, 256:512], tab("same"), LA[:, tt, :], start=True, stop=True).then_inc(unit_done, 1)
            b = next_unit()
            for m in range(2):
                for tt in range(TT):
                    mm = pe.matmul(b[:, 4 * m + 2 * tt:4 * m + 2 * tt + 2], LA[:, tt, m * P:(m + 1) * P], tab("chunk"),
                                   start=True, stop=True)
            mm.then_inc(unit_done, 1)
            pe.wait_ge(E("gla_qk"), 1)
            turn([QKD[:, tt, P * k:P * (k + 1)] for tt in range(TT) for k in range(4)])
            turned_all()
            for tt in range(TT):
                for par in range(2):
                    b = next_unit()
                    r = HD * par
                    for m in range(2):
                        mm = pe.matmul(b[:, P * m:P * (m + 1)], GT[r:r + HD, 2 + m, tt * P:(tt + 1) * P],
                                       GT[r:r + HD, m, tt * P:(tt + 1) * P], start=True, stop=True)
                    mm.then_inc(unit_done, 1)
            for some in ((0, 2), (1,)):
                b = next_unit()
                for c in some:
                    tt, r = c // 2, HD * (c % 2)
                    for h in range(4):
                        o = HD * (h % 2)
                        mm = pe.matmul(b[o:o + HD, 256 * tt + P * (h // 2):256 * tt + P * (h // 2 + 1)],
                                       KL[r:r + HD, tt, HD * h:HD * (h + 1)],
                                       PROJ1[r:r + HD, tt, 2048 + P * h:2048 + P * (h + 1)], start=True, stop=True)
                mm.then_inc(unit_done, 1)
            pe.wait_ge(E("gla_state"), 1)
            for tt in range(TT):
                b = next_unit()
                for h in range(4):
                    mm = pe.matmul(b[:, P * h:P * (h + 1)], ATTM[:, tt, P * h:P * (h + 1)],
                                   PROJ1[:, tt, 2048 + P * h:2048 + P * (h + 1)], start=True, stop=True)
                mm.then_inc(unit_done, 1)
                for par in range(2):
                    b = next_unit()
                    r = HD * par
                    for c in range(2):
                        n = 2 * tt + c
                        for m in range(2):
                            mm = pe.matmul(b[HD * c:HD * (c + 1), P * m:P * (m + 1)], GT[r:r + HD, m, n * HD:(n + 1) * HD],
                                           STATE[r:r + HD, n, m, :], start=True, stop=True)
                    mm.then_inc(unit_done, 1)
            split_rows(MIX, "mix1")
            gemm("out1")
            split_rows(H, "h2")
            gemm("router")
            pe.wait_ge(E("routed"), 1)
            b = next_unit()
            pe.matmul(b[:, 0:32], tab("before"), MASKS[:, 0, :], start=True, stop=True)
            pe.matmul(b[:, 32:64], tab("ones"), MASKS[:, 0, :], start=True, stop=False)
            pe.matmul(b[:, 32:64], tab("before"), MASKS[:, 1, :], start=False, stop=True)
            pe.matmul(b[:, 64:96], tab("ones"), MASKS[:, 0, :], start=True, stop=False)
            pe.matmul(b[:, 64:96], tab("ones"), MASKS[:, 1, :], start=False, stop=True).then_inc(unit_done, 1)
            turn([GATES[:, tt, :] for tt in range(TT)])
            turned_all()
            pe.wait_ge(unit_read, unit[0])
            pe.wait_ge(E("b_down"), 16)
            for tt in range(TT):
                for n in range(2):
                    pe.matmul(bank[2 * tt + n][:, :], GATET[:, tt * P:(tt + 1) * P], BDOWN[:, 512 * n:512 * (n + 1)],
                              start=True, stop=False, skip_group_check=True)

            def zero_bank(b, start, stop):
                for i in range(4):
                    mm = pe.matmul(b[:, P * i:P * (i + 1)], ZERO[:, :], ZERO[:, :], start=start, stop=stop, skip_group_check=True)
                return mm

            def gather(half, done):
                pe.wait_ge(m_sel, done)
                for k in range(4):
                    for tt in range(TT):
                        kk = 4 * half + k
                        mm = pe.matmul(bank[6 + half][:, P * k:P * (k + 1)], H[:, tt, P * kk:P * (kk + 1)],
                                       PSEL[:, tt, :], start=(tt == 0), stop=(tt == TT - 1))
                mm.then_inc(m_gather, 1)

            def scatter():
                for tt in range(TT):
                    for n in range(2):
                        mm = pe.matmul(bank[2 * tt + n][:, :], GSELT[:, tt * P:(tt + 1) * P],
                                       OUTE[:, 512 * n:512 * (n + 1)], start=False, stop=False, skip_group_check=True)
                return mm

            pe.wait_ge(E("zeroed"), 1)
            zero_bank(bank[5], True, True).then_inc(E("moe_begun"), 1)
            for half in (1, 0):
                gather(half, 1)
            pe.sem_inc(m_used, MOE_TILES)
            pe.wait_ge(E("moe_zero"), 1)
            pe.wait_ge(E("n_pass"), 1)
            n_pass = pe.value_load(NPASS[0:1, 0:1], min_val=1, max_val=2)
            with pe.Fori(0, n_pass) as ps:
                with pe.Fori(0, N_EXP) as ex:
                    it = ps * N_EXP + ex

                    def moe_tiles(first, last, xh, xl):
                        for t in range(first, last):
                            b, i = t // 4, t % 4
                            pe.wait_ge(*moe_lo(it, t))
                            for j in range(2):
                                k = 2 * i + j
                                mm = three(bank[4 + b % 2][:, :], xh[:, k, :], xl[:, k, :], *parts(t, j, 512), k == 0, k == KD - 1)
                            mm.then_inc(m_used, 1)

                    def turn_act(half):
                        pe.wait_ge(m_act, it * 2 + half + 1)
                        for k in range(4):
                            kk = 4 * half + k
                            mm = pe.transpose(bank[6 + half][:, P * k:P * (k + 1)], AV[:, P * kk:P * (kk + 1)], ident)
                        mm.then_inc(m_tr, 1)

                    pe.wait_ge(m_xlo, it * 2 + 2)
                    pe.wait_ge(m_down_read, it * 2 + 2)
                    moe_tiles(0, 4, XETh, XETl)
                    pe.wait_ge(m_down_read, it * 2 + 3)
                    moe_tiles(4, 8, XETh, XETl)
                    pe.wait_ge(m_up_read, it * 4 + 5)
                    moe_tiles(8, 12, XETh, XETl)
                    pe.wait_ge(m_up_read, it * 4 + 6)
                    moe_tiles(12, 16, XETh, XETl)
                    turn_act(0)
                    gather(1, it + 2)
                    pe.wait_ge(m_gtc, it + 1)
                    scatter()
                    pe.wait_ge(m_up_read, it * 4 + 8)
                    for tt in range(TT):
                        mm = pe.transpose(bank[5][:, P * tt:P * (tt + 1)], GSEL[:, tt, :], ident)
                    mm.then_inc(m_gt, 1)
                    pe.wait_ge(m_alo, it * 2 + 1)
                    pe.wait_ge(m_up_read, it * 4 + 7)
                    moe_tiles(16, 18, AVTh, AVTl)
                    pe.wait_ge(m_xlo, it * 2 + 3)
                    turn_act(1)
                    gather(0, it + 2)
                    pe.wait_ge(m_alo, it * 2 + 2)
                    moe_tiles(18, 20, AVTh, AVTl)
                    pe.wait_ge(m_gtc, it + 2)
                    moe_tiles(20, 24, AVTh, AVTl)
            pe.wait_ge(m_down_read, n_pass * (2 * N_EXP) + 3)
            pe.wait_ge(m_gtc, n_pass * N_EXP + 1)
            scatter()
            for i in range(4):
                mm = zero_bank(bank[i], False, True)
            mm.then_inc(E("moe_over"), 1)

            def ffn(name, src, ready):
                f = FFN[name]
                split_rows(src, ready)
                if name == "f1":
                    pe.wait_ge(E("moe_sum"), 1)
                u = unit[0]
                pe.wait_ge(unit_read, u)
                for i in range(4):
                    zero_bank(bank[(u + i) % GEMM_BANKS], True, False)
                acted, turned_f, read_f = E(name + "_acted"), E(name + "_turned"), E(name + "_turned_lo")

                def up(n, pair):
                    for i in range(4):
                        pe.wait_ge(lo_done, pair * (2 * FFN_TILES) + n + i + 1)
                        for tt in range(TT):
                            c = slice(tt * P, (tt + 1) * P)
                            for j in range(2):
                                k = 2 * i + j
                                mm = three(bank[6 + tt][:, :], HTh[:, k, c], HTl[:, k, c], *parts(n + i, j, 512),
                                           k == 0, k == KD - 1)
                        mm.then_inc(tile_used, 1)

                def turn_act(jj):
                    pe.wait_ge(acted, jj * TT + TT)
                    for k in range(2):
                        for tt in range(TT):
                            mm = pe.transpose(bank[5][:, S * k + P * tt:S * k + P * (tt + 1)], FA[:, tt, P * k:P * (k + 1)], ident)
                    mm.then_inc(turned_f, 1)

                def down(n, pair, two):
                    last = pair is None
                    pe.wait_ge(read_f, FFN_STEPS if last else pair * 2 + two + 1)
                    for i in range(2):
                        pe.wait_ge(lo_done, n + i + 1 if last else pair * (2 * FFN_TILES) + n + i + 1)
                        for tt in range(TT):
                            c = slice(tt * P, (tt + 1) * P)
                            for k in range(2):
                                wh, wl = parts(n + i, k, 512)
                                acc = bank[(u + 2 * tt + i) % GEMM_BANKS][:, :]
                                pe.matmul(acc, AFTh[:, k, c], wh, start=False, stop=False, skip_group_check=True)
                                pe.matmul(acc, AFTh[:, k, c], wl, start=False, stop=False, skip_group_check=True)
                                mm = pe.matmul(acc, AFTl[:, k, c], wh, start=False, stop=last and k == 1, skip_group_check=True)
                        mm.then_inc(tile_used, 1)

                up(f.n0, 0)
                with pe.Fori(0, FFN_PAIRS) as pair:
                    for two in range(2):
                        turn_act(pair * 2 + two)
                        up(f.n0 + 4 + FFN_TILES * two, pair)
                        down(f.n0 + 8 + FFN_TILES * two, pair, two)
                turn_act(FFN_STEPS - 1)
                down(f.n0 + 4 + FFN_TILES * (FFN_STEPS - 1), None, None)
                unit[0] += 4

            ffn("f1", X, "x1")
            split_rows(X, "ln1")
            gemm("in2")
            gemm("gate2")
            pe.wait_ge(E("c_norm"), 1)
            turn_split([PROJ2[:, tt, P * k:P * (k + 1)] for k in range(5) for tt in range(TT)])
            gemm("q_b")
            gemm("kv_b", kt0=3)
            pe.wait_ge(E("mla_qk"), 1)
            turn([QM[:, tt, MLA_QK * h:MLA_QK * (h + 1)] for tt in range(TT) for h in range(MLA_H)])
            turn([KM[:, tt, MLA_QK * h:MLA_QK * (h + 1)] for tt in range(TT) for h in range(MLA_H)])
            turned_all()
            attend(A_MLA)
            turn_rows(PROJ2, base=672)
            pe.wait_ge(E("bias2"), 16)
            attend(A_DIFF)
            pe.wait_ge(E("mix2"), 1)
            split_rows(MIX)
            gemm("up_mla")
            gemm("up_diff", kt0=4)
            pe.wait_ge(E("gated2"), 1)
            split_rows(MIX)
            gemm("o2")
            split_rows(X, "ln2")
            gemm("mem_q")
            pe.wait_ge(E("mem_in"), 16)
            split_rows(H)
            gemm("mem_kv")
            pe.wait_ge(E("mem_qkv"), 1)
            turn_rows(QMEM)
            turn_rows(KVM)
            attend(A_MEM)
            pe.wait_ge(E("mem_out"), 1)
            split_rows(MIX)
            gemm("mem_o")
            ffn("f2", X, "ln3")
            ffn("f3", H, "h3")
            split_rows(H, "h4")
            gemm("in3")
            pe.wait_ge(E("qk3"), 1)
            turn([PROJ3[:, tt, 3072 + P * k:3072 + P * (k + 1)] for k in range(2) for tt in range(TT)])
            turn([KI2[:, tt, :] for tt in range(TT)])
            turned_all()
            for tt in range(TT):
                nk = P * (tt + 1)
                for par in range(2):
                    b = next_unit()
                    r = HD * par
                    for hh in range(2):
                        mm = pe.matmul(b[:, hh * nk:(hh + 1) * nk], QT[r:r + HD, hh, tt * P:(tt + 1) * P],
                                       QT[r:r + HD, 2, 0:nk], start=True, stop=True)
                    mm.then_inc(unit_done, 1)
            turn_rows(PROJ3)
            turn_rows(PROJ3, base=1536)
            attend(A_MOBA)
            attend(A_DSA)
            pe.wait_ge(E("mix3"), 1)
            split_rows(MIX)
            gemm("br_dsa")
            gemm("br_moba", kt0=4)
            pe.wait_ge(E("gated3"), 1)
            split_rows(MIX)
            gemm("out3")
            ffn("f4", H, "h5")


        @block.vector
        def _(dve):
            steps = [0]
            units = [0]
            alone = [0]
            split = [0]
            rows = [0]
            outs = [0]
            vec_done = [0]
            att = [0]
            chain = sem("dve_step")

            def step(ins):
                steps[0] += 1
                ins.then_inc(chain, 1)
                dve.wait_ge(chain, steps[0])

            def mark(ins, name):
                ins.then_inc(E(name), 1)
                dve.wait_ge(E(name), 1)

            def signal(name):
                dve.sem_inc(E(name), 1)

            def unit():
                alone[0] += 1
                dve.wait_ge(unit_done, alone[0])
                units[0] += 1
                return bank[(units[0] - 1) % GEMM_BANKS]

            def low(n, hi_count):
                m = tiles[n].kts * tiles[n].cols
                dve.wait_ge(hi_done, hi_count)
                dve.tensor_tensor(w_lo[:, n % PARTS, 0:m], raw[:, n % RAW, 0:m], w_hi[:, n % PARTS, 0:m].bitcast(F32),
                                  ALU.subtract).then_inc(lo_done, 1)

            def split_to(n):
                for i in range(split[0], n):
                    low(i, i + 1)
                split[0] = max(split[0], n)

            def ahead(n):
                split_to(min(n + LOW_AHEAD, moe_at if n <= moe_at else len(tiles)))

            def gemm(name, put, tts=TT, then={}, done=lambda tt: None):
                def read(b):
                    dve.wait_ge(tile_used, b.tiles[-1].n + 1)
                    for tt in range(tts):
                        units[0] += 1
                        put(bank[(units[0] - 1) % GEMM_BANKS][:, 0:b.cols], tt, b)
                        if b is G[name][-1]:
                            done(tt)
                    then.get(G[name].index(b), lambda: None)()
                last = None
                for b in G[name]:
                    split_to(b.tiles[-1].n + 1)
                    if last is not None:
                        read(last)
                    last = b
                read(last)
                ahead(last.tiles[-1].n + 1)

            def rows_lo(dsts):
                for lo, hi in dsts:
                    g = rows[0]
                    dve.wait_ge(rows_hi, g + 1)
                    n = hi.shape[1] * hi.shape[2]
                    src = bank[4 + g % 2][:, 0:n].rearrange("p (a b) -> p a b", a=hi.shape[1])
                    dve.tensor_tensor(lo, src, hi.bitcast(F32), ALU.subtract).then_inc(rows_read, 1)
                    rows[0] += 1

            def split_rows():
                rows_lo([(HTl[:, 4 * k:4 * k + 4, tt * P:(tt + 1) * P], HTh[:, 4 * k:4 * k + 4, tt * P:(tt + 1) * P])
                         for tt in range(TT) for k in range(2)])

            def release(ins):
                ins.then_inc(unit_read, 1)
                dve.wait_ge(unit_read, units[0])

            def vec(name):
                i = vec_at[name]
                dve.wait_ge(vec_landed[i % VECS], 16 * (i // VECS + 1))
                return VEC[:, i % VECS, :]

            def vec_over(name):
                assert vec_at[name] == vec_done[0], name
                vec_done[0] += 1
                dve.sem_inc(vec_used, 1)

            def rsqrt(src, scale, eps, n=1):
                k = len(pow_widths)
                pow_widths.append(n)
                dve.tensor_scalar(st_in[:, k % 2, 0:n], src, scale, eps, ALU.mult, ALU.add).then_inc(pow_in, 1)
                return k

            def rooted(k):
                dve.wait_ge(pow_out, k + 1)
                return st_out[:, k % 2, 0:pow_widths[k]]

            def square_sum(x, col):
                w = x.shape[1]
                step(dve.tensor_tensor_reduce(SQ[:, 0:w], x, x, 1.0, 0.0, ALU.mult, ALU.add, col))

            def rms_rows(rows):
                ks = []
                for i, (out, x, g, then) in enumerate(rows):
                    square_sum(x, SUMS[:, i, 0:1])
                    ks.append(rsqrt(SUMS[:, i, 0:1], 1.0 / x.shape[1], 1e-6))
                for k, (out, x, g, then) in zip(ks, rows):
                    step(dve.scalar_tensor_tensor(out, x, rooted(k), g, ALU.mult, ALU.mult))
                    then()

            def heads_roots(rows, heads, w):
                ks = []
                for i, x in enumerate(rows):
                    sq = SQ[:, 0:heads * w]
                    step(dve.tensor_tensor(sq, x, x, ALU.mult))
                    step(dve.tensor_reduce(SUMS[:, i, 0:heads], sq.rearrange("p (h e) -> p h e", h=heads), AX, ALU.add))
                    ks.append(rsqrt(SUMS[:, i, 0:heads], 1.0 / w, 1e-6, heads))
                return ks

            def heads_scaled(ks, rows, heads, w, g, scale=1.0):
                for k, x in zip(ks, rows):
                    x = x.rearrange("p (h e) -> p h e", h=heads)
                    rb = rooted(k).unsqueeze(2).to_broadcast([P, heads, w])
                    step(dve.scalar_tensor_tensor(x, x, scale, rb, ALU.mult, ALU.mult))
                    step(dve.tensor_tensor(x, x, g.unsqueeze(1).to_broadcast([P, heads, w]), ALU.mult))

            def rms_heads(rows, heads, w, g, scale=1.0):
                heads_scaled(heads_roots(rows, heads, w), rows, heads, w, g, scale)

            def copy_out(name, dst, tts=TT, then={}, done=lambda tt: None):
                gemm(name, lambda s, tt, b: release(dve.tensor_copy(dst(tt, b.col, b.cols), s)), tts, then, done)

            stats = [0]
            asked = [0]

            def ask(tt):
                asked[0] += 1
                dve.sem_inc(stat_in, 1)

            def stat():
                stats[0] += 1
                dve.wait_ge(stat_out, stats[0])
                return STATS[:, (stats[0] - 1) % 8:(stats[0] - 1) % 8 + 1]

            def roots_of_stats(eps):
                return [rsqrt(stat(), 1.0 / D, eps) for tt in range(TT)]

            def layer_norm(n, after=lambda tt: None):
                g, b = vec(f"ln{n}_g"), vec(f"ln{n}_b")
                for tt in range(TT):
                    step(dve.tensor_scalar(NEG_MEAN[:, tt:tt + 1], stat(), -1.0 / D, None, ALU.mult))
                    ask(tt)
                ks = roots_of_stats(1e-5)
                for tt in range(TT):
                    x = X[:, tt, :]
                    step(dve.scalar_tensor_tensor(x, x, NEG_MEAN[:, tt:tt + 1], g, ALU.add, ALU.mult))
                    step(dve.scalar_tensor_tensor(x, x, rooted(ks[tt]), b, ALU.mult, ALU.add))
                    signal(f"ln{n}")
                    after(tt)
                vec_over(f"ln{n}_g")
                vec_over(f"ln{n}_b")

            def alpha_x():
                for tt in range(TT):
                    step(dve.tensor_scalar(X[:, tt, :], X[:, tt, :], ALPHA, None, ALU.mult))

            def onto_x(scale):
                def put(s, tt, b):
                    x = X[:, tt, b.col:b.col + b.cols]
                    release(dve.scalar_tensor_tensor(x, s, scale, x, ALU.mult, ALU.add))
                return put

            def ffn(name, put, alpha=False, done=lambda tt: None):
                f = FFN[name]
                n0, last = f.n0, FFN_STEPS - 1
                acted, silued = E(name + "_acted"), E(name + "_silu")
                turned_hi, turned_lo = E(name + "_turned_hi"), E(name + "_turned_lo")

                def product_of_halves(first):
                    for tt in range(TT):
                        dve.wait_ge(silued, first + tt + 1)
                        dve.tensor_tensor(FA[:, tt, :], FA[:, tt, :], bank[6 + tt][:, GLU:2 * GLU], ALU.mult).then_inc(acted, 1)

                def turned_low(turn):
                    dve.wait_ge(turned_hi, turn)
                    dve.tensor_tensor(AFTl[:, :, :], bank[5][:, :].rearrange("p (a b) -> p a b", a=2),
                                      AFTh[:, :, :].bitcast(F32), ALU.subtract).then_inc(turned_lo, 1)

                split_rows()
                split_to(n0 + 4)
                if alpha:
                    alpha_x()
                product_of_halves(0)
                with dve.Fori(0, FFN_PAIRS) as pair:
                    for two in range(2):
                        for i in range(FFN_TILES):
                            n = n0 + 4 + FFN_TILES * two + i
                            if i == 4:
                                turned_low(pair * 2 + two + 1)
                            low(n, pair * (2 * FFN_TILES) + n + 1)
                        product_of_halves(pair * (2 * TT) + TT * two + TT)
                turned_low(FFN_STEPS)
                n = n0 + 4 + FFN_TILES * last
                split[0] = n
                split_to(n + 2)
                dve.wait_ge(tile_used, n + 2)
                u = units[0]
                for tt in range(TT):
                    for i in range(2):
                        units[0] += 1
                        put(bank[(u + 2 * tt + i) % GEMM_BANKS][:, :], tt, Block(512 * i, 512, None))
                    done(tt)
                ahead(n + 2)

            def attend(a, between=None):
                n = len(a.units)

                def soften(i):
                    h, tt = a.units[i]
                    nk = a.keys(tt)
                    k = att[0] + i
                    p = PR[:, k % 3, 0:2 * nk].rearrange("p (h n) -> p h n", h=2)
                    if k >= 3:
                        dve.wait_ge(turned, group_of[k - 3] + 1)
                    s = unit()[:, 0:2 * nk].rearrange("p (h n) -> p h n", h=2)
                    if a.bias is None:
                        release(dve.tensor_scalar(p, s, a.scale, None, ALU.mult))
                    else:
                        release(dve.scalar_tensor_tensor(p, s, a.scale, a.bias(h, tt), ALU.mult, ALU.add))
                    if a.extra is not None:
                        step(dve.tensor_tensor(p, p, a.extra(tt), ALU.add))
                    step(dve.tensor_reduce(MX[:, k % 4, :], p, AX, ALU.max))
                    dve.tensor_scalar(NM[:, k % 4, :], MX[:, k % 4, :], -1.0, None, ALU.mult).then_inc(att_shifted, 1)

                def put(i):
                    h, tt = a.units[i]
                    k = att[0] + i
                    dve.wait_ge(att_exp, k + 1)
                    step(dve.reciprocal(RL[:, :], LS[:, k % 4, :]))
                    dve.wait_ge(out_done, outs[0] + 1)
                    o = bank[6 + outs[0] % 2][:, 0:2 * a.dv].rearrange("p (h e) -> p h e", h=2)
                    outs[0] += 1
                    dve.tensor_tensor(a.put(h, tt), o, RL[:, :].unsqueeze(2).to_broadcast([P, 2, a.dv]),
                                      ALU.mult).then_inc(out_read, 1)
                    dve.wait_ge(out_read, outs[0])

                for i in range(n + LOOKAHEAD + 1):
                    if i < n:
                        soften(i)
                    if i > LOOKAHEAD:
                        put(i - LOOKAHEAD - 1)
                    if between is not None and i < n:
                        between(i)
                att[0] += n

            def rotate(x1, x2, o1, o2, cos, sin, t):
                step(dve.tensor_tensor(t[0], x1, cos, ALU.mult))
                step(dve.tensor_tensor(t[1], x2, sin, ALU.mult))
                step(dve.tensor_tensor(t[2], x2, cos, ALU.mult))
                step(dve.tensor_tensor(t[3], x1, sin, ALU.mult))
                step(dve.tensor_tensor(o1, t[0], t[1], ALU.subtract))
                step(dve.tensor_tensor(o2, t[2], t[3], ALU.add))

            mark(dve.memset(ZERO[:, :].bitcast(F32), 0.0), "zeroed")
            dve.wait_ge(E("c_hi"), 1)
            dve.tensor_tensor(HTl[:, :, 0:P], CCOL.unsqueeze(2).to_broadcast([P, KD, P]), HTh[:, :, 0:P].bitcast(F32),
                              ALU.subtract).then_inc(E("c_spread"), 1)
            shift1, scale1, gate1, shift2, scale2, gate2 = MOD

            def gain(scale, name, more=1.0):
                v = vec(name)
                step(dve.scalar_tensor_tensor(scale, scale, more, v, ALU.add, ALU.mult))
                vec_over(name)

            def first_rows(tt):
                x, h = X[:, tt, :], H[:, tt, :]
                dve.wait_ge(E("x_in"), 16)
                square_sum(x, SUMS[:, 0, 0:1])
                k = rsqrt(SUMS[:, 0, 0:1], 1.0 / D, 1e-6)
                step(dve.scalar_tensor_tensor(h, x, rooted(k), scale1, ALU.mult, ALU.mult))
                step(dve.tensor_tensor(h, h, shift1, ALU.add))
                signal("h1")

            for i in range(6):
                v = vec(f"b_mod{i}")

                def modulation(s, tt, b, i=i, v=v):
                    c = slice(b.col, b.col + b.cols)
                    release(dve.tensor_tensor(MOD[i][:, c], s, v[:, c], ALU.add))

                gemm(f"mod{i}", modulation, 1)
                vec_over(f"b_mod{i}")
                if i == 1:
                    gain(scale1, "g_pre_mix")
                elif i in (2, 3):
                    first_rows(i - 2)
            dve.wait_ge(E("setup"), 64)
            mark(dve.tensor_tensor(RELS, unit()[0:24, 0:384], BUCK[0:24, 384:768], ALU.add), "rel_rows")
            dve.sem_inc(unit_read, 1)
            split_rows()

            def rotate1(tt):
                x = PROJ1[:, tt, 0:1024].rearrange("p (h two e) -> p two h e", two=2, e=32)
                o = Y[:, tt, :].rearrange("p (h two e) -> p two h e", two=2, e=32)
                t = [H[:, 0, 512 * i:512 * (i + 1)].rearrange("p (h e) -> p h e", e=32) for i in range(2)]
                t += [H[:, 1, 512 * i:512 * (i + 1)].rearrange("p (h e) -> p h e", e=32) for i in range(2)]
                cos = tab("cos1")[:, 32 * tt:32 * (tt + 1)].unsqueeze(1).to_broadcast([P, 16, 32])
                sin = tab("sin1")[:, 32 * tt:32 * (tt + 1)].unsqueeze(1).to_broadcast([P, 16, 32])
                rotate(x[:, 0], x[:, 1], o[:, 0], o[:, 1], cos, sin, t)

            copy_out("in1", lambda tt, c, n: PROJ1[:, tt, c:c + n], then={2: lambda: rotate1(0), 3: lambda: rotate1(1)})
            signal("rope1")
            gain(gate1, "g_post_mix", 0.0)
            gain(scale2, "g_pre_ffn")
            gain(gate2, "g_post_ffn", 0.0)
            attend(A_DIL)
            signal("dil_out")
            dve.wait_ge(E("small"), 16 * len(small_at))
            gb = small("b_gate", 256).unsqueeze(1).to_broadcast([P, TT, 256])
            az = H[:, :, 0:256]
            release(dve.tensor_tensor(LA, unit()[:, :].rearrange("p (t n) -> p t n", t=TT), gb, ALU.add))
            mark(dve.scalar_tensor_tensor(az, LA, -1.0, LA, ALU.mult, ALU.max), "z_abs")
            dve.wait_ge(E("z_log"), 1)
            step(dve.scalar_tensor_tensor(LA, LA, 0.0, az, ALU.min, ALU.subtract))
            mark(dve.tensor_scalar(LA, LA, 1.0 / 16.0, None, ALU.mult), "log_a")
            for tt in range(TT):
                release(dve.tensor_copy(GB[:, tt, :], unit()[:, :]))
            step(dve.tensor_tensor(GB[:, :, 256:512], GB[:, :, 256:512], GB[:, :, 0:256], ALU.subtract))
            release(dve.tensor_copy(MISC[:, 8:16], unit()[:, 0:8]))
            signal("gla_b")
            dve.wait_ge(E("gla_exp"), 1)
            qg, kg = PROJ1[:, :, 1536:1792], PROJ1[:, :, 1792:2048]
            step(dve.scalar_tensor_tensor(QKD[:, :, 0:256], qg, 64.0 ** -0.5, Y[:, :, 0:256], ALU.mult, ALU.mult))
            step(dve.tensor_tensor(QKD[:, :, 256:512], kg, Y[:, :, 256:512], ALU.mult))
            mark(dve.tensor_tensor(KL, kg, GB[:, :, 256:512], ALU.mult), "gla_qk")
            step(dve.memset(ATTM, 0.0))
            step(dve.memset(STATE[:, 0], 0.0))
            dve.wait_ge(E("gla_mask"), 16)
            for tt in range(TT):
                for par in range(2):
                    dst = ATTM[:, tt, :].rearrange("p (m two c) -> p two m c", m=2, two=2)[:, par]
                    release(dve.copy_predicated(dst, TMASK[:, 0:256].rearrange("p (m c) -> p m c", m=2),
                                                unit()[:, 0:256].rearrange("p (m c) -> p m c", m=2)))
            u02 = unit()[:, :].rearrange("p (n m e) -> p n m e", n=2, m=2)
            step(dve.tensor_copy(STATE[:, 1], u02[:, 0]))
            u1 = unit()[:, 0:256].rearrange("p (m e) -> p m e", m=2)
            for n, u in ((2, u1), (3, u02[:, 1])):
                for m in range(2):
                    step(dve.scalar_tensor_tensor(STATE[:, n, m], STATE[:, n - 1, m], AN[:, m, n - 1:n], u[:, m],
                                                  ALU.mult, ALU.add))
            dve.sem_inc(unit_read, 2)
            signal("gla_state")
            for tt in range(TT):
                release(dve.tensor_copy(OG[:, tt, :], unit()[:, :]))
                for par in range(2):
                    dst = OG[:, tt, :].rearrange("p (m two e) -> p two m e", m=2, two=2)[:, par]
                    release(dve.tensor_tensor(dst, dst, unit()[:, 0:256].rearrange("p (m e) -> p m e", m=2), ALU.add))
            rms_heads([OG[:, tt, :] for tt in range(TT)], 4, P, small("g_gla", 128))
            dve.wait_ge(E("silu_r"), 1)
            for tt in range(TT):
                step(dve.tensor_tensor(MIX[:, tt, 512:1024], OG[:, tt, :], SR[:, tt, :], ALU.mult))
                signal("mix1")

            split_rows()
            copy_out("out1", lambda tt, c, n: Y[:, tt, c:c + n], done=ask)
            ks = roots_of_stats(1e-6)
            for tt in range(TT):
                step(dve.scalar_tensor_tensor(Y[:, tt, :], Y[:, tt, :], rooted(ks[tt]), gate1, ALU.mult, ALU.mult))
                step(dve.tensor_tensor(X[:, tt, :], X[:, tt, :], Y[:, tt, :], ALU.add))
                ask(tt)
            ks = roots_of_stats(1e-6)
            for tt in range(TT):
                step(dve.scalar_tensor_tensor(H[:, tt, :], X[:, tt, :], rooted(ks[tt]), scale2, ALU.mult, ALU.mult))
                step(dve.tensor_tensor(H[:, tt, :], H[:, tt, :], shift2, ALU.add))
                signal("h2")
            split_rows()
            gemm("router", lambda s, tt, b: release(dve.tensor_tensor(RT[:, tt, :], s, small("router_b", 32), ALU.add)))
            for tt in range(TT):
                step(dve.max(TOPV[:, :], RT[:, tt, :]))
                step(dve.max_index(TOPI[:, :], TOPV[:, :], RT[:, tt, :]))
                step(dve.tensor_copy(TOPF[:, :], TOPI[:, :]))
                step(dve.tensor_scalar(MISC[:, 50:51], TOPV[:, 0:1], -1.0, None, ALU.mult))
                mark2 = f"top{tt}"
                signal(mark2)
                dve.wait_ge(E(f"top_exp{tt}"), 1)
                step(dve.reciprocal(MISC[:, 51:52], MISC[:, 52:53]))
                step(dve.tensor_scalar(MISC[:, 54:58], MISC[:, 58:62], MISC[:, 51:52], None, ALU.mult))
                for j in range(TOP_K):
                    dst = MASKS[:, tt, :] if j == 0 else TMP32
                    step(dve.tensor_scalar(dst, tab("ramp32"), TOPF[:, j:j + 1], None, ALU.is_equal))
                    if j == 0:
                        step(dve.tensor_scalar(GATES[:, tt, :], dst, MISC[:, 54:55], None, ALU.mult))
                    else:
                        step(dve.tensor_tensor(MASKS[:, tt, :], MASKS[:, tt, :], TMP32, ALU.add))
                        step(dve.scalar_tensor_tensor(GATES[:, tt, :], TMP32, MISC[:, 54 + j:55 + j], GATES[:, tt, :],
                                                      ALU.mult, ALU.add))
            signal("routed")
            b = unit()
            for tt in range(TT):
                p = POS[tt][:, 0:N_EXP]
                step(dve.scalar_tensor_tensor(p, b[:, 32 * tt:32 * (tt + 1)], 1.0, MASKS[:, tt, :], ALU.add, ALU.mult))
                step(dve.tensor_scalar(p, p, -1.0, None, ALU.add))
                step(dve.tensor_scalar(POS[tt][:, N_EXP:N_EXP + 1], POS[tt][:, 0:1], -float(CAP), None, ALU.add))
            step(dve.tensor_reduce(MISC[:, 35:36], b[:, 64:96], AX, ALU.max))
            dve.sem_inc(unit_read, 1)
            mark(dve.tensor_scalar(NPASS[:, :], MISC[:, 35:36], float(CAP), 1.0, ALU.is_gt, ALU.add), "n_pass")
            n_pass = dve.value_load(NPASS[0:1, 0:1], min_val=1, max_val=2)
            step(dve.memset(GSELT, 0.0))
            mark(dve.memset(OUTE[:, 0:512], 0.0), "moe_zero")
            pows_before.append(len(pow_widths))
            dve.sem_inc(m_up_read, 4)
            dve.sem_inc(m_lo[0], lo_per[0])

            def choose(col):
                for tt in range(TT):
                    ins = dve.tensor_scalar(PSEL[:, tt, :], tab("ramp"), POS[tt][:, col], None, ALU.is_equal)
                ins.then_inc(m_sel, 1)

            def low_of(half, lo, hi, done, hi_made, lo_made):
                k = slice(4 * half, 4 * half + 4)
                dve.wait_ge(hi_made, done)
                dve.tensor_tensor(lo[:, k, :], bank[6 + half][:, :].rearrange("p (a b) -> p a b", a=4),
                                  hi[:, k, :].bitcast(F32), ALU.subtract).then_inc(lo_made, 1)

            choose(slice(0, 1))
            low_of(1, XETl, XETh, 1, m_xhi, m_xlo)
            low_of(0, XETl, XETh, 2, m_xhi, m_xlo)
            with dve.Fori(0, n_pass) as ps:
                with dve.Fori(0, N_EXP) as ex:
                    it = ps * N_EXP + ex

                    def lows(first, last):
                        for t in range(first, last):
                            if not pool_tile(t):
                                dve.wait_ge(m_hi, it * MOE_TILES + t + 1)
                                dve.tensor_tensor(w_lo[:, t % PARTS, :], moe_raw(t), w_hi[:, t % PARTS, :].bitcast(F32),
                                                  ALU.subtract).then_inc(m_lo[0], 1)

                    def add_bias(b):
                        c = slice(512 * b, 512 * (b + 1))
                        dve.wait_ge(m_used, moe_used(it, 4 * b + 3))
                        dve.tensor_tensor(GU[:, c], bank[4 + b % 2][:, :], BB[:, c], ALU.add).then_inc(m_up_read, 1)

                    def clip(half):
                        f = slice(512 * half, 512 * (half + 1))
                        dve.wait_ge(m_up_read, it * 4 + 6 + 2 * half)
                        dve.tensor_scalar(GL[:, f], glu_in[:, f, 0], 7.0, None, ALU.min).then_inc(m_glu, 1)
                        dve.tensor_scalar(AV[:, f], glu_in[:, f, 1], 7.0, -7.0, ALU.min, ALU.max).then_inc(m_chain, 1)

                    def activate(half):
                        f = slice(512 * half, 512 * (half + 1))
                        dve.wait_ge(m_sig, it * 2 + half + 1)
                        dve.wait_ge(m_chain, it * M_STEPS + 2 * half + 1)
                        dve.tensor_tensor(GL[:, f], GL[:, f], SG[:, f], ALU.mult).then_inc(m_chain, 1)
                        dve.wait_ge(m_chain, it * M_STEPS + 2 * half + 2)
                        dve.scalar_tensor_tensor(AV[:, f], AV[:, f], 1.0, GL[:, f], ALU.add, ALU.mult).then_inc(m_act, 1)

                    lows(0, 7)
                    dve.wait_ge(m_bias, it + 1)
                    add_bias(0)
                    lows(7, 11)
                    add_bias(1)
                    lows(11, 12)
                    clip(0)
                    lows(12, 14)
                    activate(0)
                    lows(14, 15)
                    add_bias(2)
                    for tt in range(TT):
                        dve.tensor_scalar(GSEL[:, tt, :], tab("ramp"), POS[tt][:, bass.ds(ex, 1)],
                                          GATES[:, tt, bass.ds(ex, 1)], ALU.is_equal, ALU.mult)
                    dve.wait_ge(m_gather, it * 2 + 2)
                    choose(bass.ds(ex + 1, 1))
                    lows(15, 18)
                    add_bias(3)
                    clip(1)
                    low_of(0, AVTl, AVTh, it * 2 + 1, m_ahi, m_alo)
                    low_of(1, XETl, XETh, it * 2 + 3, m_xhi, m_xlo)
                    activate(1)
                    lows(18, 21)
                    low_of(1, AVTl, AVTh, it * 2 + 2, m_ahi, m_alo)
                    lows(21, 22)
                    low_of(0, XETl, XETh, it * 2 + 4, m_xhi, m_xlo)
                    lows(22, MOE_TILES)
                for tt in range(TT):
                    dve.tensor_scalar(POS[tt], POS[tt], -float(CAP), None, ALU.add).then_inc(m_pass, 1)
                dve.wait_ge(m_pass, ps * TT + TT)
            dve.wait_ge(E("moe_over"), 1)
            for i in range(4):
                ask(i)
            ks = []
            for tt in range(TT):
                first, second = stat(), stat()
                step(dve.tensor_tensor(SUMS[:, tt, 0:1], first, second, ALU.add))
                ks.append(rsqrt(SUMS[:, tt, 0:1], 1.0 / D, 1e-6))
            for tt in range(TT):
                for i in range(2):
                    c = slice(512 * i, 512 * (i + 1))
                    step(dve.scalar_tensor_tensor(Y[:, tt, c], bank[2 * tt + i][:, :], rooted(ks[tt]), gate2[:, c],
                                                  ALU.mult, ALU.mult))
                step(dve.tensor_tensor(X[:, tt, :], X[:, tt, :], Y[:, tt, :], ALU.add))
                signal("x1")
            signal("moe_sum")

            ffn("f1", onto_x(0.5), True, ask)
            layer_norm(1)
            split_rows()

            def norm_c(a, n, name):
                rms_rows([(PROJ2[:, tt, a:a + n], PROJ2[:, tt, a:a + n], small(name, n), lambda: None) for tt in range(TT)])

            def lam_products():
                for i in range(2):
                    step(dve.tensor_tensor_reduce(SQ[:, 0:64], small(f"lam_q{i + 1}_2", 64), small(f"lam_k{i + 1}_2", 64),
                                                  1.0, 0.0, ALU.mult, ALU.add, MISC[:, 16 + i:17 + i]))
                signal("lam_in")

            angles2 = [(tab("cos2")[:, 16 * tt:16 * (tt + 1)], tab("sin2")[:, 16 * tt:16 * (tt + 1)]) for tt in range(TT)]

            def rotate_key():
                for tt in range(TT):
                    t = [SQ[:, 16 * i:16 * (i + 1)] for i in range(4)]
                    r = PROJ2[:, tt, 640:672]
                    rotate(r[:, 0:16], r[:, 16:32], r[:, 0:16], r[:, 16:32], *angles2[tt], t)

            copy_out("in2", lambda tt, c, n: PROJ2[:, tt, c:c + n],
                     then={2: lambda: norm_c(0, 384, "q_norm_g_2"), 3: lambda: norm_c(384, 256, "kv_norm_g_2")})
            signal("c_norm")
            gate_bias = [vec(f"b_gate2_{i}") for i in range(2)]

            def gate(s, tt, b):
                v = gate_bias[b.col // D]
                release(dve.tensor_tensor(GATE2[:, tt, b.col:b.col + b.cols], s, v[:, b.col % D:b.col % D + b.cols], ALU.add))

            gemm("gate2", gate, then={0: lam_products, 1: rotate_key})
            for i in range(2):
                vec_over(f"b_gate2_{i}")
            signal("gate2_in")
            rows_lo([(HTl[:, k:k + n, :], HTh[:, k:k + n, :]) for k, n in ((0, 2), (2, 2), (4, 1))])
            kms = [KM[:, tt, 0:MLA_H * MLA_QK].rearrange("p (h e) -> p h e", h=MLA_H) for tt in range(TT)]

            def rotate_queries():
                for tt in range(TT):
                    t = [SQ[:, 128 * i:128 * (i + 1)].rearrange("p (h e) -> p h e", e=16) for i in range(4)]
                    x = QM[:, tt, :].rearrange("p (h e) -> p h e", h=MLA_H)
                    cos, sin = (a.unsqueeze(1).to_broadcast([P, MLA_H, 16]) for a in angles2[tt])
                    rotate(x[:, :, 64:80], x[:, :, 80:96], x[:, :, 64:80], x[:, :, 80:96], cos, sin, t)

            def key_value(s, tt, b):
                h = slice(b.col // P, (b.col + b.cols) // P)
                s = s.rearrange("p (h e) -> p h e", e=P)
                step(dve.tensor_copy(kms[tt][:, h, 0:MLA_NOPE], s[:, :, 0:MLA_NOPE]))
                release(dve.tensor_copy(KV[:, tt, :].rearrange("p (h e) -> p h e", e=P)[:, h, MLA_NOPE:], s[:, :, MLA_NOPE:]))

            copy_out("q_b", lambda tt, c, n: QM[:, tt, c:c + n])
            for tt in range(TT):
                r = PROJ2[:, tt, 640:672]
                step(dve.tensor_copy(kms[tt][:, :, MLA_NOPE:], r.unsqueeze(1).to_broadcast([P, MLA_H, MLA_ROPE])))
            gemm("kv_b", key_value, then={0: rotate_queries})
            dve.wait_ge(E("lam_exp"), 1)
            step(dve.tensor_tensor(MISC[:, 20:21], MISC[:, 19:20], MISC[:, 18:19], ALU.subtract))
            step(dve.tensor_scalar(MISC[:, 21:22], MISC[:, 20:21], -LAM_INIT, None, ALU.add))
            signal("mla_qk")
            alpha_x()
            attend(A_MLA)
            dve.wait_ge(E("bias2"), 16)
            attend(A_DIFF)
            signal("diff_done")
            for tt in range(TT):
                o = OD8[:, tt, :].rearrange("p (h two e) -> p two h e", two=2, e=P)
                d = MIX[:, tt, 512:1024].rearrange("p (h e) -> p h e", h=4)
                step(dve.scalar_tensor_tensor(d, o[:, 1], MISC[:, 21:22], o[:, 0], ALU.mult, ALU.add))
            rms_heads([MIX[:, tt, 512:1024] for tt in range(TT)], 4, P, small("diff_norm_g_2", 128), 1.0 - LAM_INIT)
            signal("mix2")
            split_rows()
            dve.wait_ge(E("gate2_sig"), 1)

            def gated_pair(first, second, gates, at):
                def put_first(s, tt, b):
                    release(dve.tensor_tensor(Y[:, tt, b.col:b.col + b.cols], s,
                                              gates[:, tt, at + b.col:at + b.col + b.cols], ALU.mult))

                def put_second(s, tt, b):
                    c = slice(b.col, b.col + b.cols)
                    release(dve.tensor_tensor(MIX[:, tt, c], s, gates[:, tt, at + D + b.col:at + D + b.col + b.cols], ALU.mult))
                    step(dve.tensor_tensor(MIX[:, tt, c], MIX[:, tt, c], Y[:, tt, c], ALU.add))

                gemm(first, put_first)
                gemm(second, put_second)

            gated_pair("up_mla", "up_diff", GATE2, 0)
            signal("gated2")
            split_rows()
            gemm("o2", onto_x(1.0), done=ask)
            layer_norm(2)
            split_rows()
            copy_out("mem_q", lambda tt, c, n: QMEM[:, tt, c:c + n])
            split_rows()
            copy_out("mem_kv", lambda tt, c, n: KVM[:, tt, c:c + n])
            signal("mem_qkv")
            alpha_x()
            attend(A_MEM)
            signal("mem_out")
            split_rows()
            gemm("mem_o", onto_x(1.0), done=ask)
            layer_norm(3)
            ffn("f2", onto_x(0.5), True, ask)
            layer_norm(4, ask)

            def normed(name, ready):
                v = vec(name)
                ks = roots_of_stats(1e-6)
                for tt in range(TT):
                    step(dve.scalar_tensor_tensor(H[:, tt, :], X[:, tt, :], rooted(ks[tt]), v, ALU.mult, ALU.mult))
                    signal(ready)
                vec_over(name)

            normed("ffn1_norm", "h3")
            ffn("f3", onto_x(0.5), done=ask)
            normed("mix_norm", "h4")
            split_rows()
            gate3 = [vec(f"b_gate3_{i}") for i in range(2)]
            ends3 = [IN3 - 2 * D, IN3 - D, IN3]

            def put3(s, tt, b):
                c, pieces = b.col, []
                for end, bias in zip(ends3, [None] + gate3):
                    e = min(end, b.col + b.cols)
                    if c < e:
                        pieces.append((c, e, bias, end - D))
                        c = e
                for c, e, bias, first in pieces:
                    dst, src = PROJ3[:, tt, c:e], s[:, c - b.col:e - b.col]
                    ins = (dve.tensor_copy(dst, src) if bias is None else
                           dve.tensor_tensor(dst, src, bias[:, c - first:e - first], ALU.add))
                    if e == b.col + b.cols:
                        release(ins)
                    else:
                        step(ins)

            roots3 = {}

            def qk_roots(c):
                roots3[c] = heads_roots([PROJ3[:, tt, c:c + 512] for tt in range(TT)], 8, HD)

            def qk_scaled(c, name):
                heads_scaled(roots3[c], [PROJ3[:, tt, c:c + 512] for tt in range(TT)], 8, HD, small(name, HD))

            def index_rows():
                for tt in range(TT):
                    step(dve.tensor_copy(KI2[:, tt, :].rearrange("p (a e) -> p a e", a=2),
                                         PROJ3[:, tt, 3328:3392].unsqueeze(1).to_broadcast([P, 2, 64])))
                    step(dve.tensor_scalar(MISC[:, 4 * tt:4 * tt + 4], PROJ3[:, tt, 3392:3396], 4.0 ** -0.5, None, ALU.mult))

            gemm("in3", put3, then={
                1: lambda: qk_roots(0), 2: lambda: qk_scaled(0, "q_norm_dsa_3"),
                3: lambda: qk_roots(512), 4: lambda: qk_scaled(512, "k_norm_dsa_3"),
                5: lambda: qk_roots(1536), 6: lambda: qk_scaled(1536, "q_norm_moba_3"),
                7: lambda: qk_roots(2048), 8: lambda: qk_scaled(2048, "k_norm_moba_3"), 9: index_rows})
            for i in range(2):
                vec_over(f"b_gate3_{i}")
            signal("gate3_in")
            signal("qk3")
            for tt in range(TT):
                nk = P * (tt + 1)
                sc = SEL[:, tt, 0:nk]
                for i in range(4):
                    if i % 2 == 0:
                        b = unit()
                    h = 2 * (i % 2) + i // 2
                    w = MISC[:, 4 * tt + h:4 * tt + h + 1]
                    dots = SQ[:, 0:nk]
                    ins = dve.tensor_scalar(dots, b[:, (i % 2) * nk:(i % 2 + 1) * nk], 64.0 ** -0.5, 0.0, ALU.mult, ALU.max)
                    if i % 2 == 1:
                        release(ins)
                    else:
                        step(ins)
                    if i == 0:
                        step(dve.tensor_scalar(sc, dots, w, None, ALU.mult))
                    else:
                        step(dve.scalar_tensor_tensor(sc, dots, w, sc, ALU.mult, ALU.add))
                m = tab("causal")[:, P:S] if tt == 0 else tab("causal")
                step(dve.tensor_tensor(sc, sc, m, ALU.add))

            def choose_round(i):
                tt, r = divmod(i, DSA_TOPK // 8)
                sc = SEL[:, tt, 0:P * (tt + 1)]
                step(dve.max(TOPV[:, :], sc))
                step(dve.match_replace(sc, TOPV[:, :], sc, TAKEN))
                if r == DSA_TOPK // 8 - 1:
                    step(dve.tensor_scalar(sc, sc, TAKEN / 2, NEG, ALU.is_gt, ALU.mult))

            dve.wait_ge(E("bias3b"), 16)
            each = TT * (DSA_TOPK // 8) // len(A_MOBA.units)
            attend(A_MOBA, lambda i: [choose_round(each * i + j) for j in range(each)])
            signal("moba_done")
            dve.wait_ge(E("bias3a"), 16)
            attend(A_DSA)
            signal("mix3")
            split_rows()
            dve.wait_ge(E("gate3_sig"), 1)
            gated_pair("br_dsa", "br_moba", PROJ3, 3396)
            signal("gated3")
            split_rows()
            gemm("out3", onto_x(1.0), done=ask)
            normed("ffn2_norm", "h5")
            ffn("f4", onto_x(0.5))
            signal("result")

        @block.scalar
        def _(act):
            group = [0]
            att = [0]
            split = [0]
            rows = [0]

            def high(n, landed, used):
                m = tiles[n].kts * tiles[n].cols
                act.wait_ge(raw_landed[n % RAW], landed)
                if used is not None:
                    act.wait_ge(tile_used, used)
                act.activation(w_hi[:, n % PARTS, 0:m], raw[:, n % RAW, 0:m], ACT.Copy).then_inc(hi_done, 1)

            def split_to(n):
                for i in range(split[0], n):
                    high(i, tiles[i].landed, i - PARTS + 1 if i >= PARTS else None)
                split[0] = max(split[0], n)

            def gemm(*names):
                n = G[names[-1]][-1].tiles[-1].n + 1
                split_to(min(n + PARTS, moe_at if n <= moe_at else len(tiles)))

            def rows_hi_to(dsts):
                for dst in dsts:
                    g = rows[0]
                    act.wait_ge(rows_turned, g + 1)
                    n = dst.shape[1] * dst.shape[2]
                    act.activation(dst, bank[4 + g % 2][:, 0:n].rearrange("p (a b) -> p a b", a=dst.shape[1]),
                                   ACT.Copy).then_inc(rows_hi, 1)
                    rows[0] += 1

            def split_rows():
                rows_hi_to([HTh[:, 4 * k:4 * k + 4, tt * P:(tt + 1) * P] for tt in range(TT) for k in range(2)])

            def turned_to(dsts):
                for dst, rows, n in dsts:
                    g = group[0]
                    act.wait_ge(turned, g + 1)
                    src = bank[4 + g % 2][0:rows, 0:n]
                    if len(dst.shape) == 3:
                        src = src.rearrange("p (a b) -> p a b", a=dst.shape[1])
                    act.activation(dst, src, ACT.Copy).then_inc(turned_read, 1)
                    group[0] += 1

            def rows_to(dst):
                turned_to([(dst[:, 4 * k:4 * k + 4, tt * P:(tt + 1) * P], P, 512) for tt in range(TT) for k in range(2)])

            stats = [0]

            def row_sum(src, func, bias=0.0):
                j = stats[0]
                stats[0] += 1
                if j:
                    act.wait_ge(stat_out, j)
                act.wait_ge(stat_in, j + 1)
                act.activation(SQ[:, 0:src.shape[1]], src, func, bias=bias, accum_out=STATS[:, j % 8:j % 8 + 1]).then_inc(stat_out, 1)

            def squares(buf):
                for tt in range(TT):
                    row_sum(buf[:, tt, :], ACT.Square)

            def distances():
                for tt in range(TT):
                    row_sum(X[:, tt, :], ACT.Identity)
                for tt in range(TT):
                    row_sum(X[:, tt, :], ACT.Square, NEG_MEAN[:, tt:tt + 1])

            def attend(a):
                n = len(a.units)
                for i in range(n + LOOKAHEAD):
                    if i < n:
                        h, tt = a.units[i]
                        nk = a.keys(tt)
                        k = att[0] + i
                        act.wait_ge(att_shifted, k + 1)
                        for hh in range(2):
                            p = PR[:, k % 3, hh * nk:(hh + 1) * nk]
                            ins = act.activation(p, p, ACT.Exp, bias=NM[:, k % 4, hh:hh + 1],
                                                 accum_out=LS[:, k % 4, hh:hh + 1])
                        ins.then_inc(att_exp, 1)
                    if i >= LOOKAHEAD:
                        h, tt = a.units[i - LOOKAHEAD]
                        k = att[0] + i - LOOKAHEAD
                        turned_to([(PT[:, k % 2, 0:2 * a.keys(tt)], P, 2 * a.keys(tt))])
                att[0] += n

            def ffn(name):
                f = FFN[name]
                n0, last = f.n0, FFN_STEPS - 1

                def silu(used):
                    act.wait_ge(tile_used, used)
                    for tt in range(TT):
                        act.activation(FA[:, tt, :], bank[6 + tt][:, 0:GLU], ACT.Silu).then_inc(E(name + "_silu"), 1)

                def turned_high(turn):
                    act.wait_ge(E(name + "_turned"), turn)
                    act.activation(AFTh[:, :, :], bank[5][:, :].rearrange("p (a b) -> p a b", a=2),
                                   ACT.Copy).then_inc(E(name + "_turned_hi"), 1)

                split_rows()
                split_to(n0 + 4)
                silu(n0 + 4)
                with act.Fori(0, FFN_PAIRS) as pair:
                    for two in range(2):
                        for i in range(FFN_TILES):
                            n = n0 + 4 + FFN_TILES * two + i
                            if i == 4:
                                turned_high(pair * 2 + two + 1)
                            high(n, pair * (32 * 2 * FFN_TILES // RAW) + tiles[n].landed, pair * (2 * FFN_TILES) + n - PARTS + 1)
                        silu(pair * (2 * FFN_TILES) + n0 + 8 + FFN_TILES * two)
                turned_high(FFN_STEPS)
                n = n0 + 4 + FFN_TILES * last
                split[0] = n
                split_to(min(n + 2 + PARTS, len(tiles)))

            def one(wait, name, *ops):
                act.wait_ge(E(wait), 1)
                for o in ops:
                    ins = act.activation(*o[0:3], **o[3])
                ins.then_inc(E(name), 1)

            act.wait_ge(E("c_in"), 16)
            act.activation(CCOL, CCOL, ACT.Silu).then_inc(E("c_act"), 1)
            act.wait_ge(E("c_act"), 1)
            act.activation(HTh[:, :, 0:P], CCOL.unsqueeze(2).to_broadcast([P, KD, P]), ACT.Copy).then_inc(E("c_hi"), 1)
            gemm("mod5")
            split_rows()
            gemm("in1")
            rows_to(QT)
            attend(A_DIL)
            turned_to([(GLRT, 16, 256)])
            az = H[:, :, 0:256]
            act.wait_ge(E("z_abs"), 1)
            act.activation(az, az, ACT.Exp, scale=-1.0).then_inc(E("z_exp"), 1)
            act.wait_ge(E("z_exp"), 1)
            act.activation(az, az, ACT.Ln, bias=1.0).then_inc(E("z_log"), 1)
            one("gla_b", "gla_exp", (Y[:, :, 0:256], GB[:, :, 0:256], ACT.Exp, {}),
                (Y[:, :, 256:512], GB[:, :, 0:256], ACT.Exp, {"scale": -1.0}),
                (AN.rearrange("p m n -> p (m n)"), MISC[:, 8:16], ACT.Exp, {}),
                (GB[:, :, 256:512], GB[:, :, 256:512], ACT.Exp, {}))
            act.activation(SR, PROJ1[:, :, 2560:3072], ACT.Silu).then_inc(E("silu_r"), 1)
            act.wait_ge(E("rel_rows"), 1)
            turned_to([(GT[:, 0:4, tt * P:(tt + 1) * P], P, 512) for tt in range(TT)])
            split_rows()
            gemm("out1")
            squares(Y)
            squares(X)
            split_rows()
            gemm("router")
            for tt in range(TT):
                act.wait_ge(E(f"top{tt}"), 1)
                act.activation(MISC[:, 58:62], TOPV[:, 0:4], ACT.Exp, bias=MISC[:, 50:51],
                               accum_out=MISC[:, 52:53]).then_inc(E(f"top_exp{tt}"), 1)
            turned_to([(GATET, 32, 256)])
            act.wait_ge(E("n_pass"), 1)
            n_pass = act.value_load(NPASS[0:1, 0:1], min_val=1, max_val=2)

            def high_of(half, hi, done, made, hi_made):
                act.wait_ge(made, done)
                act.activation(hi[:, 4 * half:4 * half + 4, :], bank[6 + half][:, :].rearrange("p (a b) -> p a b", a=4),
                               ACT.Copy).then_inc(hi_made, 1)

            def out_half(n, used):
                act.wait_ge(m_used, used)
                act.activation(OUTE[:, 512 * n:512 * (n + 1)], bank[4 + n][:, :], ACT.Copy).then_inc(m_down_read, 1)

            act.wait_ge(E("moe_begun"), 1)
            act.wait_ge(E("moe_zero"), 1)
            act.sem_inc(m_down_read, 2)
            act.sem_inc(m_gtc, 1)
            high_of(1, XETh, 1, m_gather, m_xhi)
            high_of(0, XETh, 2, m_gather, m_xhi)
            act.activation(MISC[:, 22:23], MISC[:, 52:53], ACT.Sigmoid)
            with act.Fori(0, n_pass) as ps:
                with act.Fori(0, N_EXP) as ex:
                    it = ps * N_EXP + ex

                    def highs(first, last):
                        for t in range(first, last):
                            act.wait_ge(m_landed[t % MOE_RAW], it * (16 * MOE_TILES // MOE_RAW) + 16 * (t // MOE_RAW + 1))
                            act.wait_ge(m_used, moe_used(it, t - PARTS))
                            act.activation(w_hi[:, t % PARTS, :], moe_raw(t), ACT.Copy).then_inc(m_hi, 1)

                    def sigmoid(half):
                        f = slice(512 * half, 512 * (half + 1))
                        act.wait_ge(m_glu, it * 2 + half + 1)
                        act.activation(SG[:, f], GL[:, f], ACT.Sigmoid, scale=1.702).then_inc(m_sig, 1)

                    highs(0, 4)
                    out_half(1, moe_used(it, -1))
                    highs(4, 14)
                    sigmoid(0)
                    highs(14, 18)
                    high_of(0, AVTh, it * 2 + 1, m_tr, m_ahi)
                    high_of(1, XETh, it * 2 + 3, m_gather, m_xhi)
                    sigmoid(1)
                    highs(18, 20)
                    act.wait_ge(m_gt, it + 1)
                    act.activation(GSELT, bank[5][:, 0:2 * P], ACT.Copy).then_inc(m_gtc, 1)
                    highs(20, 21)
                    high_of(1, AVTh, it * 2 + 2, m_tr, m_ahi)
                    highs(21, 22)
                    high_of(0, XETh, it * 2 + 4, m_gather, m_xhi)
                    highs(22, 23)
                    out_half(0, moe_used(it, 19))
                    highs(23, MOE_TILES)
            out_half(1, n_pass * (N_EXP * MOE_TILES) + MOE_TILES)
            act.wait_ge(E("moe_over"), 1)
            for i in range(4):
                row_sum(bank[i][:, :], ACT.Square)
            ffn("f1")
            distances()
            split_rows()
            gemm("in2", "gate2")
            act.wait_ge(E("gate2_in"), 1)
            act.activation(GATE2, GATE2, ACT.Sigmoid).then_inc(E("gate2_sig"), 1)
            rows_hi_to([HTh[:, k:k + n, :] for k, n in ((0, 2), (2, 2), (4, 1))])
            act.wait_ge(E("lam_in"), 1)
            act.activation(MISC[:, 18:20], MISC[:, 16:18], ACT.Exp).then_inc(E("lam_exp"), 1)
            gemm("q_b", "kv_b")
            for dst in (QT, KT):
                turned_to([(dst[0:MLA_QK, 4 * k:4 * k + 4, tt * P:(tt + 1) * P], MLA_QK, 512)
                           for tt in range(TT) for k in range(2)])
            attend(A_MLA)
            rows_to(QT)
            attend(A_DIFF)
            split_rows()
            gemm("up_mla", "up_diff")
            split_rows()
            gemm("o2")
            distances()
            split_rows()
            gemm("mem_q")
            split_rows()
            gemm("mem_kv")
            rows_to(QT)
            rows_to(KT)
            attend(A_MEM)
            split_rows()
            gemm("mem_o")
            distances()
            ffn("f2")
            distances()
            squares(X)
            ffn("f3")
            squares(X)
            split_rows()
            gemm("in3")
            turned_to([(QT[:, 0:2, :], P, 512), (QT[:, 2, :], P, 256)])
            rows_to(QT)
            rows_to(KT)
            attend(A_MOBA)
            act.wait_ge(E("moba_done"), 1)
            act.dma_start(BIAS[:, :, :], bias_rows(8)).then_inc(E("bias3a"), 16)
            act.wait_ge(E("gate3_in"), 1)
            g3 = PROJ3[:, :, IN3 - 2 * D:IN3]
            act.activation(g3, g3, ACT.Sigmoid).then_inc(E("gate3_sig"), 1)
            attend(A_DSA)
            split_rows()
            gemm("br_dsa", "br_moba")
            split_rows()
            gemm("out3")
            squares(X)
            ffn("f4")

        @block.gpsimd
        def _(pool):
            for name, (a, n, src) in small_at.items():
                pool.dma_start(SMALL[:, a:a + n], src[0:1, :].to_broadcast([P, n])).then_inc(E("small"), 16)
            pool.wait_ge(E("setup"), 64)

            def powers(first, last):
                for k in range(first, last):
                    n = pow_widths[k]
                    pool.wait_ge(pow_in, k + 1)
                    pool.tensor_tensor(st_out[:, k % 2, 0:n], st_in[:, k % 2, 0:n], tab("half").to_broadcast([P, n]),
                                       ALU.pow).then_inc(pow_out, 1)

            powers(0, pows_before[0])
            pool.wait_ge(E("n_pass"), 1)
            n_pass = pool.value_load(NPASS[0:1, 0:1], min_val=1, max_val=2)
            pool.sem_inc(m_lo[1], lo_per[1])
            with pool.Fori(0, n_pass) as ps:
                with pool.Fori(0, N_EXP) as ex:
                    it = ps * N_EXP + ex
                    pool.wait_ge(m_up_read, it * 4 + 4)
                    pool.dma_start(BROW, I["b_gate_up"][0][bass.ds(ex, 1), :]).then_inc(m_brow, 16)
                    pool.wait_ge(m_brow, it * 16 + 16)
                    pool.sem_inc(E("moe_bias_row_seen"), 1)
                    pool.partition_broadcast(BB, BROW).then_inc(m_bias, 1)
                    for t in range(MOE_TILES):
                        if pool_tile(t):
                            pool.wait_ge(m_hi, it * MOE_TILES + t + 1)
                            pool.tensor_tensor(w_lo[:, t % PARTS, :], moe_raw(t), w_hi[:, t % PARTS, :].bitcast(F32),
                                               ALU.subtract).then_inc(m_lo[1], 1)
            powers(pows_before[0], len(pow_widths))

        @block.sync
        def _(sp):
            sp.dma_start(CCOL, I["c"].rearrange("a (k p) -> p (a k)", p=P), allow_slow_non_contiguous=True).then_inc(E("c_in"), 16)

            def load_tables():
                sp.dma_start(TAB[:, :], I["table"]).then_inc(E("setup"), 16)
                sp.dma_start(BUCK, I["buckets"]).then_inc(E("setup"), 16)
                sp.dma_start(SMALLB[:, 0:8], I["rel_bias_2"]).then_inc(E("setup"), 16)
                sp.dma_start(SMALLB[:, 8:24], I["rel_bias_3"]).then_inc(E("setup"), 16)
                sp.dma_start(X[:, :, :], I["x"][0].rearrange("(t p) n -> p t n", p=P)).then_inc(E("x_in"), 16)
                sp.dma_start(TMASK, I["gla_mask"]).then_inc(E("gla_mask"), 16)
                sp.dma_start(WGLR[:, :], I["w_gate_lr"][0]).then_inc(E("gate_lr"), 16)

            def load(n, loads, freed):
                if freed is not None:
                    sp.wait_ge(lo_done, freed)
                t = tiles[n]
                dst = raw[:, n % RAW, 0:t.kts * t.cols].rearrange("p (k n) -> p k n", k=t.kts)
                for part, src in loads(dst):
                    sp.dma_start(part, src).then_inc(raw_landed[n % RAW], 16)

            def load_ffn(f):
                def up(n, col, freed):
                    for i in range(4):
                        load(n + i, lambda dst: [(dst[:, :, c:c + m], src) for c, m, src in f.up(i, col)], freed + i)

                def down(n, j, freed):
                    for i in range(2):
                        load(n + i, lambda dst: [(dst[:, k:k + 1, :], f.down_src[j, k:k + 1, :, 512 * i:512 * (i + 1)]
                                                  .rearrange("j k p n -> p (j k) n")) for k in range(2)], freed + i)

                n0, last = f.n0, FFN_STEPS - 1
                up(n0, slice(0, GLU), n0 - RAW + 1)
                with sp.Fori(0, FFN_PAIRS) as pair:
                    for two in range(2):
                        n = n0 + 4 + FFN_TILES * two
                        freed = pair * (2 * FFN_TILES) + n + 1 - RAW
                        up(n, bass.ds(pair * (2 * GLU) + GLU * (two + 1), GLU), freed)
                        down(n + 4, bass.ds(pair * 2 + two, 1), freed + 4)
                n = n0 + 4 + FFN_TILES * last
                down(n, slice(last, last + 1), n + 1 - RAW)

            for kind, c in order:
                if kind == "tile":
                    load(c.n, lambda dst: [(dst[:, :, a:a + m], src) for a, m, src in c.loads],
                         c.n - RAW + 1 if c.n >= RAW else None)
                    if c.n == RAW - 1:
                        load_tables()
                    if c.n == G["out1"][0].tiles[0].n + RAW - 1:
                        sp.wait_ge(E("rel_rows"), 1)
                        sp.dma_start(arr_dram.ap(), RELS).then_inc(E("rel_stored"), 16)
                        sp.wait_ge(E("rel_stored"), 16)
                        sp.dma_start(skew_dram.ap().rearrange("h (p n) -> h p n", p=P),
                                     arr_dram.ap().unsqueeze(1).to_broadcast([24, P, 384])).then_inc(E("rel_skewed"), 16)
                elif kind == "vec":
                    src = vecs[c]
                    if c >= VECS:
                        sp.wait_ge(vec_used, c - VECS + 1)
                    sp.dma_start(VEC[:, c % VECS, :], src[0:1, :].to_broadcast([P, D])).then_inc(vec_landed[c % VECS], 16)
                elif kind == "mem":
                    sp.wait_ge(E("diff_done"), 1)
                    sp.dma_start(H[:, :, :], I["mem_2"][0].rearrange("(t p) n -> p t n", p=P)).then_inc(E("mem_in"), 16)
                    sp.dma_start(BIAS[:, :, :], bias_rows(16)).then_inc(E("bias3b"), 16)
                elif kind == "ffn":
                    load_ffn(c)
                elif kind == "moe":
                    sp.wait_ge(lo_done, moe_at)
                    sp.wait_ge(E("mix1"), TT)
                    sp.dma_start(BDOWN, I["b_down"][0]).then_inc(E("b_down"), 16)
                    sp.wait_ge(E("n_pass"), 1)
                    n_pass = sp.value_load(NPASS[0:1, 0:1], min_val=1, max_val=2)
                    wu = I["w_gate_up"][0].rearrange("e (k p) n -> e p k n", p=P)
                    wd = I["w_down"][0].rearrange("e (k p) n -> e p k n", p=P)
                    with sp.Fori(0, n_pass) as ps:
                        with sp.Fori(0, N_EXP) as ex:
                            it = ps * N_EXP + ex
                            for t in range(MOE_TILES):
                                b, k = t // 4, 2 * (t % 4)
                                w, b = (wu, b) if b < 4 else (wd, b - 4)
                                sp.wait_ge(*moe_lo(it, t - MOE_RAW))
                                sp.dma_start(moe_raw(t).rearrange("p (k n) -> p k n", k=2),
                                             w[bass.ds(ex, 1), :, k:k + 2, 512 * b:512 * (b + 1)]
                                             .rearrange("e p k n -> p (e k) n")).then_inc(m_landed[t % MOE_RAW], 16)
                    sp.wait_ge(E("moe_over"), 1)
                    sp.wait_ge(E("rel_skewed"), 16)
                    sp.dma_start(BIAS[:, :, :], bias_rows(0)).then_inc(E("bias2"), 16)
            sp.wait_ge(E("result"), 1)
            sp.dma_start(out[0].rearrange("(t p) n -> p t n", p=P), X[:, :, :]).then_inc(E("stored"), 16)
            sp.wait_ge(E("stored"), 16)


NAMES = """x c w_mod b_mod g_pre_mix w_in w_gate_lr b_gate g_gla w_out g_post_mix g_pre_ffn router_w router_b w_gate_up
b_gate_up w_down b_down g_post_ffn mem_2 rel_bias_2 ffn1_w1_2 ffn1_w3_2 ffn1_w2_2 ln1_g_2 ln1_b_2 w_in_2 q_norm_g_2
kv_norm_g_2 w_q_b_2 w_kv_b_2 lam_q1_2 lam_k1_2 lam_q2_2 lam_k2_2 diff_norm_g_2 w_gate_2 b_gate_2 w_up_mla_2
w_up_diff_2 w_o_2 ln2_g_2 ln2_b_2 mem_w_q_2 mem_w_kv_2 mem_w_o_2 ln3_g_2 ln3_b_2 ffn2_w1_2 ffn2_w3_2 ffn2_w2_2 ln4_g_2
ln4_b_2 ffn1_norm_3 ffn1_w_gu_3 ffn1_w_down_3 mix_norm_3 w_in_3 b_gate_3 q_norm_dsa_3 k_norm_dsa_3 q_norm_moba_3
k_norm_moba_3 w_branch_dsa_3 w_branch_moba_3 w_out_3 ffn2_norm_3 ffn2_w_gu_3 ffn2_w_down_3 rel_bias_3""".split()


def kernel(**inputs):
    import concourse.bacc as bacc
    from concourse.bass_utils import run_bass_kernel_spmd

    nc = bacc.Bacc("TRN2", target_bir_lowering=False, num_devices=1)
    arrays = {name: np.ascontiguousarray(inputs[name]) for name in NAMES}
    arrays.update(table=TABLE, buckets=BUCKETS, gla_mask=GLA_MASK)
    I = {name: nc.dram_tensor(f"in_{name}", a.shape, mybir.dt.from_np(a.dtype), kind="ExternalInput").ap()
         for name, a in arrays.items()}
    out = nc.dram_tensor("result", (1, S, D), F32, kind="ExternalOutput").ap()
    build(nc, I, out)
    got = run_bass_kernel_spmd(nc, [{f"in_{k}": a for k, a in arrays.items()}], core_ids=[0])
    return got.results[0]["result"]
```
